# Optimizing a Trainium2 kernel written in Bass

```python
import jax, jax.numpy as jnp
from jax import lax
import math
import jax
import jax.numpy as jnp
import numpy as np

D_MODEL = 1024
BATCH = 1
SEQ = 512
DEPTH = 1

D_MIX = D_MODEL
D_RWKV = D_MIX // 2
D_CONV = D_MIX - D_RWKV
HEAD_DIM = 64
N_RWKV_HEADS = D_RWKV // HEAD_DIM
N_CONV_GROUPS = D_CONV // HEAD_DIM
W_LORA = 32
A_LORA = 32
V_LORA = 32
G_LORA = 96
CONV_WIDTH = 31
FFN_CONV_WIDTH = 3
D_FF = 2816
GLU_COLS = 2 * D_CONV
RWKV_COLS = 3 * D_RWKV + W_LORA + A_LORA + G_LORA
COLS_FIRST = GLU_COLS + RWKV_COLS
COLS_REST = COLS_FIRST + V_LORA
RMS_EPS = 1e-6
LN_EPS = 1e-5
GN_EPS = 64e-5


def _rms_norm(x, g):
    xf = x.astype(jnp.float32)
    y = xf * lax.rsqrt(jnp.mean(xf * xf, axis=-1, keepdims=True) + RMS_EPS)
    return (y * g.astype(jnp.float32)).astype(x.dtype)

def _layer_norm(x, g, b):
    xf = x.astype(jnp.float32)
    mu = jnp.mean(xf, axis=-1, keepdims=True)
    var = jnp.mean(jnp.square(xf - mu), axis=-1, keepdims=True)
    y = (xf - mu) * lax.rsqrt(var + LN_EPS)
    return (y * g.astype(jnp.float32) + b.astype(jnp.float32)).astype(x.dtype)

def _token_shift(p):
    return jnp.pad(p, ((0, 0), (1, 0), (0, 0)))[:, :-1]

def _causal_dwconv(x, w, b):
    K = w.shape[0]
    y = lax.conv_general_dilated(
        x, w[:, None, :].astype(x.dtype), window_strides=(1,), padding=((K - 1, 0),),
        dimension_numbers=("NWC", "WIO", "NWC"), feature_group_count=x.shape[-1])
    return y + b.astype(x.dtype)

def _wkv7(r, decay, k, v, a_vec, b_vec):
    B, T, H, N = r.shape

    def step(S, inp):
        r_t, w_t, k_t, v_t, a_t, b_t = inp
        sa = jnp.einsum("bhvk,bhk->bhv", S, a_t)
        S = S * w_t[:, :, None, :] + sa[..., None] * b_t[:, :, None, :] + v_t[..., None] * k_t[:, :, None, :]
        y = jnp.einsum("bhvk,bhk->bhv", S, r_t)
        return S, y

    xs = tuple(jnp.moveaxis(t.astype(jnp.float32), 1, 0) for t in (r, decay, k, v, a_vec, b_vec))
    S0 = jnp.zeros((B, H, N, N), jnp.float32)
    _, ys = lax.scan(step, S0, xs)
    return jnp.moveaxis(ys, 0, 1)

def _head_group_norm(y, g, b):
    B, T, H, N = y.shape
    mu = jnp.mean(y, axis=-1, keepdims=True)
    var = jnp.mean(jnp.square(y - mu), axis=-1, keepdims=True)
    y = ((y - mu) * lax.rsqrt(var + GN_EPS)).reshape(B, T, H * N)
    return y * g.astype(jnp.float32) + b.astype(jnp.float32)

def _hybrid_mixer(h, w_in, mu, vres_v0, vres_up, v_first, decay_w0, decay_up, iclr_a0, iclr_up,
                  gate_up, k_k, k_a, r_k, lnx_g, lnx_b, cconv_w, cconv_b, cln_g, cln_b, w_out):
    B, T, _ = h.shape
    H, N = N_RWKV_HEADS, HEAD_DIM
    p = h @ w_in.astype(h.dtype)
    u = p[..., :GLU_COLS]
    q = p[..., GLU_COLS:]
    q = q + (_token_shift(q) - q) * mu.astype(h.dtype)
    o1, o2, o3 = D_RWKV, 2 * D_RWKV, 3 * D_RWKV
    o4, o5, o6 = o3 + W_LORA, o3 + W_LORA + A_LORA, RWKV_COLS
    r, k, v = q[..., :o1], q[..., o1:o2], q[..., o2:o3]
    wd, ad, gd = q[..., o3:o4], q[..., o4:o5], q[..., o5:o6]

    wf = (decay_w0 + jnp.tanh(wd) @ decay_up).astype(jnp.float32)
    decay = jnp.exp(-jnp.exp(-jax.nn.softplus(-wf) - 0.5))
    if v_first is None:
        v_first = v
    else:
        vd = q[..., o6:]
        v = v + (v_first - v) * jax.nn.sigmoid(vres_v0 + vd @ vres_up)
    a = jax.nn.sigmoid(iclr_a0 + ad @ iclr_up)
    g = jax.nn.sigmoid(gd) @ gate_up
    kk = (k * k_k).reshape(B, T, H, N).astype(jnp.float32)
    kk = kk * lax.rsqrt(jnp.maximum(jnp.sum(kk * kk, axis=-1, keepdims=True), 1e-24))
    k = k * (1 + (a - 1) * k_a)
    r_h = r.reshape(B, T, H, N)
    k_h = k.reshape(B, T, H, N)
    v_h = v.reshape(B, T, H, N)
    a_h = a.reshape(B, T, H, N).astype(jnp.float32)
    y = _wkv7(r_h, decay.reshape(B, T, H, N), k_h, v_h, -kk, kk * a_h)
    y = _head_group_norm(y, lnx_g, lnx_b).astype(h.dtype)
    bonus = jnp.sum(r_h * k_h * r_k.astype(h.dtype), axis=-1, keepdims=True) * v_h
    rwkv_out = (y + bonus.reshape(B, T, D_RWKV)) * g

    c = u[..., :D_CONV] * jax.nn.sigmoid(u[..., D_CONV:])
    c = _causal_dwconv(c, cconv_w, cconv_b)
    c = jax.nn.silu(_layer_norm(c, cln_g, cln_b))

    mix = jnp.concatenate([rwkv_out, c], axis=-1) @ w_out.astype(h.dtype)
    return mix, v_first

def _conv_ffn(h, ffn_up, ffn_conv_w, ffn_conv_b, ffn_down):
    hid = h @ ffn_up.astype(h.dtype)
    hid = _causal_dwconv(hid, ffn_conv_w, ffn_conv_b)
    gate, up = hid[..., :D_FF], hid[..., D_FF:]
    return (jax.nn.gelu(gate, approximate=True) * up) @ ffn_down.astype(h.dtype)

def first_inputs(seed: int = 0) -> dict:
    key = jax.random.key(seed)
    ks = iter(jax.random.split(key, 40))
    f32 = jnp.float32

    def nrm(shape, scale):
        return jax.random.normal(next(ks), shape, f32) * scale

    def unif(shape, lo, hi):
        return jax.random.uniform(next(ks), shape, f32, lo, hi)

    L, Lr = DEPTH, DEPTH - 1
    return {
        "x": nrm((BATCH, SEQ, D_MODEL), 1.0),
        "w_in_first": nrm((D_MODEL, COLS_FIRST), D_MODEL ** -0.5),
        "mu_first": unif((RWKV_COLS,), 0.0, 1.0),
        "w_in_rest": nrm((Lr, D_MODEL, COLS_REST), D_MODEL ** -0.5),
        "mu_rest": unif((Lr, RWKV_COLS + V_LORA), 0.0, 1.0),
        "vres_v0": nrm((Lr, D_RWKV), 0.5),
        "vres_up": nrm((Lr, V_LORA, D_RWKV), 0.1),
        "decay_w0": unif((L, D_RWKV), -6.0, 1.0),
        "decay_up": nrm((L, W_LORA, D_RWKV), 0.1),
        "iclr_a0": nrm((L, D_RWKV), 0.5),
        "iclr_up": nrm((L, A_LORA, D_RWKV), 0.1),
        "gate_up": nrm((L, G_LORA, D_RWKV), G_LORA ** -0.5),
        "k_k": 0.85 + nrm((L, D_RWKV), 0.05),
        "k_a": 1.0 + nrm((L, D_RWKV), 0.05),
        "r_k": nrm((L, N_RWKV_HEADS, HEAD_DIM), 0.1),
        "lnx_g": 1.0 + nrm((L, D_RWKV), 0.05),
        "lnx_b": nrm((L, D_RWKV), 0.01),
        "cconv_w": nrm((L, CONV_WIDTH, D_CONV), CONV_WIDTH ** -0.5),
        "cconv_b": nrm((L, D_CONV), 0.01),
        "cln_g": 1.0 + nrm((L, D_CONV), 0.05),
        "cln_b": nrm((L, D_CONV), 0.01),
        "w_out": nrm((L, D_MIX, D_MODEL), D_MIX ** -0.5),
        "norm_pre_mix": 1.0 + nrm((L, D_MODEL), 0.05),
        "norm_post_mix": 1.0 + nrm((L, D_MODEL), 0.05),
        "norm_pre_ffn": 1.0 + nrm((L, D_MODEL), 0.05),
        "norm_post_ffn": 1.0 + nrm((L, D_MODEL), 0.05),
        "ffn_up": nrm((L, D_MODEL, 2 * D_FF), D_MODEL ** -0.5),
        "ffn_conv_w": nrm((L, FFN_CONV_WIDTH, 2 * D_FF), FFN_CONV_WIDTH ** -0.5),
        "ffn_conv_b": nrm((L, 2 * D_FF), 0.01),
        "ffn_down": nrm((L, D_FF, D_MODEL), D_FF ** -0.5),
    }

def first_block(x, w_in_first, mu_first, w_in_rest, mu_rest, vres_v0, vres_up, decay_w0, decay_up,
              iclr_a0, iclr_up, gate_up, k_k, k_a, r_k, lnx_g, lnx_b, cconv_w, cconv_b, cln_g, cln_b,
              w_out, norm_pre_mix, norm_post_mix, norm_pre_ffn, norm_post_ffn, ffn_up, ffn_conv_w,
              ffn_conv_b, ffn_down):
    v_first = None
    for i in range(DEPTH):
        if i == 0:
            w_in_i, mu_i, v0_i, vup_i = w_in_first, mu_first, None, None
        else:
            w_in_i, mu_i, v0_i, vup_i = w_in_rest[i - 1], mu_rest[i - 1], vres_v0[i - 1], vres_up[i - 1]
        h = _rms_norm(x, norm_pre_mix[i])
        mix, v_first = _hybrid_mixer(
            h, w_in_i, mu_i, v0_i, vup_i, v_first, decay_w0[i], decay_up[i], iclr_a0[i], iclr_up[i],
            gate_up[i], k_k[i], k_a[i], r_k[i], lnx_g[i], lnx_b[i], cconv_w[i], cconv_b[i],
            cln_g[i], cln_b[i], w_out[i])
        x = x + _rms_norm(mix, norm_post_mix[i])
        h = _rms_norm(x, norm_pre_ffn[i])
        f = _conv_ffn(h, ffn_up[i], ffn_conv_w[i], ffn_conv_b[i], ffn_down[i])
        x = x + _rms_norm(f, norm_post_ffn[i])
    return x


DEPTH_2 = 2

CTX_LEN = 256
GRID_W = 64
N_MIXERS = 4
Q_BLOCK = 128
WINDOW = 128
ROPE_THETA = 10000.0
NORM_EPS = 1e-6
WIDTH = D_MODEL

A_HEADS = 16
A_Q_LORA = 256
A_KV_LORA = 128
A_NOPE = 64
A_ROPE = 32
A_V = 64
A_IN = A_Q_LORA + A_KV_LORA + A_ROPE + WIDTH

B_HEADS = 8
B_HEAD = 64
B_IN = 3 * (2 * B_HEADS * B_HEAD) + WIDTH

C_HEADS = 8
C_KV_HEADS = 2
C_HEAD = 128
C_IN = (C_HEADS + 2 * C_KV_HEADS) * C_HEAD + WIDTH

D_HEADS = 16
D_KV_HEADS = 2
D_HEAD = 64
D_IN = (D_HEADS + 2 * D_KV_HEADS) * D_HEAD + WIDTH

DEEPNORM_ALPHA = (2 * DEPTH_2) ** 0.25
DEEPNORM_BETA = (8 * DEPTH_2) ** -0.25


def rms_norm(x, g):
    xf = x.astype(jnp.float32)
    y = xf * lax.rsqrt(jnp.mean(xf * xf, axis=-1, keepdims=True) + NORM_EPS)
    return (y * g.astype(jnp.float32)).astype(x.dtype)

def layer_norm(x, g, b):
    xf = x.astype(jnp.float32)
    xc = xf - jnp.mean(xf, axis=-1, keepdims=True)
    var = jnp.mean(xc * xc, axis=-1, keepdims=True)
    y = xc * lax.rsqrt(var + NORM_EPS) * g.astype(jnp.float32) + b.astype(jnp.float32)
    return y.astype(x.dtype)

def axial_rope_tables(rows, rot_dim):
    row = jnp.repeat(jnp.arange(rows, dtype=jnp.float32), GRID_W)
    col = jnp.tile(jnp.arange(GRID_W, dtype=jnp.float32), rows)
    n_freq = rot_dim // 4
    inv_freq = ROPE_THETA ** (-jnp.arange(n_freq, dtype=jnp.float32) / n_freq)
    ang = jnp.concatenate([row[:, None] * inv_freq, col[:, None] * inv_freq], axis=-1)
    return jnp.cos(ang)[:, None, :], jnp.sin(ang)[:, None, :]

def apply_rope(x, cos, sin):
    half = x.shape[-1] // 2
    x1 = x[..., :half].astype(jnp.float32)
    x2 = x[..., half:].astype(jnp.float32)
    return jnp.concatenate([x1 * cos - x2 * sin, x2 * cos + x1 * sin], axis=-1).astype(x.dtype)

def adaln(cvec, w, b):
    m = jax.nn.silu(cvec) @ w + b
    return jnp.split(m, 3, axis=-1)

def gated(o, gate):
    return o.reshape(gate.shape) * jax.nn.silu(gate)

def dense_attention(q, k, v, scale):
    bsz, s_len, hk, g, d = q.shape
    dv = v.shape[-1]
    nb = s_len // Q_BLOCK
    q_blocks = jnp.moveaxis(q.reshape(bsz, nb, Q_BLOCK, hk, g, d), 1, 0)

    def one_block(qb):
        s = jnp.einsum('bqhgd,bkhd->bhgqk', qb, k).astype(jnp.float32) * scale
        p = jax.nn.softmax(s, axis=-1).astype(v.dtype)
        return jnp.einsum('bhgqk,bkhv->bqhgv', p, v)

    o = lax.map(one_block, q_blocks)
    return jnp.moveaxis(o, 0, 1).reshape(bsz, s_len, hk, g, dv)

def prefix_attention(q, k, v, q_c, k_c, v_c, scale, need_ctx):
    o = dense_attention(q, jnp.concatenate([k, k_c], axis=1), jnp.concatenate([v, v_c], axis=1), scale)
    o_c = dense_attention(q_c, k_c, v_c, scale) if need_ctx else None
    return o, o_c

def window_sink_attention(q, k, v, k_c, v_c, sinks, scale):
    bsz, s_len, hk, g, d = q.shape
    dv = v.shape[-1]
    nb = s_len // Q_BLOCK
    kw = 3 * Q_BLOCK
    pad = ((0, 0), (Q_BLOCK, Q_BLOCK), (0, 0), (0, 0))
    k_pad = jnp.pad(k, pad)
    v_pad = jnp.pad(v, pad)
    offs_q = jnp.arange(Q_BLOCK)
    offs_k = jnp.arange(kw) - Q_BLOCK
    in_band = jnp.abs(offs_k[None, :] - offs_q[:, None]) <= WINDOW
    sink_logit = sinks.reshape(hk, g).astype(jnp.float32)[None, :, :, None, None]

    def one_block(n):
        start = n * Q_BLOCK
        qb = lax.dynamic_slice_in_dim(q, start, Q_BLOCK, axis=1)
        kb = lax.dynamic_slice_in_dim(k_pad, start, kw, axis=1)
        vb = lax.dynamic_slice_in_dim(v_pad, start, kw, axis=1)
        kpos = start + offs_k
        valid = in_band & ((kpos >= 0) & (kpos < s_len))[None, :]
        s_loc = jnp.einsum('bqhgd,bkhd->bhgqk', qb, kb).astype(jnp.float32) * scale
        s_loc = jnp.where(valid, s_loc, -jnp.inf)
        s_ctx = jnp.einsum('bqhgd,bkhd->bhgqk', qb, k_c).astype(jnp.float32) * scale
        s_sink = jnp.broadcast_to(sink_logit, s_loc.shape[:-1] + (1,))
        p = jax.nn.softmax(jnp.concatenate([s_loc, s_ctx, s_sink], axis=-1), axis=-1).astype(v.dtype)
        o_loc = jnp.einsum('bhgqk,bkhv->bqhgv', p[..., :kw], vb)
        o_ctx = jnp.einsum('bhgqk,bkhv->bqhgv', p[..., kw:kw + k_c.shape[1]], v_c)
        return o_loc + o_ctx

    o = lax.map(one_block, jnp.arange(nb))
    return jnp.moveaxis(o, 0, 1).reshape(bsz, s_len, hk, g, dv)

def context_sink_attention(q_c, k_c, v_c, sinks, scale):
    hk, g = q_c.shape[2], q_c.shape[3]
    s = jnp.einsum('bqhgd,bkhd->bhgqk', q_c, k_c).astype(jnp.float32) * scale
    s_sink = jnp.broadcast_to(sinks.reshape(hk, g).astype(jnp.float32)[None, :, :, None, None], s.shape[:-1] + (1,))
    p = jax.nn.softmax(jnp.concatenate([s, s_sink], axis=-1), axis=-1)[..., :-1].astype(v_c.dtype)
    return jnp.einsum('bhgqk,bkhv->bqhgv', p, v_c)

def mla_mixer(h, h_c, rows, need_ctx, w_in, g_qa, w_qb, g_kva, w_kvb):
    cos, sin = axial_rope_tables(rows, A_ROPE)
    splits = [A_Q_LORA, A_Q_LORA + A_KV_LORA, A_Q_LORA + A_KV_LORA + A_ROPE]

    def project(t, rope):
        bsz, n = t.shape[:2]
        q_lat, kv_lat, k_pe, gate = jnp.split(t @ w_in, splits, axis=-1)
        q = (rms_norm(q_lat, g_qa) @ w_qb).reshape(bsz, n, A_HEADS, A_NOPE + A_ROPE)
        kv = (rms_norm(kv_lat, g_kva) @ w_kvb).reshape(bsz, n, A_HEADS, A_NOPE + A_V)
        q_nope, q_pe = q[..., :A_NOPE], q[..., A_NOPE:]
        k_nope, v = kv[..., :A_NOPE], kv[..., A_NOPE:]
        k_pe = k_pe[:, :, None, :]
        if rope:
            q_pe = apply_rope(q_pe, cos, sin)
            k_pe = apply_rope(k_pe, cos, sin)
        q = jnp.concatenate([q_nope, q_pe], axis=-1)[:, :, :, None, :]
        k = jnp.concatenate([k_nope, jnp.broadcast_to(k_pe, (bsz, n, A_HEADS, A_ROPE))], axis=-1)
        return q, k, v, gate

    q, k, v, gate = project(h, True)
    q_c, k_c, v_c, gate_c = project(h_c, False)
    o, o_c = prefix_attention(q, k, v, q_c, k_c, v_c, (A_NOPE + A_ROPE) ** -0.5, need_ctx)
    return gated(o, gate), (gated(o_c, gate_c) if need_ctx else None)

def diff_mixer(h, h_c, rows, need_ctx, layer_idx, w_in, lam, g_sub):
    cos, sin = axial_rope_tables(rows, B_HEAD)
    lambda_init = 0.8 - 0.6 * math.exp(-0.3 * layer_idx)
    lam = lam.astype(jnp.float32)
    lam_full = jnp.exp(jnp.sum(lam[0] * lam[1])) - jnp.exp(jnp.sum(lam[2] * lam[3])) + lambda_init
    scale = B_HEAD ** -0.5

    def project(t, rope):
        bsz, n = t.shape[:2]
        q, k, v, gate = jnp.split(t @ w_in, 4, axis=-1)
        q = q.reshape(bsz, n, 2 * B_HEADS, B_HEAD)
        k = k.reshape(bsz, n, 2 * B_HEADS, B_HEAD)
        if rope:
            q = apply_rope(q, cos, sin)
            k = apply_rope(k, cos, sin)
        q = q.reshape(bsz, n, B_HEADS, 2, B_HEAD)
        k = k.reshape(bsz, n, B_HEADS, 2, B_HEAD)
        v = v.reshape(bsz, n, B_HEADS, 2 * B_HEAD)
        return q, k, v, gate

    def combine(o1, o2, gate):
        o = o1 - lam_full.astype(o1.dtype) * o2
        o = rms_norm(o, g_sub) * (1.0 - lambda_init)
        return gated(o, gate)

    q, k, v, gate = project(h, True)
    q_c, k_c, v_c, gate_c = project(h_c, False)
    o1, o1_c = prefix_attention(q[:, :, :, 0:1], k[:, :, :, 0], v, q_c[:, :, :, 0:1], k_c[:, :, :, 0], v_c, scale, need_ctx)
    o2, o2_c = prefix_attention(q[:, :, :, 1:2], k[:, :, :, 1], v, q_c[:, :, :, 1:2], k_c[:, :, :, 1], v_c, scale, need_ctx)
    return combine(o1, o2, gate), (combine(o1_c, o2_c, gate_c) if need_ctx else None)

def qknorm_gqa_mixer(h, h_c, rows, need_ctx, w_in, g_q, g_k):
    cos, sin = axial_rope_tables(rows, C_HEAD)
    splits = [C_HEADS * C_HEAD, (C_HEADS + C_KV_HEADS) * C_HEAD, (C_HEADS + 2 * C_KV_HEADS) * C_HEAD]

    def project(t, rope):
        bsz, n = t.shape[:2]
        q, k, v, gate = jnp.split(t @ w_in, splits, axis=-1)
        q = rms_norm(q.reshape(bsz, n, C_HEADS, C_HEAD), g_q)
        k = rms_norm(k.reshape(bsz, n, C_KV_HEADS, C_HEAD), g_k)
        v = v.reshape(bsz, n, C_KV_HEADS, C_HEAD)
        if rope:
            q = apply_rope(q, cos, sin)
            k = apply_rope(k, cos, sin)
        q = q.reshape(bsz, n, C_KV_HEADS, C_HEADS // C_KV_HEADS, C_HEAD)
        return q, k, v, gate

    q, k, v, gate = project(h, True)
    q_c, k_c, v_c, gate_c = project(h_c, False)
    o, o_c = prefix_attention(q, k, v, q_c, k_c, v_c, C_HEAD ** -0.5, need_ctx)
    return gated(o, gate), (gated(o_c, gate_c) if need_ctx else None)

def swa_sink_mixer(h, h_c, rows, need_ctx, w_in, sinks):
    cos, sin = axial_rope_tables(rows, D_HEAD)
    splits = [D_HEADS * D_HEAD, (D_HEADS + D_KV_HEADS) * D_HEAD, (D_HEADS + 2 * D_KV_HEADS) * D_HEAD]
    scale = D_HEAD ** -0.5

    def project(t, rope):
        bsz, n = t.shape[:2]
        q, k, v, gate = jnp.split(t @ w_in, splits, axis=-1)
        q = q.reshape(bsz, n, D_HEADS, D_HEAD)
        k = k.reshape(bsz, n, D_KV_HEADS, D_HEAD)
        v = v.reshape(bsz, n, D_KV_HEADS, D_HEAD)
        if rope:
            q = apply_rope(q, cos, sin)
            k = apply_rope(k, cos, sin)
        q = q.reshape(bsz, n, D_KV_HEADS, D_HEADS // D_KV_HEADS, D_HEAD)
        return q, k, v, gate

    q, k, v, gate = project(h, True)
    q_c, k_c, v_c, gate_c = project(h_c, False)
    o = window_sink_attention(q, k, v, k_c, v_c, sinks, scale)
    o_c = gated(context_sink_attention(q_c, k_c, v_c, sinks, scale), gate_c) if need_ctx else None
    return gated(o, gate), o_c

def second_inputs(seed: int = 0) -> dict:
    key = jax.random.key(seed)
    ks = iter(jax.random.split(key, 32))

    def nrm(shape, std):
        return jax.random.normal(next(ks), shape, jnp.float32) * std

    def gain(shape):
        return 1.0 + nrm(shape, 0.02)

    n_a = len(range(0, DEPTH_2, N_MIXERS))
    n_b = len(range(1, DEPTH_2, N_MIXERS))
    n_c = len(range(2, DEPTH_2, N_MIXERS))
    n_d = len(range(3, DEPTH_2, N_MIXERS))
    return {
        'x': nrm((BATCH, SEQ, D_MODEL), 1.0),
        'c': nrm((BATCH, D_MODEL), 1.0),
        'ctx': nrm((BATCH, CTX_LEN, D_MODEL), 1.0),
        'c_ctx': nrm((D_MODEL,), 1.0),
        'ada_w': nrm((DEPTH_2, D_MODEL, 3 * D_MODEL), 0.02),
        'ada_b': nrm((DEPTH_2, 3 * D_MODEL), 0.02),
        'out_w': nrm((DEPTH_2, WIDTH, D_MODEL), DEEPNORM_BETA * WIDTH ** -0.5),
        'ln_g': gain((DEPTH_2, D_MODEL)),
        'ln_b': nrm((DEPTH_2, D_MODEL), 0.02),
        'mla_w_in': nrm((n_a, D_MODEL, A_IN), D_MODEL ** -0.5),
        'mla_g_qa': gain((n_a, A_Q_LORA)),
        'mla_w_qb': nrm((n_a, A_Q_LORA, A_HEADS * (A_NOPE + A_ROPE)), A_Q_LORA ** -0.5),
        'mla_g_kva': gain((n_a, A_KV_LORA)),
        'mla_w_kvb': nrm((n_a, A_KV_LORA, A_HEADS * (A_NOPE + A_V)), A_KV_LORA ** -0.5),
        'diff_w_in': nrm((n_b, D_MODEL, B_IN), D_MODEL ** -0.5),
        'diff_lambda': nrm((n_b, 4, B_HEAD), 0.1),
        'diff_g_sub': gain((n_b, 2 * B_HEAD)),
        'gqa_w_in': nrm((n_c, D_MODEL, C_IN), D_MODEL ** -0.5),
        'gqa_g_q': gain((n_c, C_HEAD)),
        'gqa_g_k': gain((n_c, C_HEAD)),
        'swa_w_in': nrm((n_d, D_MODEL, D_IN), D_MODEL ** -0.5),
        'swa_sink': nrm((n_d, D_HEADS), 0.5),
    }

def second_block(x, c, ctx, c_ctx, ada_w, ada_b, out_w, ln_g, ln_b,
              mla_w_in, mla_g_qa, mla_w_qb, mla_g_kva, mla_w_kvb,
              diff_w_in, diff_lambda, diff_g_sub,
              gqa_w_in, gqa_g_q, gqa_g_k,
              swa_w_in, swa_sink):
    ROWS = x.shape[1] // GRID_W
    for i in range(DEPTH_2):
        kind, j = i % N_MIXERS, i // N_MIXERS
        need_ctx = i < DEPTH_2 - 1
        shift, scale, gate = adaln(c, ada_w[i], ada_b[i])
        shift_c, scale_c, gate_c = adaln(c_ctx, ada_w[i], ada_b[i])
        h = x * (1.0 + scale[:, None, :]) + shift[:, None, :]
        h_c = ctx * (1.0 + scale_c) + shift_c
        if kind == 0:
            o, o_c = mla_mixer(h, h_c, ROWS, need_ctx, mla_w_in[j], mla_g_qa[j], mla_w_qb[j], mla_g_kva[j], mla_w_kvb[j])
        elif kind == 1:
            o, o_c = diff_mixer(h, h_c, ROWS, need_ctx, i, diff_w_in[j], diff_lambda[j], diff_g_sub[j])
        elif kind == 2:
            o, o_c = qknorm_gqa_mixer(h, h_c, ROWS, need_ctx, gqa_w_in[j], gqa_g_q[j], gqa_g_k[j])
        else:
            o, o_c = swa_sink_mixer(h, h_c, ROWS, need_ctx, swa_w_in[j], swa_sink[j])
        x = layer_norm(DEEPNORM_ALPHA * x + gate[:, None, :] * (o @ out_w[i]), ln_g[i], ln_b[i])
        if need_ctx:
            ctx = layer_norm(DEEPNORM_ALPHA * ctx + gate_c * (o_c @ out_w[i]), ln_g[i], ln_b[i])
    return x


def setup_inputs(seed=0):
    out = dict(first_inputs(seed))
    for name, value in second_inputs(seed + 1).items():
        if name != "x":
            out[name + "_2"] = value
    return out


def reference(
    x, w_in_first, mu_first, w_in_rest, mu_rest, vres_v0, vres_up, decay_w0, decay_up, iclr_a0,
    iclr_up, gate_up, k_k, k_a, r_k, lnx_g, lnx_b, cconv_w, cconv_b, cln_g, cln_b, w_out,
    norm_pre_mix, norm_post_mix, norm_pre_ffn, norm_post_ffn, ffn_up, ffn_conv_w, ffn_conv_b,
    ffn_down, c_2, ctx_2, c_ctx_2, ada_w_2, ada_b_2, out_w_2, ln_g_2, ln_b_2, mla_w_in_2,
    mla_g_qa_2, mla_w_qb_2, mla_g_kva_2, mla_w_kvb_2, diff_w_in_2, diff_lambda_2, diff_g_sub_2,
    gqa_w_in_2, gqa_g_q_2, gqa_g_k_2, swa_w_in_2, swa_sink_2,
):
    x = first_block(
        x, w_in_first, mu_first, w_in_rest, mu_rest, vres_v0, vres_up, decay_w0, decay_up,
        iclr_a0, iclr_up, gate_up, k_k, k_a, r_k, lnx_g, lnx_b, cconv_w, cconv_b, cln_g, cln_b,
        w_out, norm_pre_mix, norm_post_mix, norm_pre_ffn, norm_post_ffn, ffn_up, ffn_conv_w,
        ffn_conv_b, ffn_down,
    )
    return second_block(
        x, c_2, ctx_2, c_ctx_2, ada_w_2, ada_b_2, out_w_2, ln_g_2, ln_b_2, mla_w_in_2,
        mla_g_qa_2, mla_w_qb_2, mla_g_kva_2, mla_w_kvb_2, diff_w_in_2, diff_lambda_2,
        diff_g_sub_2, gqa_w_in_2, gqa_g_q_2, gqa_g_k_2, swa_w_in_2, swa_sink_2,
    )


_drawn_inputs = setup_inputs


def setup_inputs(seed=0):
    import zlib

    import numpy as np

    out = dict(_drawn_inputs(seed))
    spreads = {}
    factors = {'decay_up': 3.708,
     'lnx_b': 8.0,
     'cconv_b': 4.606,
     'cln_b': 8.0,
     'ffn_conv_b': 6.982,
     'ctx_2': 4.721,
     'ada_b_2': 8.0,
     'mla_g_qa_2': 8.0,
     'mla_w_qb_2': 4.942,
     'mla_g_kva_2': 8.0,
     'diff_lambda_2': 7.091,
     'diff_g_sub_2': 111.668}
    for name, (base, spread) in spreads.items():
        noise = np.random.default_rng([zlib.crc32(name.encode()), seed]).standard_normal(out[name].shape)
        drawn = base * np.exp(spread * noise) if base else spread * noise
        out[name] = jnp.asarray(drawn.astype(out[name].dtype))
    for name, factor in factors.items():
        out[name] = (out[name] * factor).astype(out[name].dtype)
    return out
```

```python
from contextlib import ExitStack, contextmanager
import math

import numpy as np
import concourse.bass as bass
from concourse import mybir

F32 = mybir.dt.float32
F32R = mybir.dt.float32r
U8 = mybir.dt.uint8
ALU = mybir.AluOpType
ACT = mybir.ActivationFunctionType
AX = mybir.AxisListType

P = 128
T = 512
C = 256
TA = T + C
D = 1024
KT = D // P
HALF = 512
CT = HALF // P
CHUNK = 64
NCH = T // CHUNK
TAPS = 31
DFF = 2816
FT = DFF // P
A_HEADS, A_QK, A_V = 16, 96, 64
B_HEADS, B_D = 8, 64
RMS_EPS, LN_EPS, GN_EPS = 1e-6, 1e-5, 64e-5
ALPHA = 4.0 ** 0.25
LAMBDA_INIT = 0.8 - 0.6 * math.exp(-0.3)
TILES = 16
WBLK = TILES * P

N_IN, N_OUT, N_UP, N_DOWN = 11, 4, FT, 12
N_MLA_IN, N_MLA, N_MLA_OUT, N_DIFF, N_DIFF_OUT = 6, 8, 4, 16, 4
ADA_BLOCKS = 24
STREAM = {}
_at = 0
for _name, _n in (("in", N_IN), ("out", N_OUT), ("up", N_UP), ("down", N_DOWN), ("mla_in", N_MLA_IN),
                  ("mla", N_MLA), ("mla_out", N_MLA_OUT), ("diff", N_DIFF), ("diff_out", N_DIFF_OUT)):
    STREAM[_name] = _at
    _at += _n
N_BLOCKS = _at

PCOL = {}
_at = 0
for _name, _n in (("mu", 14), ("w0", 4), ("a0", 4), ("k_k", 4), ("k_a", 4), ("r_k", 4), ("lnx_g", 4),
                  ("lnx_b", 4), ("cconv_w", 4 * TAPS), ("cconv_b", 4), ("cln_g", 4), ("cln_b", 4),
                  ("pre_mix", 8), ("post_mix", 8), ("pre_ffn", 8), ("post_ffn", 8),
                  ("fconv_w", 3 * 2 * FT), ("fconv_b", 2 * FT), ("c", 16), ("ada_b", 96),
                  ("ln_g", 16), ("ln_b", 16), ("g_qa", 2), ("g_kva", 1), ("lam", 4), ("g_sub", 1)):
    PCOL[_name] = _at
    _at += _n
N_PCOL = _at


class Chain:

    def __init__(self, eng, sem):
        self.eng, self.sem, self.n, self.reg = eng, sem, 0, None

    def mark(self, ins):
        self.n += 1
        ins.then_inc(self.sem, 1)
        return self.n

    def wait(self, n=None):
        n = self.n if n is None else n
        self.eng.wait_ge(self.sem, n if self.reg is None else self.reg + n)

    def link(self, ins):
        self.mark(ins)
        self.wait()

    @contextmanager
    def loop(self, count, per):
        start = self.n
        with self.eng.Fori(0, count) as i:
            self.reg = i * per
            yield i
            assert self.n - start == per, (self.n - start, per)
            self.reg = None
        self.n = start + per * count


def build(nc, x_t, ctx_t, stream, ada_w, vectors, squares, level_masks, scan_mask, ropes, lora_w, gate_w,
          out_t):
    es = ExitStack()

    base = 16512
    place = [base]

    def at(name, shape, dt, offset):
        return nc.alloc_sbuf_tensor_at(name, shape, dt, offset=offset)

    def fixed(name, shape, dt=F32, size=4):
        n = size
        for s in shape[1:]:
            n *= s
        t = at(name, shape, dt, place[0])
        place[0] += (n + 31) // 32 * 32
        return t

    raw = fixed("raw", [P, 2, WBLK])
    w_hi = fixed("w_hi", [P, 2, TILES, P], F32R)
    w_lo = fixed("w_lo", [P, 2, TILES, P], F32R)
    sq_c = fixed("sq_c", [P, 7, P])
    lvl = fixed("lvl", [P, 12, P], U8, 1)
    prm = fixed("prm", [P, N_PCOL])
    der = fixed("der", [P, 128])
    ada = fixed("ada", [P, 2, 3, KT, 2])
    tmp_at = place[0]
    scan_m = fixed("scan_m", [P, T])
    lora = fixed("lora", [64, HALF])
    gup = fixed("gup", [96, HALF])
    S0 = place[0]
    KB = 1024

    def reg(name, shape, kb, dt=F32):
        return at(name, shape, dt, S0 + int(kb * KB))

    ident, ones, head_ones = sq_c[:, 0, :], sq_c[:, 1, :], sq_c[:, 2, :]
    before, until_m = sq_c[:, 3, :], sq_c[:, 4, :]

    lvl_f = reg("lvl_f", [P, 12, P], 137)
    xT = reg("xT", [P, KT, T], 0)
    h1_hi = reg("h1_hi", [P, KT, T], 16, F32R)
    h1_lo = reg("h1_lo", [P, KT, T], 32, F32R)
    sq = reg("sq", [P, 2, T], 48)
    htmp = reg("htmp", [P, 2, T], 52)
    rstd = reg("rstd", [P, T], 56)
    glu_s = reg("glu_s", [P, 2, T], 58)
    Q = reg("Q", [P, 14, T], 64)
    cpad = reg("cpad", [P, CT, TAPS - 1 + T], 92)
    cacc = reg("cacc", [P, CT, T], 101)
    ada_raw = reg("ada_raw", [P, 2, KT, 256], 109)
    ada_row = reg("ada_row", [32, 2, 256], 125)
    ada_col = reg("ada_col", [P, 4, 32], 127)

    aB = reg("aB", [P, CT, T], 0)
    eA = reg("eA", [P, CT, T], 8)
    lw = reg("lw", [P, CT, T], 16)
    cc = reg("cc", [P, CT, T], 24)
    e1 = reg("e1", [P, CT, T], 32)
    kk = reg("kk", [P, CT, T], 40)
    eR = reg("eR", [P, CT, T], 48)
    gg = reg("gg", [P, CT, T], 56)
    rr, ky, vv = Q[:, 0:4, :], Q[:, 4:8, :], Q[:, 8:12, :]
    A_tok = reg("A_tok", [P, CT, HALF], 16)
    B_tok = reg("B_tok", [P, CT, HALF], 24)
    K_tok = reg("K_tok", [P, CT, HALF], 32)
    V_tok = reg("V_tok", [P, CT, HALF], 40)
    U = reg("U", [P, CT, HALF], 80)
    Di = [reg(f"Di{e}", [P, 4, P], 109 + 13 * e) for e in range(2)]
    DiT = [reg(f"DiT{e}", [P, 4, P], 111 + 13 * e) for e in range(2)]
    Lt = [reg(f"Lt{e}", [P, 4, P], 113 + 13 * e) for e in range(2)]
    Gt = [reg(f"Gt{e}", [P, 4, P], 115 + 13 * e) for e in range(2)]
    Mt = [reg(f"Mt{e}", [P, 4, P], 117 + 13 * e) for e in range(2)]
    RKt = [reg(f"RKt{e}", [P, 4, P], 119 + 13 * e) for e in range(2)]
    MV = [reg(f"MV{e}", [P, 4, 64], 121 + 13 * e) for e in range(2)]
    RBt = [reg(f"RBt{h}", [P, 4, P], 92 + 2 * h if h < 4 else 135 + 2 * (h - 4)) for h in range(8)]
    SA = reg("SA", [P, HALF], 88)
    St = [reg("St0", [P, CT, P], 143), reg("St1", [P, CT, P], 90)]
    sqk = reg("sqk", [P, 2, T], 129)
    knt = reg("knt", [P, 2, T], 133)
    kft = reg("kft", [P, 2, T], 137)

    pairs = [es.enter_context(nc.psum_tensor(f"banks{2 * i}{2 * i + 1}", [P, 2, 512], F32)) for i in range(4)]
    banks = [pairs[i // 2][:, i % 2, :] for i in range(8)]

    def wide(w, n=TA):
        return pairs[w][:, :, :].rearrange("p a b -> p (a b)")[:, 0:n]


    def sem(name):
        return es.enter_context(nc.semaphore(name))

    def col(name, i=0, n=1):
        return prm[:, bass.ds(i + PCOL[name], n)] if not isinstance(i, int) else prm[:, PCOL[name] + i:PCOL[name] + i + n]

    s_x = [sem(f"x_loaded{k}") for k in range(2)]
    s_const = sem("constants_loaded")
    raw_full = [sem("raw_full0"), sem("raw_full1")]
    split_full = sem("split_full")
    block_done = sem("block_done")
    tile0_full = sem("tile0_full")
    hi_done = sem("hi_done")
    ada_full = [sem("ada_full0"), sem("ada_full1")]
    ada_free = [sem("ada_free0"), sem("ada_free1")]
    act_step, dve_step = sem("act_step"), sem("dve_step")
    sq_full, sq_free, sqrt_done = sem("sq_full"), sem("sq_free"), sem("sqrt_done")
    htmp_full = sem("htmp_full")
    h_hi_full, h_ready = sem("h_hi_full"), sem("h_ready")
    proj_free = [sem(f"proj_free{i}") for i in range(4)]
    glu_s_full, glu_s_free = sem("glu_s_full"), sem("glu_s_free")
    q_copied = sem("q_copied")
    silu_c, ada_done = sem("silu_c"), sem("ada_done")
    prep_done = sem("prep_done")
    zeros_done, one_done = sem("zeros_done"), sem("one_done")
    q_mixed = sem("q_mixed")
    conv_done = sem("conv_done")
    out_done = sem("out_done")

    ONE = 124
    OMU, OKA = 0, 14
    SILU_C = 18

    lora_in, lora_full, lora_evac = sem("lora_in"), sem("lora_full"), sem("lora_evac")
    chunk_end, exps_in, exps_done = sem("chunk_end"), sem("exps_in"), sem("exps_done")
    kk_raw, kk_sq, kk_sum, kk_max, kk_root = (sem(n) for n in ("kk_raw", "kk_sq", "kk_sum", "kk_max", "kk_root"))
    bonus_in, bonus_sum, bonus_done = sem("bonus_in"), sem("bonus_sum"), sem("bonus_done")
    ada_rows, ada_rows_free, ada_zero = sem("ada_rows"), sem("ada_rows_free"), sem("ada_zero")
    abkv_ready = sem("abkv_ready")
    tok_full, tok_done = sem("tok_full"), sem("tok_done")
    CT_END, ECT = 40, 72
    cln_sum, cln_centred, cln_sq, cln_root, cln_normed, conv_out = (sem(n) for n in (
        "cln_sum", "cln_centred", "cln_sq", "cln_root", "cln_normed", "conv_out"))
    csq = reg("csq", [P, CT, T], 109)
    cstd = reg("cstd", [P, T], 117)
    PE_STEPS = ["L", "LT", "MT", "RB", "RK", "MV", "Y0"] + [s + str(n) for n in range(1, 6) for s in "GPQ"][:-2] + ["Q5", "W", "U"]
    ACT_STEPS = ["DI", "DIT", "LT", "MV", "Y0", "G1", "G2", "G3", "G4", "G5", "W", "U"]
    DVE_STEPS = ["MT", "RB", "D0", "DT0", "RK"] + [s + str(n) for n in range(1, 5) for s in "PQ"] + ["Q5"]
    u_pe = [sem(f"unit_tensor{e}") for e in range(2)]
    u_act = [sem(f"unit_scalar{e}") for e in range(2)]
    u_dve = [sem(f"unit_vector{e}") for e in range(2)]

    def pe_at(c, step):
        return len(PE_STEPS) * c + PE_STEPS.index(step) + 1

    def act_at(c, step):
        return len(ACT_STEPS) * c + ACT_STEPS.index(step) + 1

    def dve_at(c, step):
        return len(DVE_STEPS) * c + DVE_STEPS.index(step) + 1

    sa_full, sa_done, st_full, st_done, y_full, y_done = (sem(n) for n in ("sa_full", "sa_done", "st_full", "st_done", "y_full", "y_done"))
    st_zero = sem("st_zero")
    mixo = reg("mixo", [P, KT, T], 64)
    fout = reg("fout", [P, KT, T], 16)
    act_hi = reg("act_hi", [P, FT, T], 48, F32R)
    act_lo = reg("act_lo", [P, FT, T], 92, F32R)
    yg = reg("yg", [P, 2, T], 136)
    yu = reg("yu", [P, 2, T], 140)
    nt = at("nt", [P, 2, T], F32, tmp_at)
    nr = at("nr", [P, T], F32, tmp_at + 4 * KB)
    nh = reg("nh", [P, 2, T], 140)
    nacc = reg("nacc", [P, T], 138)
    msq = reg("msq", [P, 2, T], 121)
    mrs = reg("mrs", [P, 2, T], 125)
    gn_mean, gn_centred, gn_sq, gn_var, gn_root, gn_normed, gn_scaled, mix_full, mix_hi_full, mix_ready = (sem(n) for n in (
        "gn_mean", "gn_centred", "gn_sq", "gn_var", "gn_root", "gn_normed", "gn_scaled", "mix_full", "mix_hi_full", "mix_ready"))
    x_again = sem("x_again")
    out_copied, out_sq, out_summed = sem("out_copied"), sem("out_sq"), sem("out_summed")
    post_sum, post_root, x_done, pre_sq, pre_sq_read, pre_root = (sem(n) for n in (
        "post_sum", "post_root", "x_done", "pre_sq", "pre_sq_read", "pre_root"))
    nh_full, nh_hi, nh_ready = sem("nh_full"), sem("nh_hi"), sem("nh_ready")
    up_first, up_conv, up_gelu, up_prod, up_hi, act_ready = (sem(n) for n in (
        "up_first", "up_conv", "up_gelu", "up_prod", "up_hi", "act_ready"))
    down_full, down_free, conv2 = sem("down_full"), sem("down_free"), sem("ffn_conv_step")

    def half_of(n):
        return n % 2

    def both_parts(k):
        return (k + CT) % KT
    gate_s = reg("gate_s", [P, KT, TA], 16)
    lat = reg("lat", [P, 3, TA], 40)
    lat_hi = reg("lat_hi", [P, 3, TA], 49, F32R)
    lat_lo = reg("lat_lo", [P, 3, TA], 58, F32R)
    h2_hi = reg("h2_hi", [P, KT, TA], 67, F32R)
    h2_lo = reg("h2_lo", [P, KT, TA], 91, F32R)
    ctxT = reg("ctxT", [P, KT, C], 115)
    mh = reg("mh", [P, 2, TA], 123)
    lsq = reg("lsq", [P, 2, TA], 129)
    lrs = reg("lrs", [P, TA], 135)
    qT = [reg(f"qT{h}", [P, TA], 115 + 3 * h) for h in range(2)]
    kT = [reg(f"kT{h}", [P, TA], 121 + 3 * h) for h in range(2)]
    Vt = reg("Vt", [P, 6, P], 127)
    Pm = [reg(f"Pm{h}", [P, TA], 130 + 3 * h) for h in range(2)]
    PT = reg("PT", [P, 6, P], 136)
    Ob = reg("Ob", [P, 6, P], 139)
    otmp = reg("otmp", [P, TA], 142)
    rope = at("rope", [P, 2, T], F32, tmp_at)
    z = reg("z", [P, KT, TA], 16)
    ctx2 = reg("ctx2", [P, KT, C], 40)
    zacc = reg("zacc", [P, TA], 115)
    zsq = reg("zsq", [P, 2, TA], 118)
    zrs = reg("zrs", [P, TA], 124)
    zh = reg("zh", [P, 2, TA], 127)
    MX, NM, RS, RL = 40, 52, 64, 76
    s_ctx, s_rope = sem("ctx_loaded"), sem("rope_loaded")
    mh_full, mh_hi, mh_ready = sem("mh_full"), sem("mh_hi"), sem("mh_ready")
    wide_free = [sem("wide_free0"), sem("wide_free1")]
    wide_full = sem("wide_full")
    lat_sq, lat_sum, lat_root, lat_normed, lat_high, lat_ready = (sem(n) for n in (
        "lat_sq", "lat_sum", "lat_root", "lat_normed", "lat_high", "lat_ready"))
    kpe_copied, kpe_rot, kpe_done, gate_done = sem("kpe_copied"), sem("kpe_rot"), sem("kpe_done"), sem("gate_done")
    pr_evac, rope_done = sem("head_evac"), sem("rope_done")
    nm_ready, p_full, ta_full, tb_full, eva_done, evb_done, pv_done, o_done = (sem(n) for n in (
        "nm_ready", "p_full", "ta_full", "tb_full", "eva_done", "evb_done", "pv_done", "o_done"))
    ot_done, ot_hi, ot_ready = sem("ot_done"), sem("ot_hi"), sem("ot_ready")
    z_gated, z_acc, z_sum, z_centred, z_sq, z_root, z_normed, z_out = (sem(n) for n in (
        "z_gated", "z_acc", "z_sum", "z_centred", "z_sq", "z_root", "z_normed", "z_out"))
    ada_one = sem("ada_one")
    z1 = reg("z1", [P, KT, T], 0)

    def z_of(layer):
        return z if layer == 0 else z1
    A_SCALE = (A_QK) ** -0.5
    T0_MLA = STREAM["down"]
    KEYS = [slice(0, TA)] * 4 + [slice(T, TA)] * 2
    O_tok = reg("O_tok", [P, 4, D], 0)
    gate2 = reg("gate2", [P, KT, T], 40)
    dq = reg("dq", [P, T], 115)
    dk = reg("dk", [P, TA], 117)
    dV = reg("dV", [P, 6, P], 120)
    dP = [reg(f"dP{i}", [P, TA], 123 + 3 * i) for i in range(2)]
    dPT = reg("dPT", [P, 6, P], 129)
    dv = reg("dv", [P, TA], 132)
    dt = reg("dt", [P, T], 135)
    o_first = reg("o_first", [P, P], 137)
    o_junk = reg("o_junk", [P, 2, P], 143)
    og = reg("og", [P, 2, T], 138)
    o_ss = reg("o_ss", [P, 32], 142)
    o_rs = reg("o_rs", [P, 32], 142.25)
    NL, LAM = 88, 96
    lam_prod, lam_sum, lam_exp, rope_k = (sem(n) for n in ("lam_prod", "lam_sum", "lam_exp", "q_turned"))
    o_sq, o_root, o_scaled, og_full, og_hi, og_ready = (sem(n) for n in (
        "o_sq", "o_root", "o_scaled", "og_full", "og_hi", "og_ready"))
    B_SCALE = B_D ** -0.5
    N_MLA_UNITS = 12 * A_HEADS // 2
    N_MLA_FULL = 17 * A_HEADS // 2
    N_MLA_XUNITS = 8 * A_HEADS // 2
    N_MLA_EVAC = 4 * A_HEADS // 2
    N_MLA_USES = 6 + 9 * A_HEADS // 2 + 4
    D_USES, D_FULL, D_UNITS, D_EVAC = 7, 12, 8, 5
    block = es.enter_context(nc.Block())

    @block.sync
    def _(sp):
        for k in range(2):
            sp.dma_start(xT[:, 4 * k:4 * k + 4, :], x_t[:, 4 * k:4 * k + 4, :]).then_inc(s_x[k], 16)
        sp.dma_start(prm[:, :], vectors).then_inc(s_const, 16)
        sp.dma_start(sq_c[:, :, :], squares).then_inc(s_const, 16)
        sp.dma_start(lvl_f[:, :, :], level_masks).then_inc(s_const, 16)
        sp.dma_start(scan_m[:, :], scan_mask).then_inc(s_const, 16)
        sp.dma_start(lora[:, :], lora_w).then_inc(s_const, 16)
        sp.dma_start(gup[:, :], gate_w).then_inc(s_const, 16)

        def weights(n, half, first=False):
            if not first:
                sp.wait_ge(split_full, n - 1)
            sp.dma_start(raw[:, half, :], stream[n, :, :]).then_inc(raw_full[half], 16)

        def ada_block(b, half, use, first=False):
            if not first:
                sp.wait_ge(ada_free[half], use)
            sp.dma_start(ada_raw[:, half, :, :], ada_w[b, :, :, :]).then_inc(ada_full[half], 16)

        for s in range(2):
            weights(s, s, first=True)
        with sp.Fori(0, N_IN // 2 - 1) as i:
            for s in range(2):
                weights(2 * i + (2 + s), s)
        weights(N_IN - 1, 0)
        for a in range(2):
            ada_block(a, a, 0, first=True)
        with sp.Fori(1, ADA_BLOCKS // 2) as i:
            for a in range(2):
                ada_block(2 * i + a, a, i)
        weights(N_IN, 1)
        with sp.Fori(0, (N_BLOCKS - N_IN - 1) // 2) as i:
            for s in range(2):
                weights(2 * i + (N_IN + 1 + s), s)
        if (N_BLOCKS - N_IN - 1) % 2:
            weights(N_BLOCKS - 1, 0)
        for k in range(KT):
            sp.wait_ge(z_out, KT + k + 1)
            sp.dma_start(out_t[:, k, :], z1[:, k, :]).then_inc(out_done, 16)
        sp.wait_ge(out_done, 16 * KT)

    @block.gpsimd
    def _(pool):
        def split(n, half, use, first=False):
            pool.wait_ge(raw_full[half], 16 * (use + 1))
            if not first:
                pool.wait_ge(block_done, n - 1)
            src = raw[:, half, :].rearrange("p (t c) -> p t c", t=TILES)
            pool.tensor_tensor(w_hi[:, half, :, :], src, one, ALU.mult).then_inc(hi_done, 1)
            pool.wait_ge(hi_done, n + 1)
            pool.tensor_tensor(w_lo[:, half, :, :], src, w_hi[:, half, :, :], ALU.subtract).then_inc(split_full, 1)

        pool.memset(der[:, ONE:ONE + 1], 1.0).then_inc(one_done, 1)
        pool.wait_ge(one_done, 1)
        one = der[:, ONE:ONE + 1].unsqueeze(1).broadcast_to([P, TILES, P])
        pool.memset(cpad[:, :, 0:TAPS - 1], 0.0).then_inc(zeros_done, 1)
        total = N_BLOCKS
        for s in range(2):
            split(s, s, 0, first=True)
        with pool.Fori(0, total // 2 - 1) as i:
            for s in range(2):
                split(2 * i + (2 + s), s, i + 1)
        if total % 2:
            split(total - 1, 0, total // 2)

    @block.tensor
    def _(pe):
        pe.wait_ge(s_const, 96)
        for k in range(KT):
            pe.wait_ge(sq_full, k + 1)
            pe.matmul(banks[6][:, :], ones, sq[:, k % 2, :], start=(k == 0), stop=(k == KT - 1)).then_inc(sq_free, 1)

        def project(bank_of, half, n, frees, rhs_hi, rhs_lo, tiles=2):
            pe.wait_ge(split_full, n + 1)
            for j in range(tiles):
                b = bank_of[j]
                pe.wait_ge(proj_free[b], frees)
                for k in range(KT):
                    t = KT * j + k
                    hi, lo = w_hi[:, half, t, :], w_lo[:, half, t, :]
                    pe.matmul(banks[b][:, :], hi, rhs_hi[:, k, :], start=(k == 0), stop=False)
                    pe.matmul(banks[b][:, :], hi, rhs_lo[:, k, :], start=False, stop=False)
                    mm = pe.matmul(banks[b][:, :], lo, rhs_hi[:, k, :], start=False, stop=(k == KT - 1))
                mm.then_inc(tile0_full if j == 0 else block_done, 1)

        pe.wait_ge(h_ready, KT)
        with pe.Fori(0, N_IN // 2) as i:
            for s in range(2):
                project([2 * s, 2 * s + 1], s, 2 * i + s, i + 1, h1_hi, h1_lo)
        project([0, 1], 0, N_IN - 1, N_IN // 2 + 1, h1_hi, h1_lo)
        pe.wait_ge(lora_in, 2)
        for c in range(CT):
            for j, (w, x) in enumerate(((lora[0:32], Q[0:32, 12]), (lora[32:64], Q[32:64, 12]), (gup[0:96], Q[0:96, 13]))):
                m = 3 * c + j
                if m == 0:
                    pe.wait_ge(q_mixed, 14)
                if m >= 6:
                    pe.wait_ge(lora_evac, m - 5)
                pe.matmul(banks[m % 6][:, :], w[:, P * c:P * c + P], x, start=True, stop=True).then_inc(lora_full, 1)

        def ada_rows_of(g):
            if g >= 2:
                pe.wait_ge(ada_rows_free, g - 1)
            for a in range(2):
                pe.wait_ge(ada_full[a], 16 * (g + 1))
                for k in range(KT):
                    mm = pe.matmul(banks[6 + g % 2][0:2, 256 * a:256 * a + 256], der[:, SILU_C + 2 * k:SILU_C + 2 * k + 2],
                                   ada_raw[:, a, k, :], start=(k == 0), stop=(k == KT - 1))
                mm.then_inc(ada_free[a] if a == 0 else ada_rows, 1)

        def head_sums(ready, src, full, b0, c):
            pe.wait_ge(ready, c + 1)
            pe.matmul(banks[b0 + c][:, :], head_ones, src, start=True, stop=True).then_inc(full, 1)

        pe.wait_ge(silu_c, 1)
        for c in range(CT):
            if c < 2:
                pe.wait_ge(lora_evac, 7 + c)
            head_sums(kk_sq, sqk[:, c % 2, :], kk_sum, 0, c)
            ada_rows_of(c)
        for g in range(4, 8):
            ada_rows_of(g)
        for c in range(CT):
            if c < 2:
                pe.wait_ge(lora_evac, 11 + c)
            head_sums(bonus_in, rr[:, c, :], bonus_sum, 0, c)
        for g in range(8, 12):
            ada_rows_of(g)
        n = 0
        for a, src in enumerate((eA, aB, ky, vv)):
            pe.wait_ge(abkv_ready, min(a + 1, 3))
            for tt in range(4):
                b = n % 4
                if n < 4:
                    pe.wait_ge(bonus_done, CT)
                else:
                    pe.wait_ge(tok_done, n - 3)
                for c in range(CT):
                    mm = pe.transpose(banks[b][:, P * c:P * c + P], src[:, c, P * tt:P * tt + P], ident)
                mm.then_inc(tok_full, 1)
                n += 1
        def unit(c, e, step):
            X = banks[4 * e:4 * e + 4]
            rows, h = slice(64 * e, 64 * e + 64), 2 * c + e
            cols = slice(64 * h, 64 * h + 64)
            if step == "L":
                if c == 0:
                    pe.wait_ge(tok_done, 16)
                    pe.wait_ge(ada_rows_free, 12)
                else:
                    pe.wait_ge(u_act[e], act_at(c - 1, "W"))
                b, lhs, rhs = X[0], eA[rows, c, :], aB[rows, c, :]
            elif step == "LT":
                if c:
                    pe.wait_ge(u_act[e], act_at(c - 1, "U"))
                b, lhs, rhs = X[1], aB[rows, c, :], eA[rows, c, :]
            elif step == "MT":
                if c:
                    pe.wait_ge(u_dve[e], dve_at(c - 1, "Q5"))
                b, lhs, rhs = X[2], ky[rows, c, :], eA[rows, c, :]
            elif step == "RB":
                if c:
                    pe.wait_ge(u_act[e], act_at(c - 1, "Y0"))
                b, lhs, rhs = X[3], aB[rows, c, :], eR[rows, c, :]
            elif step == "RK":
                pe.wait_ge(u_dve[e], dve_at(c, "MT"))
                b, lhs, rhs = X[2], ky[rows, c, :], eR[rows, c, :]
            elif step == "MV":
                pe.wait_ge(u_dve[e], dve_at(c, "RB"))
                for tt in range(4):
                    mm = pe.matmul(X[3][:, 64 * tt:64 * tt + 64], Mt[e][:, tt, :], V_tok[:, tt, cols], start=True, stop=True)
                mm.then_inc(u_pe[e], 1)
                return
            elif step == "Y0":
                pe.wait_ge(u_dve[e], dve_at(c, "RK"))
                pe.wait_ge(u_act[e], act_at(c, "MV"))
                for tt in range(4):
                    mm = pe.matmul(X[3][rows, P * tt:P * tt + P], V_tok[:, tt, cols], RKt[e][:, tt, :], start=True, stop=True)
                mm.then_inc(u_pe[e], 1)
                return
            elif step == "W":
                pe.wait_ge(u_dve[e], dve_at(c, "Q5"))
                for tt in range(4):
                    mm = pe.matmul(X[0][rows, P * tt:P * tt + P], A_tok[:, tt, cols], DiT[e][:, tt, :], start=True, stop=True)
                mm.then_inc(u_pe[e], 1)
                return
            elif step == "U":
                for tt in range(4):
                    mm = pe.matmul(X[1][:, 64 * tt:64 * tt + 64], DiT[e][:, tt, :], MV[e][:, tt, :], start=True, stop=True)
                mm.then_inc(u_pe[e], 1)
                return
            else:
                n = int(step[1])
                if step[0] == "G":
                    if n == 1:
                        pe.wait_ge(u_act[e], act_at(c, "LT"))
                        pe.wait_ge(u_dve[e], dve_at(c, "DT0"))
                    else:
                        pe.wait_ge(u_dve[e], dve_at(c, f"Q{n - 1}"))
                    b, lhs, rhs = X[0], Lt[e], Di[e]
                elif step[0] == "P":
                    pe.wait_ge(u_act[e], act_at(c, f"G{n}"))
                    b, lhs, rhs = X[1], DiT[e], Gt[e]
                else:
                    if n == 1:
                        pe.wait_ge(u_dve[e], dve_at(c, "RK"))
                    pe.wait_ge(u_act[e], act_at(c, f"G{n}"))
                    b, lhs, rhs = X[2], Gt[e], DiT[e]
                for tt in range(4):
                    mm = pe.matmul(b[:, P * tt:P * tt + P], lhs[:, tt, :], rhs[:, tt, :], start=True, stop=True)
                mm.then_inc(u_pe[e], 1)
                return
            for tt in range(4):
                ts = slice(P * tt, P * tt + P)
                mm = pe.matmul(b[:, ts], lhs[:, ts], rhs[:, ts], start=True, stop=True)
            mm.then_inc(u_pe[e], 1)

        for c in range(CT):
            for step in PE_STEPS:
                for e in range(2):
                    unit(c, e, step)

        pe.wait_ge(st_zero, 1)
        for e in range(2):
            pe.wait_ge(u_act[e], act_at(CT - 1, "U"))
        for n in range(NCH):
            tt, r = n // 2, slice(64 * (n % 2), 64 * (n % 2) + 64)
            t0 = CHUNK * n
            state = St[n % 2]
            if n:
                pe.wait_ge(st_done, 2 * n)
            for c in range(CT):
                mm = pe.matmul(banks[0][r, P * c:P * c + P], eA[:, c, t0:t0 + CHUNK], state[:, c, :], start=True, stop=True)
            mm.then_inc(sa_full, 1)
            if n >= 2:
                pe.wait_ge(y_done, n - 1)
            yb = banks[2 + n % 2]
            for c in range(CT):
                pe.matmul(yb[:, CHUNK * c:CHUNK * c + CHUNK], state[:, c, :], eR[:, c, t0:t0 + CHUNK], start=(c == 0), stop=False,
                          skip_group_check=True)
            if n < NCH - 1:
                for c in range(CT):
                    pe.matmul(banks[1][:, P * c:P * c + P], ident, state[:, c, :], start=(c == 0), stop=False, skip_group_check=True)
            pe.wait_ge(sa_done, n + 1)
            if n < NCH - 1:
                for c in range(CT):
                    ch = slice(P * c, P * c + P)
                    pe.matmul(banks[1][:, ch], B_tok[r, tt, ch], SA[r, ch], start=False, stop=False, skip_group_check=True)
                    mm = pe.matmul(banks[1][:, ch], K_tok[r, tt, ch], V_tok[r, tt, ch], start=False, stop=(c == CT - 1), skip_group_check=True)
                mm.then_inc(st_full, 1)
            for h in range(8):
                c, hr = h // 2, slice(64 * (h % 2), 64 * (h % 2) + 64)
                mm = pe.matmul(yb[hr, CHUNK * c:CHUNK * c + CHUNK], SA[r, 64 * h:64 * h + 64],
                               RBt[h][r, tt, 64 * (n % 2):64 * (n % 2) + 64], start=False, stop=(h == 7), skip_group_check=True)
            mm.then_inc(y_full, 1)
            if n == 0:
                for c in range(CT):
                    mm = pe.matmul(banks[4][:, :], ones, cacc[:, c, :], start=(c == 0), stop=(c == CT - 1))
                mm.then_inc(cln_sum, 1)
            if n == 3:
                for c in range(CT):
                    pe.wait_ge(cln_sq, c + 1)
                    pe.matmul(banks[5][:, :], ones, csq[:, c, :], start=(c == 0), stop=(c == CT - 1)).then_inc(cln_sum, 1)
        pe.wait_ge(y_done, NCH)
        for c in range(CT):
            pe.matmul(banks[4 + c][:, :], head_ones, ky[:, c, :], start=True, stop=True).then_inc(gn_mean, 1)
        for c in range(CT):
            pe.wait_ge(gn_sq, c + 1)
            pe.matmul(banks[4 + c][:, :], head_ones, msq[:, c % 2, :], start=True, stop=True).then_inc(gn_var, 1)
        pe.wait_ge(mix_ready, KT)
        for n in range(STREAM["out"], STREAM["out"] + N_OUT):
            s = half_of(n)
            project([2 * s, 2 * s + 1], s, n, n // 2 + 1, h1_hi, h1_lo)

        def post_and_pre(m):
            pe.wait_ge(out_summed, KT * (m + 1))
            pe.matmul(banks[6][:, :], ones, nacc[:, :], start=True, stop=True).then_inc(post_sum, 1)
            if m == 0:
                for k in range(KT):
                    pe.wait_ge(pre_sq, k + 1)
                    pe.matmul(banks[7][:, :], ones, nt[:, k % 2, :], start=(k == 0), stop=(k == KT - 1)).then_inc(pre_sq_read, 1)

        post_and_pre(0)
        pe.wait_ge(nh_ready, KT)
        with pe.Fori(0, N_UP // 2) as i:
            for u in range(2):
                s = half_of(STREAM["up"] + u)
                n = 2 * i + (STREAM["up"] + u)
                project([2 * s, 2 * s + 1], s, n, i + (STREAM["up"] + u) // 2 + 1, h1_hi, h1_lo)
        pe.wait_ge(act_ready, FT)
        with pe.Fori(0, 2) as i:
            for u in range(6):
                s = half_of(STREAM["down"] + u)
                pe.wait_ge(split_full, 6 * i + (STREAM["down"] + u + 1))
                for t in range(TILES):
                    t_of = TILES * (u % 3) + t
                    j, k = t_of // FT, t_of % FT
                    if j == 2:
                        break
                    m = 2 * (u // 3) + j
                    b = banks[4 + m]
                    if k == 0:
                        pe.wait_ge(down_free, 4 * i + (m + 1))
                    hi, lo = w_hi[:, s, t, :], w_lo[:, s, t, :]
                    pe.matmul(b[:, :], hi, act_hi[:, k, :], start=(k == 0), stop=False)
                    pe.matmul(b[:, :], hi, act_lo[:, k, :], start=False, stop=False)
                    mm = pe.matmul(b[:, :], lo, act_hi[:, k, :], start=False, stop=(k == FT - 1))
                    if k == FT - 1 and j == 0:
                        mm.then_inc(down_full, 1)
                mm.then_inc(block_done, 1)
        post_and_pre(1)
        def wide_project(j, k0, kn, w, s, rhs_hi, rhs_lo, n_cols=TA, tile0=0):
            for k in range(kn):
                t = tile0 + k
                hi, lo = w_hi[:, s, t, :], w_lo[:, s, t, :]
                for a, b in ((0, 512), (512, TA)):
                    if a >= n_cols:
                        continue
                    out = pairs[w][:, a // 512, 0:b - a]
                    pe.matmul(out, hi, rhs_hi[:, k0 + k, a:b], start=(k == 0), stop=False)
                    pe.matmul(out, hi, rhs_lo[:, k0 + k, a:b], start=False, stop=False)
                for a, b in ((0, 512), (512, TA)):
                    if a >= n_cols:
                        continue
                    mm = pe.matmul(pairs[w][:, a // 512, 0:b - a], lo, rhs_hi[:, k0 + k, a:b], start=False, stop=(k == kn - 1))
            return mm

        def wide_sum(src, n, first, last, w=2):
            for a, b in ((0, 512), (512, n)):
                mm = pe.matmul(pairs[w][:, a // 512, 0:b - a], ones, src[:, a:b], start=first, stop=last, skip_group_check=True)
            return mm

        pe.wait_ge(mh_ready, KT)
        for m in range(12):
            n = STREAM["mla_in"] + m // 2
            if m % 2 == 0:
                pe.wait_ge(split_full, n + 1)
            if m >= 2:
                pe.wait_ge(wide_free[m % 2], m // 2)
            mm = wide_project(0, 0, KT, m % 2, half_of(n), h2_hi, h2_lo, tile0=KT * (m % 2))
            mm.then_inc(tile0_full if m % 2 == 0 else block_done, 1)
            if m == 3:
                for c in range(2):
                    pe.wait_ge(lat_sq, c + 1)
                    mm = wide_sum(lsq[:, c, :], TA, c == 0, c == 1)
                mm.then_inc(lat_sum, 1)
            if m == 5:
                pe.wait_ge(lat_root, 1)
                pe.wait_ge(lat_sq, 3)
                wide_sum(lsq[:, 0, :], TA, True, True).then_inc(lat_sum, 1)
                pe.wait_ge(kpe_copied, 1)
                pe.matmul(banks[6][64:96, :], sq_c[64:96, 5, 64:96], kT[0][64:96, 0:T], start=True, stop=True).then_inc(kpe_rot, 1)

        def mla_pair(u, p):
            n = STREAM["mla"] + u
            s = half_of(n)
            pe.wait_ge(split_full, p + (STREAM["mla"] + 1))

            def take(i):
                pe.wait_ge(wide_free[i % 2], 9 * p + (6 + i // 2))
                return i % 2

            w = take(0)
            wide_project(0, 0, 2, w, s, lat_hi, lat_lo, tile0=0).then_inc(wide_full, 1)
            w = take(1)
            wide_project(0, 2, 1, w, s, lat_hi, lat_lo, tile0=4).then_inc(wide_full, 1)
            w = take(2)
            wide_project(0, 0, 2, w, s, lat_hi, lat_lo, tile0=2).then_inc(wide_full, 1)
            w = take(3)
            for tt in range(6):
                out = wide(w)[:, P * tt:P * tt + P]
                ts = slice(P * tt, P * tt + P)
                pe.matmul(out, lat_hi[:, 2, ts], w_hi[:, s, 5, :], start=True, stop=False)
                pe.matmul(out, lat_hi[:, 2, ts], w_lo[:, s, 5, :], start=False, stop=False)
                mm = pe.matmul(out, lat_lo[:, 2, ts], w_hi[:, s, 5, :], start=False, stop=True)
            mm.then_inc(block_done, 1)
            w = take(4)
            pe.wait_ge(pr_evac, 4 * p + 3)
            for hh in range(2):
                mm = pe.matmul(pairs[w][0:96, hh, :], sq_c[0:96, 5, 0:96], qT[hh][0:96, 0:T], start=True, stop=True)
            mm.then_inc(wide_full, 1)

            def scores(v):
                hh, qt = v // 6, v % 6
                if v % 6 == 0:
                    pe.wait_ge(rope_done, 2 * p + (hh + 1))
                w = take(5 + v)
                q = qT[hh][0:96, P * qt:P * qt + P]
                if qt < 4:
                    pe.matmul(pairs[w][:, 0, :], q, kT[hh][0:96, 0:512], start=True, stop=True)
                    mm = pe.matmul(pairs[w][:, 1, 0:256], q, kT[hh][0:96, 512:TA], start=True, stop=True)
                else:
                    mm = pe.matmul(pairs[w][:, 0, 0:256], q, kT[hh][0:96, 512:TA], start=True, stop=True)
                mm.then_inc(wide_full, 1)

            def turn(v):
                pe.wait_ge(p_full, 12 * p + (v + 1))
                kts = range(6) if v % 6 < 4 else range(2)
                for kt in kts:
                    mm = pe.transpose(banks[4 + kt // 3][:, P * (kt % 3):P * (kt % 3) + P], Pm[v % 2][:, P * kt:P * kt + P], ident)
                    if kt == 2 or len(kts) == 2 and kt == 1:
                        mm.then_inc(ta_full, 1)
                if len(kts) == 6:
                    mm.then_inc(tb_full, 1)

            def values(v):
                hh, qt = v // 6, v % 6
                pe.wait_ge(eva_done, 12 * p + (v + 1))
                if v >= 2:
                    pe.wait_ge(o_done, 12 * p + (v - 1))
                kts = range(6) if qt < 4 else range(2)
                if qt < 4:
                    pe.wait_ge(evb_done, 8 * p + (4 * hh + qt + 1))
                if v == 0:
                    pe.wait_ge(pr_evac, 4 * p + 4)
                for kt in kts:
                    vk = kt if qt < 4 else 4 + kt
                    mm = pe.matmul(banks[6 + v % 2][:, 0:P], PT[:, kt, :], Vt[:, vk, :], start=(kt == 0), stop=(kt == kts[-1]))
                mm.then_inc(pv_done, 1)

            scores(0)
            for v in range(12):
                if v + 1 < 12:
                    scores(v + 1)
                if v:
                    values(v - 1)
                turn(v)
            values(11)
            w = take(17)
            pe.wait_ge(o_done, 12 * p + 12)
            for tt in range(6):
                mm = pe.transpose(wide(w)[:, P * tt:P * tt + P], Ob[:, tt, :], ident)
            mm.then_inc(wide_full, 1)

        pe.wait_ge(lat_ready, 3)
        pe.wait_ge(kpe_done, 1)
        with pe.Fori(0, A_HEADS // 4) as i:
            for u in range(2):
                mla_pair(u, 2 * i + u)

        def residual_product(name, before_uses, n_cols, tile0_before, layer):
            for m in range(KT):
                n = STREAM[name] + m // 2
                if m % 2 == 0:
                    pe.wait_ge(split_full, n + 1)
                pe.wait_ge(wide_free[m % 2], before_uses + m // 2)
                mm = wide_project(0, 0, KT, m % 2, half_of(n), h2_hi, h2_lo, n_cols=n_cols, tile0=KT * (m % 2))
                mm.then_inc(tile0_full if m % 2 == 0 else block_done, 1)
            pe.wait_ge(z_acc, KT * (layer + 1))
            wide_sum(zacc, n_cols, True, True).then_inc(z_sum, 1) if n_cols > 512 else \
                pe.matmul(banks[4][:, :], ones, zacc[:, 0:T], start=True, stop=True).then_inc(z_sum, 1)
            for k in range(KT):
                pe.wait_ge(z_sq, KT * layer + k + 1)
                if n_cols > 512:
                    for a, b in ((0, 512), (512, TA)):
                        mm = pe.matmul(pairs[3][:, a // 512, 0:b - a], ones, zsq[:, k % 2, a:b], start=(k == 0), stop=(k == KT - 1),
                                       skip_group_check=True)
                else:
                    mm = pe.matmul(banks[6][:, :], ones, zsq[:, k % 2, 0:T], start=(k == 0), stop=(k == KT - 1))
                mm.then_inc(z_sum, 1)

        pe.wait_ge(ot_ready, A_HEADS // 2)
        residual_product("mla_out", 6 + 9 * 8, TA, 0, 0)
        pe.wait_ge(mh_ready, 2 * KT)
        pe.wait_ge(lam_prod, 1)
        pe.matmul(banks[4][:, 0:2], ones[0:64, :], der[0:64, LAM:LAM + 2], start=True, stop=True).then_inc(lam_sum, 1)

        with pe.Fori(0, B_HEADS) as h:
            def take(i):
                pe.wait_ge(wide_free[i % 2], D_USES * h + (N_MLA_USES + i // 2))
                return i % 2

            A, B = half_of(STREAM["diff"]), half_of(STREAM["diff"] + 1)
            pe.wait_ge(split_full, 2 * h + (STREAM["diff"] + 1))
            wide_project(0, 0, KT, take(0), A, h2_hi, h2_lo, n_cols=T).then_inc(wide_full, 1)
            wide_project(0, 0, KT, take(1), A, h2_hi, h2_lo, tile0=KT).then_inc(block_done, 1)
            pe.wait_ge(split_full, 2 * h + (STREAM["diff"] + 2))
            wide_project(0, 0, KT, take(2), B, h2_hi, h2_lo).then_inc(wide_full, 1)
            wide_project(0, 0, KT, take(3), B, h2_hi, h2_lo, n_cols=T, tile0=KT).then_inc(block_done, 1)
            take(4)
            pe.wait_ge(pr_evac, D_EVAC * h + (N_MLA_EVAC + 2))
            pe.matmul(pairs[0][:, 0, :], sq_c[:, 6, :], dq[:, :], start=True, stop=True)
            pe.matmul(pairs[0][:, 1, :], sq_c[:, 6, :], dk[:, 0:T], start=True, stop=True).then_inc(wide_full, 1)
            take(5)
            pe.wait_ge(pr_evac, D_EVAC * h + (N_MLA_EVAC + 3))
            for kt in range(6):
                mm = pe.transpose(wide(1)[:, P * kt:P * kt + P], dv[:, P * kt:P * kt + P], ident)
            mm.then_inc(wide_full, 1)

            def scores(v):
                qt, m = v // 2, v % 2
                if v == 0:
                    pe.wait_ge(rope_done, h + (A_HEADS + 1))
                w = take(6 + v)
                q, rows = dq[64 * m:64 * m + 64, P * qt:P * qt + P], slice(64 * m, 64 * m + 64)
                pe.matmul(pairs[w][:, 0, :], q, dk[rows, 0:512], start=True, stop=True)
                pe.matmul(pairs[w][:, 1, 0:256], q, dk[rows, 512:TA], start=True, stop=True).then_inc(wide_full, 1)

            def turn(v):
                pe.wait_ge(p_full, D_UNITS * h + (N_MLA_UNITS + v + 1))
                for kt in range(6):
                    mm = pe.transpose(banks[4 + kt // 3][:, P * (kt % 3):P * (kt % 3) + P], dP[v % 2][:, P * kt:P * kt + P], ident)
                    if kt % 3 == 2:
                        mm.then_inc([ta_full, tb_full][kt // 3], 1)

            def values(v):
                pe.wait_ge(eva_done, D_UNITS * h + (N_MLA_UNITS + v + 1))
                pe.wait_ge(evb_done, D_UNITS * h + (N_MLA_XUNITS + v + 1))
                pe.wait_ge(o_done, D_UNITS * h + (N_MLA_UNITS + v - 1))
                if v == 0:
                    pe.wait_ge(pr_evac, D_EVAC * h + (N_MLA_EVAC + 5))
                for kt in range(6):
                    mm = pe.matmul(banks[6 + v % 2][:, 0:P], dPT[:, kt, :], dV[:, kt, :], start=(kt == 0), stop=(kt == 5))
                mm.then_inc(pv_done, 1)

            scores(0)
            for v in range(8):
                if v + 1 < 8:
                    scores(v + 1)
                if v:
                    values(v - 1)
                turn(v)
            values(7)

        pe.wait_ge(o_scaled, 4)
        for h in range(B_HEADS):
            pe.wait_ge(wide_free[h % 2], N_MLA_USES + D_USES * B_HEADS + h // 2)
            for qt in range(4):
                mm = pe.transpose(wide(h % 2)[:, P * qt:P * qt + P], O_tok[:, qt, P * h:P * h + P], ident)
            mm.then_inc(wide_full, 1)
        pe.wait_ge(og_ready, KT)
        residual_product("diff_out", N_MLA_USES + D_USES * B_HEADS + KT // 2, T, 0, 1)

    @block.scalar
    def _(act):
        chain = Chain(act, act_step)
        for k in range(KT):
            act.wait_ge(s_x[k // 4], 16)
            if k >= 2:
                act.wait_ge(sq_free, k - 1)
            act.activation(sq[:, k % 2, :], xT[:, k, :], ACT.Square).then_inc(sq_full, 1)
        act.wait_ge(s_const, 96)
        act.activation(der[:, SILU_C:SILU_C + 16], col("c", 0, 16), ACT.Silu).then_inc(silu_c, 1)
        act.wait_ge(sq_free, KT)
        act.wait_ge(prep_done, 2)
        act.activation(rstd[:, :], banks[6][:, :], ACT.Sqrt, scale=1.0 / D, bias=der[:, 127:128]).then_inc(sqrt_done, 1)
        for k in range(KT):
            act.wait_ge(htmp_full, k + 1)
            act.activation(h1_hi[:, k, :], htmp[:, k % 2, :], ACT.Copy).then_inc(h_hi_full, 1)
        with act.Fori(0, 2) as i:
            for s in range(2):
                act.wait_ge(block_done, 2 * i + (s + 1))
                act.wait_ge(glu_s_free, 2 * i + (s + 1))
                act.activation(glu_s[:, s, :], banks[2 * s + 1][:, :], ACT.Sigmoid).then_inc(glu_s_full, 1)

        def q_tile(j, b, n):
            act.wait_ge(tile0_full if b % 2 == 0 else block_done, n + 1)
            act.activation(Q[:, j, :], banks[b][:, :], ACT.Copy, scale=der[:, bass.ds(j + OMU, 1)]).then_inc(q_copied, 1)

        with act.Fori(0, 3) as i:
            for s in range(4):
                q_tile(4 * i + s, s, 2 * i + (4 + s // 2))
        for s in range(2):
            q_tile(12 + s, s, N_IN - 1)
        act.wait_ge(q_mixed, 14)
        act.activation(Q[0:32, 12, :], Q[0:32, 12, :], ACT.Tanh).then_inc(lora_in, 1)
        act.activation(Q[0:96, 13, :], Q[0:96, 13, :], ACT.Sigmoid).then_inc(lora_in, 1)
        for c in range(CT):
            for j in range(3):
                m = 3 * c + j
                act.wait_ge(lora_full, m + 1)
                if j == 2:
                    act.activation(gg[:, c, :], banks[m % 6][:, :], ACT.Copy).then_inc(lora_evac, 1)
                else:
                    act.activation((lw, aB)[j][:, c, :], banks[m % 6][:, :], ACT.Sigmoid,
                                   bias=col(("w0", "a0")[j], c)).then_inc(lora_evac, 1)
        for c in range(CT):
            act.wait_ge(kk_raw, c + 1)
            if c >= 2:
                act.wait_ge(kk_sum, c - 1)
            act.activation(sqk[:, c % 2, :], kk[:, c, :], ACT.Square).then_inc(kk_sq, 1)
        act.wait_ge(chunk_end, 1)
        act.activation(der[:, ECT:ECT + 32], der[:, CT_END:CT_END + 32], ACT.Exp).then_inc(exps_done, 1)
        act.wait_ge(exps_in, 1)
        act.activation(e1[:, :, :], cc[:, :, :], ACT.Exp, scale=-1.0).then_inc(exps_done, 1)
        act.activation(eR[:, :, :], cc[:, :, :], ACT.Exp).then_inc(exps_done, 1)
        act.wait_ge(exps_in, 2)
        act.activation(eA[:, :, :], eA[:, :, :], ACT.Exp).then_inc(exps_done, 1)
        for c in range(CT):
            act.wait_ge(kk_max, c + 1)
            act.activation(knt[:, c % 2, :], knt[:, c % 2, :], ACT.Sqrt).then_inc(kk_root, 1)
        for n in range(16):
            act.wait_ge(tok_full, n + 1)
            act.activation((A_tok, B_tok, K_tok, V_tok)[n // 4][:, n % 4, :], banks[n % 4][:, :], ACT.Copy).then_inc(tok_done, 1)
        ident4 = ident.unsqueeze(1).broadcast_to([P, 4, P])

        def unit(c, e, step):
            X = banks[4 * e:4 * e + 4]
            rows, h = slice(64 * e, 64 * e + 64), 2 * c + e
            if step in ("DI", "DIT"):
                if c:
                    act.wait_ge(u_pe[e], pe_at(c - 1, "U"))
                else:
                    act.wait_ge(ada_done, 1)
                act.activation((Di if step == "DI" else DiT)[e][:, :, :], ident4, ACT.Copy).then_inc(u_act[e], 1)
                return
            act.wait_ge(u_pe[e], pe_at(c, step))
            if step == "LT":
                out, src = Lt[e][:, :, :], X[1][:, :]
            elif step == "MV":
                out, src = MV[e][:, :, :], X[3][:, 0:256]
            elif step == "Y0":
                out, src = ky[rows, c, :], X[3][rows, :]
            elif step[0] == "G":
                out, src = Gt[e][:, :, :], X[0][:, :]
            elif step == "W":
                out, src = eA[rows, c, :], X[0][rows, :]
            else:
                out, src = U[:, :, 64 * h:64 * h + 64], X[1][:, 0:256]
            if len(out.shape) == 3:
                src = src.rearrange("p (a b) -> p a b", a=4)
            act.activation(out, src, ACT.Copy).then_inc(u_act[e], 1)

        for c in range(CT):
            for step in ACT_STEPS:
                for e in range(2):
                    unit(c, e, step)
        for c in range(CT):
            act.wait_ge(cln_centred, c + 1)
            act.activation(csq[:, c, :], cacc[:, c, :], ACT.Square).then_inc(cln_sq, 1)
        act.wait_ge(cln_sum, 1 + CT)
        act.activation(cstd[:, :], banks[5][:, :], ACT.Sqrt, scale=1.0 / HALF, bias=der[:, 126:127]).then_inc(cln_root, 1)
        for c in range(CT):
            act.wait_ge(cln_normed, c + 1)
            act.activation(cacc[:, c, :], cacc[:, c, :], ACT.Silu, scale=col("cln_g", c), bias=col("cln_b", c)).then_inc(conv_out, 1)
        for c in range(CT):
            act.wait_ge(gn_centred, c + 1)
            if c >= 2:
                act.wait_ge(gn_var, c - 1)
            act.activation(msq[:, c % 2, :], ky[:, c, :], ACT.Square).then_inc(gn_sq, 1)

        def high(k, src, done):
            act.activation(h1_hi[:, k, :], src, ACT.Copy).then_inc(done, 1)

        for c in range(CT):
            act.wait_ge(gn_var, c + 1)
            act.activation(mrs[:, c % 2, :], banks[4 + c][:, :], ACT.Sqrt, scale=1.0 / 64, bias=der[:, 125:126]).then_inc(gn_root, 1)
            if c == 0:
                act.wait_ge(y_done, NCH)
                act.dma_start(xT[:, :, :], x_t).then_inc(x_again, 16)
            high(CT + c, cacc[:, c, :], mix_hi_full)
            act.wait_ge(gn_normed, c + 1)
            act.activation(ky[:, c, :], ky[:, c, :], ACT.Identity, scale=col("lnx_g", c), bias=col("lnx_b", c)).then_inc(gn_scaled, 1)
        for c in range(CT):
            act.wait_ge(mix_full, c + 1)
            high(c, ky[:, c, :], mix_hi_full)

        def copy_and_square(m, bank, out, wait, free):
            wait()
            act.activation(out, banks[bank][:, :], ACT.Copy).then_inc(out_copied, 1)
            if m >= 2:
                act.wait_ge(out_summed, m - 1)
            act.activation(nt[:, m % 2, :], banks[bank][:, :], ACT.Square).then_inc(out_sq, 1)
            act.wait_ge(out_sq, m + 1)
            act.sem_inc(free, 1)

        for m in range(KT):
            n = STREAM["out"] + m // 2
            b = 2 * half_of(n) + m % 2
            copy_and_square(m, b, mixo[:, m, :], lambda: act.wait_ge(tile0_full if m % 2 == 0 else block_done, n + 1), proj_free[b])

        act.wait_ge(post_sum, 1)
        act.activation(nr[:, :], banks[6][:, :], ACT.Sqrt, scale=1.0 / D, bias=der[:, 127:128]).then_inc(post_root, 1)
        for k in range(KT):
            act.wait_ge(x_done, k + 1)
            if k >= 2:
                act.wait_ge(pre_sq_read, k - 1)
            act.activation(nt[:, k % 2, :], xT[:, k, :], ACT.Square).then_inc(pre_sq, 1)
        act.wait_ge(pre_sq_read, KT)
        act.activation(nr[:, :], banks[7][:, :], ACT.Sqrt, scale=1.0 / D, bias=der[:, 127:128]).then_inc(pre_root, 1)
        for k in range(KT):
            act.wait_ge(nh_full, k + 1)
            act.activation(h1_hi[:, k, :], nh[:, k % 2, :], ACT.Copy).then_inc(nh_hi, 1)

        for _ in range(4):
            act.sem_inc(down_free, 1)
        with act.Fori(0, N_UP // 2) as i:
            for u in range(2):
                n0 = STREAM["up"] + u
                s = half_of(n0)
                j = 2 * i + u
                for g, buf in enumerate((yg, yu)):
                    act.wait_ge(tile0_full if g == 0 else block_done, 2 * i + (n0 + 1))
                    act.activation(buf[:, s, :], banks[2 * s + g][:, :], ACT.Identity,
                                   scale=prm[:, bass.ds(6 * j + (PCOL["fconv_w"] + 3 * g + 2), 1)],
                                   bias=prm[:, bass.ds(2 * j + (PCOL["fconv_b"] + g), 1)]).then_inc(up_first, 1)
                act.wait_ge(up_conv, 4 * i + (2 * u + 1))
                act.activation(yg[:, s, :], yg[:, s, :], ACT.Gelu_apprx_tanh).then_inc(up_gelu, 1)
                act.wait_ge(up_prod, j + 1)
                act.activation(act_hi[:, j, :], yg[:, s, :], ACT.Copy).then_inc(up_hi, 1)

        for q in range(4):
            for j in range(2):
                m = KT + 2 * q + j
                n = STREAM["down"] + 3 * q + 3
                copy_and_square(m, 4 + (2 * q + j) % 4, fout[:, 2 * q + j, :],
                                lambda: act.wait_ge(down_full, q + 1) if j == 0 else act.wait_ge(block_done, n), down_free)
        act.wait_ge(post_sum, 2)
        act.activation(nr[:, :], banks[6][:, :], ACT.Sqrt, scale=1.0 / D, bias=der[:, 127:128]).then_inc(post_root, 1)
        act.wait_ge(block_done, STREAM["mla_in"])
        act.dma_start(ctxT[:, :, :], ctx_t).then_inc(s_ctx, 16)
        act.wait_ge(x_done, KT + 1)
        act.dma_start(rope[:, :, :], ropes[0, :, :, :]).then_inc(s_rope, 16)
        for k in range(KT):
            act.wait_ge(mh_full, k + 1)
            act.activation(h2_hi[:, k, :], mh[:, k % 2, :], ACT.Copy).then_inc(mh_hi, 1)
        T0 = STREAM["down"] + 1
        freed = [0, 0]
        for m in range(12):
            w = m % 2
            act.wait_ge(*((tile0_full, T0 + m // 2) if w == 0 else (block_done, STREAM["mla_in"] + m // 2 + 1)))
            if m < 3:
                act.activation(lat[:, m, :], wide(w), ACT.Copy)
                if m == 2:
                    act.wait_ge(lat_sum, 1)
                act.activation(lsq[:, m % 2, :], wide(w), ACT.Square).then_inc(lat_sq, 1)
                act.wait_ge(lat_sq, m + 1)
                act.sem_inc(wide_free[w], 1)
                if m == 2:
                    act.activation(lrs[:, :], wide(2), ACT.Sqrt, scale=1.0 / 256, bias=der[:, 127:128]).then_inc(lat_root, 1)
            elif m == 3:
                act.activation(kT[0][64:96, :], wide(w)[64:96, :], ACT.Copy).then_inc(kpe_copied, 1)
                act.wait_ge(kpe_copied, 1)
                act.sem_inc(wide_free[w], 1)
            else:
                act.activation(gate_s[:, m - 4, :], wide(w), ACT.Silu).then_inc(wide_free[w], 1)
            if m == 5:
                act.wait_ge(lat_normed, 2)
                act.wait_ge(lat_sum, 2)
                act.activation(lrs[:, :], wide(2), ACT.Sqrt, scale=1.0 / 128, bias=der[:, 127:128]).then_inc(lat_root, 1)
            if m == 8:
                for c in range(2):
                    act.activation(lat_hi[:, c, :], lat[:, c, :], ACT.Copy).then_inc(lat_high, 1)
            if m == 11:
                act.wait_ge(lat_normed, 3)
                act.activation(lat_hi[:, 2, :], lat[:, 2, :], ACT.Copy).then_inc(lat_high, 1)

        with act.Fori(0, A_HEADS // 2) as p:
            act.wait_ge(wide_full, 17 * p + 1)
            act.activation(qT[0][0:96, :], wide(0)[0:96, :], ACT.Copy).then_inc(pr_evac, 1)
            act.wait_ge(pr_evac, 4 * p + 1)
            act.sem_inc(wide_free[0], 1)
            act.wait_ge(wide_full, 17 * p + 2)
            act.activation(kT[0][0:64, :], wide(1)[0:64, :], ACT.Copy)
            act.activation(kT[1][0:64, :], wide(1)[64:128, :], ACT.Copy).then_inc(pr_evac, 1)
            act.wait_ge(pr_evac, 4 * p + 2)
            act.sem_inc(wide_free[1], 1)
            act.wait_ge(wide_full, 17 * p + 3)
            act.activation(qT[1][0:96, :], wide(0)[0:96, :], ACT.Copy).then_inc(pr_evac, 1)
            act.wait_ge(pr_evac, 4 * p + 3)
            act.sem_inc(wide_free[0], 1)
            act.wait_ge(block_done, p + (STREAM["mla"] + 1))
            act.activation(Vt[:, :, :].rearrange("p a b -> p (a b)"), wide(1), ACT.Copy).then_inc(pr_evac, 1)
            act.wait_ge(pr_evac, 4 * p + 4)
            act.sem_inc(wide_free[1], 1)
            for v in range(12):
                hh, qt = v // 6, v % 6
                act.wait_ge(nm_ready, 12 * p + (v + 1))
                if v >= 2 and (v - 2) % 6 >= 4:
                    act.wait_ge(ta_full, 12 * p + (v - 1))
                keys = TA if qt < 4 else C
                w = (5 + v) % 2
                act.activation(Pm[v % 2][:, 0:keys], wide(w, keys), ACT.Exp, scale=A_SCALE, bias=der[:, NM + v:NM + v + 1],
                               accum_out=der[:, RS + v:RS + v + 1]).then_inc(p_full, 1)
                act.wait_ge(p_full, 12 * p + (v + 1))
                act.sem_inc(wide_free[w], 1)
                if qt < 4:
                    act.wait_ge(tb_full, 8 * p + (4 * hh + qt + 1))
                    if v:
                        act.wait_ge(pv_done, 12 * p + v)
                    act.activation(PT[:, 3:6, :].rearrange("p a b -> p (a b)"), banks[5][:, 0:3 * P], ACT.Copy).then_inc(evb_done, 1)
            act.wait_ge(ot_done, p + 1)
            act.activation(h2_hi[:, p, :], otmp[:, :], ACT.Copy).then_inc(ot_hi, 1)

        def norm_out(layer, name, n_cols, t0):
            xg = ada[:, layer, 2, :, :]
            for m in range(KT):
                w = m % 2
                act.wait_ge(*((tile0_full, t0 + m // 2) if w == 0 else (block_done, STREAM[name] + m // 2 + 1)))
                ins = act.activation(z_of(layer)[:, m, 0:T], wide(w, T), ACT.Copy, scale=xg[:, m, 0:1])
                if n_cols > T:
                    ins = act.activation(z_of(layer)[:, m, T:TA], wide(w)[:, T:TA], ACT.Copy, scale=xg[:, m, 1:2])
                ins.then_inc(z_gated, 1)
                act.wait_ge(z_gated, KT * layer + m + 1)
                act.sem_inc(wide_free[w], 1)
            for k in range(KT):
                act.wait_ge(z_centred, KT * layer + k + 1)
                if k >= 2:
                    act.wait_ge(z_sum, 9 * layer + k)
                act.activation(zsq[:, k % 2, 0:n_cols], z_of(layer)[:, k, 0:n_cols], ACT.Square).then_inc(z_sq, 1)
            act.wait_ge(z_sum, 9 * layer + 9)
            act.activation(zrs[:, 0:n_cols], wide(3, n_cols), ACT.Sqrt, scale=1.0 / D, bias=der[:, 127:128]).then_inc(z_root, 1)
            for k in range(KT):
                act.wait_ge(z_normed, KT * layer + k + 1)
                act.activation(z_of(layer)[:, k, 0:n_cols], z_of(layer)[:, k, 0:n_cols], ACT.Identity, scale=col("ln_g", KT * layer + k),
                               bias=col("ln_b", KT * layer + k)).then_inc(z_out, 1)

        act.wait_ge(ot_ready, A_HEADS // 2)
        act.dma_start(ctx2[:, :, :], ctx_t).then_inc(s_ctx, 16)
        norm_out(0, "mla_out", TA, T0 + N_MLA_IN)
        act.dma_start(rope[:, :, :], ropes[1, :, :, :]).then_inc(s_rope, 16)
        for k in range(KT):
            act.wait_ge(mh_full, KT + k + 1)
            act.activation(h2_hi[:, k, :], zh[:, k % 2, :], ACT.Copy).then_inc(mh_hi, 1)
        act.wait_ge(lam_sum, 1)
        act.activation(der[:, LAM + 2:LAM + 4], banks[4][:, 0:2], ACT.Exp).then_inc(lam_exp, 1)

        with act.Fori(0, B_HEADS) as h:
            def evacuate(i, w, dst, src):
                act.activation(dst, src, ACT.Copy).then_inc(pr_evac, 1)
                act.wait_ge(pr_evac, D_EVAC * h + (N_MLA_EVAC + i + 1))
                act.sem_inc(wide_free[w], 1)

            act.wait_ge(wide_full, D_FULL * h + (N_MLA_FULL + 1))
            evacuate(0, 0, dq[:, :], wide(0, T))
            act.wait_ge(block_done, 2 * h + (STREAM["diff"] + 1))
            evacuate(1, 1, dk[:, :], wide(1))
            act.wait_ge(wide_full, D_FULL * h + (N_MLA_FULL + 2))
            evacuate(2, 0, dv[:, :], wide(0))
            act.wait_ge(block_done, 2 * h + (STREAM["diff"] + 2))
            evacuate(3, 1, gate2[:, h, :], wide(1, T))
            act.wait_ge(wide_full, D_FULL * h + (N_MLA_FULL + 4))
            evacuate(4, 1, dV[:, :, :].rearrange("p a b -> p (a b)"), wide(1))

            def square(v):
                act.wait_ge(o_done, D_UNITS * h + (N_MLA_UNITS + v + 1))
                act.activation(o_junk[:, (v // 2) % 2, :], O_tok[:, v // 2, bass.ds(P * h, P)], ACT.Square,
                               accum_out=o_ss[:, bass.ds(4 * h + v // 2, 1)]).then_inc(o_sq, 1)

            for v in range(8):
                act.wait_ge(nm_ready, D_UNITS * h + (N_MLA_UNITS + v + 1))
                act.activation(dP[v % 2][:, :], wide(v % 2), ACT.Exp, scale=B_SCALE, bias=der[:, NM + v:NM + v + 1],
                               accum_out=der[:, RS + v:RS + v + 1]).then_inc(p_full, 1)
                act.wait_ge(p_full, D_UNITS * h + (N_MLA_UNITS + v + 1))
                act.sem_inc(wide_free[v % 2], 1)
                act.wait_ge(tb_full, D_UNITS * h + (N_MLA_XUNITS + v + 1))
                if v:
                    act.wait_ge(pv_done, D_UNITS * h + (N_MLA_UNITS + v))
                act.activation(dPT[:, 3:6, :].rearrange("p a b -> p (a b)"), banks[5][:, 0:3 * P], ACT.Copy).then_inc(evb_done, 1)
                if v % 2 and v > 1:
                    square(v - 2)
            square(7)

        act.wait_ge(o_sq, 4 * B_HEADS)
        act.activation(o_rs[:, :], o_ss[:, :], ACT.Sqrt, scale=1.0 / P, bias=der[:, 127:128]).then_inc(o_root, 1)
        for m in range(KT):
            act.activation(gate2[:, m, :], gate2[:, m, :], ACT.Silu).then_inc(gate_done, 1)
        for h in range(B_HEADS):
            act.wait_ge(og_full, h + 1)
            act.activation(h2_hi[:, h, 0:T], og[:, h % 2, :], ACT.Copy).then_inc(og_hi, 1)
        norm_out(1, "diff_out", T, T0 + N_MLA_IN + N_MLA_OUT)

    @block.vector
    def _(dve):
        chain = Chain(dve, dve_step)
        for b in range(4):
            dve.sem_inc(proj_free[b], 1)
        dve.sem_inc(glu_s_free, 2)
        dve.memset(der[:, 127:128], RMS_EPS)
        dve.memset(der[:, 126:127], LN_EPS)
        dve.memset(der[:, 125:126], GN_EPS).then_inc(prep_done, 1)
        dve.wait_ge(s_const, 96)
        chain.link(dve.tensor_copy(lvl[:, :, :], lvl_f[:, :, :]))
        dve.tensor_scalar(der[:, OMU:OMU + 14], col("mu", 0, 14), -1.0, 1.0, ALU.mult, ALU.add)
        chain.link(dve.tensor_scalar(der[:, OKA:OKA + 4], col("k_a", 0, 4), -1.0, 1.0, ALU.mult, ALU.add))
        dve.sem_inc(prep_done, 1)
        dve.wait_ge(sqrt_done, 1)
        chain.link(dve.reciprocal(rstd[:, :], rstd[:, :]))
        for k in range(KT):
            if k >= 2:
                dve.wait_ge(h_hi_full, k - 1)
            dve.scalar_tensor_tensor(out=htmp[:, k % 2, :], in0=xT[:, k, :], scalar=col("pre_mix", k), in1=rstd[:, :],
                                     op0=ALU.mult, op1=ALU.mult).then_inc(htmp_full, 1)
            if k:
                dve.wait_ge(h_hi_full, k)
                dve.tensor_tensor(h1_lo[:, k - 1, :], htmp[:, (k - 1) % 2, :], h1_hi[:, k - 1, :], ALU.subtract).then_inc(h_ready, 1)
                dve.wait_ge(h_ready, k)
        dve.wait_ge(h_hi_full, KT)
        dve.tensor_tensor(h1_lo[:, KT - 1, :], htmp[:, (KT - 1) % 2, :], h1_hi[:, KT - 1, :], ALU.subtract).then_inc(h_ready, 1)
        dve.wait_ge(zeros_done, 1)
        with chain.loop(2, 2) as i:
            for s in range(2):
                dve.wait_ge(glu_s_full, 2 * i + s + 1)
                chain.link(dve.tensor_tensor(cpad[:, 2 * i + s, TAPS - 1:], banks[2 * s][:, :], glu_s[:, s, :], ALU.mult))
                dve.sem_inc(proj_free[2 * s], 1)
                dve.sem_inc(proj_free[2 * s + 1], 1)
                dve.sem_inc(glu_s_free, 1)

        conv = Chain(dve, conv_done)
        for j in range(CT):
            conv.mark(dve.tensor_scalar(cacc[:, j, :], cpad[:, j, 0:T], col("cconv_w", TAPS * j), col("cconv_b", j),
                                        ALU.mult, ALU.add))

        def tap(t):
            for j in range(CT):
                conv.wait(conv.n - (CT - 1))
                conv.mark(dve.scalar_tensor_tensor(out=cacc[:, j, :], in0=cpad[:, j, bass.ds(t, T)],
                                                   scalar=prm[:, bass.ds(t + (PCOL["cconv_w"] + TAPS * j), 1)],
                                                   in1=cacc[:, j, :], op0=ALU.mult, op1=ALU.add))

        def q_tile(j, b, copied):
            dve.wait_ge(q_copied, copied)
            dve.scalar_tensor_tensor(out=Q[:, j, 1:T], in0=banks[b][:, 0:T - 1], scalar=prm[:, bass.ds(j + PCOL["mu"], 1)],
                                     in1=Q[:, j, 1:T], op0=ALU.mult, op1=ALU.add).then_inc(q_mixed, 1)
            dve.wait_ge(q_mixed, copied)
            dve.sem_inc(proj_free[b], 1)

        with conv.loop(3, 8 * CT) as i:
            for s in range(2):
                for j in range(2):
                    q_tile(4 * i + 2 * s + j, 2 * s + j, 4 * i + (2 * s + j + 1))
                    for u in range(2):
                        tap(8 * i + (4 * s + 2 * j + u + 1))
        for j in range(2):
            q_tile(12 + j, j, 13 + j)
        for t in range(25, TAPS):
            tap(t)
        dve.memset(ada_row[:, :, :], 0.0).then_inc(ada_zero, 1)
        for c in range(CT):
            dve.wait_ge(lora_evac, 3 * c + 1)
            chain.link(dve.tensor_scalar(lw[:, c, :], lw[:, c, :], -math.exp(-0.5), None, ALU.mult))
            chain.mark(dve.tensor_tensor_scan(cc[:, c, :], scan_m[:, :], lw[:, c, :], 0.0, ALU.mult, ALU.add))
            dve.tensor_scalar(kk[:, c, :], ky[:, c, :], col("k_k", c), None, ALU.mult).then_inc(kk_raw, 1)
        chain.wait()
        by_chunk = cc[:, :, :].rearrange("p c (n t) -> p (c n) t", t=CHUNK)
        chain.link(dve.tensor_copy(der[:, CT_END:CT_END + 32], by_chunk[:, :, CHUNK - 1]))
        dve.sem_inc(chunk_end, 1)
        chain.link(dve.tensor_tensor(by_chunk, by_chunk, der[:, CT_END:CT_END + 32].unsqueeze(2).broadcast_to([P, 32, CHUNK]),
                                     ALU.subtract))
        dve.sem_inc(exps_in, 1)
        dve.tensor_tensor(eA[:, :, :], cc[:, :, :], lw[:, :, :], ALU.subtract).then_inc(exps_in, 1)

        def ada_columns(g):
            dve.wait_ge(ada_rows, g + 1)
            chain.link(dve.tensor_copy(ada_row[0:2, :, :], banks[6 + g % 2][0:2, :].rearrange("p (a n) -> p a n", a=2)))
            dve.sem_inc(ada_rows_free, 1)
            dve.sem_inc(ada_free[1], 1)
            row = ada_row[:, :, :].rearrange("p a (t q c) -> p (a t) q c", t=2, q=4)
            for q in range(4):
                last = dve.transpose(ada_col[32 * q:32 * q + 32, :, :], row[:, :, q, :])
            chain.link(last)
            n = slice(8 * g, 8 * g + 8)
            flat = ada[:, :, :, :, :].rearrange("p l s k v -> p (l s k v)")
            chain.link(dve.tensor_tensor(flat[:, n].rearrange("p (t v) -> p t v", v=2), ada_col[:, :, 0:2],
                                         col("ada_b", 8 * g, 8).rearrange("p (t v) -> p t v", v=2), ALU.add))

        dve.wait_ge(ada_zero, 1)
        for c in range(CT):
            dve.wait_ge(kk_sum, c + 1)
            if c >= 2:
                chain.wait()
            dve.tensor_scalar(knt[:, c % 2, :], banks[c][:, :], 1e-24, None, ALU.max).then_inc(kk_max, 1)
            ada_columns(c)
            dve.wait_ge(kk_root, c + 1)
            chain.link(dve.reciprocal(knt[:, c % 2, :], knt[:, c % 2, :]))
            chain.link(dve.tensor_tensor(kk[:, c, :], kk[:, c, :], knt[:, c % 2, :], ALU.mult))
        for c in range(CT):
            chain.link(dve.tensor_scalar(kft[:, c % 2, :], aB[:, c, :], col("k_a", c), der[:, OKA + c:OKA + c + 1], ALU.mult, ALU.add))
            chain.link(dve.tensor_tensor(ky[:, c, :], ky[:, c, :], kft[:, c % 2, :], ALU.mult))
        dve.wait_ge(exps_done, 3)
        chain.link(dve.tensor_tensor(eR[:, :, :], eR[:, :, :], rr, ALU.mult))
        for c in range(CT):
            dve.scalar_tensor_tensor(out=rr[:, c, :], in0=rr[:, c, :], scalar=col("r_k", c), in1=ky[:, c, :],
                                     op0=ALU.mult, op1=ALU.mult).then_inc(bonus_in, 1)
        for g in range(4, 8):
            ada_columns(g)
        dve.wait_ge(exps_done, 4)
        dve.scalar_tensor_tensor(out=eA[:, :, :].rearrange("p c t -> p (c t)"), in0=kk[:, :, :].rearrange("p c t -> p (c t)"), scalar=-1.0,
                                 in1=eA[:, :, :].rearrange("p c t -> p (c t)"), op0=ALU.mult, op1=ALU.mult).then_inc(abkv_ready, 1)
        chain.link(dve.tensor_tensor(aB[:, :, :], aB[:, :, :], kk[:, :, :], ALU.mult))
        dve.tensor_tensor(aB[:, :, :], aB[:, :, :], e1[:, :, :], ALU.mult).then_inc(abkv_ready, 1)
        dve.wait_ge(bonus_in, CT)
        dve.tensor_tensor(ky, ky, e1[:, :, :], ALU.mult).then_inc(abkv_ready, 1)
        for c in range(CT):
            dve.wait_ge(bonus_sum, c + 1)
            dve.tensor_tensor(rr[:, c, :], banks[c][:, :], vv[:, c, :], ALU.mult).then_inc(bonus_done, 1)
        for g in range(8, 12):
            ada_columns(g)
        dve.sem_inc(ada_done, 1)
        def unit(c, e, step):
            X = banks[4 * e:4 * e + 4]

            def bank(i):
                return X[i][:, :].rearrange("p (a b) -> p a b", a=4)

            def masked(out, src, mask):
                dve.tensor_tensor(out[:, :, :], src, mask.unsqueeze(1).broadcast_to([P, 4, P]), ALU.mult).then_inc(u_dve[e], 1)

            def placed(out, src, n):
                dve.copy_predicated(out[:, :, :], lvl[:, n, :].unsqueeze(1).broadcast_to([P, 4, P]), src).then_inc(u_dve[e], 1)

            if step == "MT":
                dve.wait_ge(u_pe[e], pe_at(c, "MT"))
                masked(Mt[e], bank(2), before)
            elif step == "RB":
                dve.wait_ge(u_pe[e], pe_at(c, "RB"))
                masked(RBt[2 * c + e], bank(3), until_m)
            elif step == "RK":
                dve.wait_ge(u_pe[e], pe_at(c, "RK"))
                masked(RKt[e], bank(2), until_m)
            elif step == "D0":
                dve.wait_ge(u_act[e], act_at(c, "LT"))
                placed(Di[e], bank(0), 0)
            elif step == "DT0":
                placed(DiT[e], Lt[e][:, :, :], 6)
            else:
                n = int(step[1])
                dve.wait_ge(u_pe[e], pe_at(c, f"Q{n}"))
                placed(*((Di[e], bank(1), n) if step[0] == "P" else (DiT[e], bank(2), 6 + n)))

        for st in St:
            last = dve.memset(st[:, :, :], 0.0)
        last.then_inc(st_zero, 1)
        for c in range(CT):
            for step in DVE_STEPS:
                for e in range(2):
                    unit(c, e, step)
        for n in range(NCH):
            tt, r = n // 2, slice(64 * (n % 2), 64 * (n % 2) + 64)
            dve.wait_ge(sa_full, n + 1)
            if n:
                dve.wait_ge(y_full, n)
            dve.tensor_tensor(SA[r, :], banks[0][r, :], U[r, tt, :], ALU.add).then_inc(sa_done, 1)
            if n < NCH - 1:
                dve.wait_ge(st_full, n + 1)
                for e in range(2):
                    hr = slice(64 * e, 64 * e + 64)
                    src = banks[1][hr, :].rearrange("p (c v) -> p c v", c=CT)[:, :, hr]
                    decay = der[hr, ECT:ECT + 32].rearrange("p (c n) -> p c n", n=NCH)[:, :, n + 1:n + 2].broadcast_to([64, CT, 64])
                    dve.tensor_tensor(St[(n + 1) % 2][hr, :, hr], src, decay, ALU.mult).then_inc(st_done, 1)
            if n == 1:
                dve.wait_ge(cln_sum, 1)
                for c in range(CT):
                    dve.scalar_tensor_tensor(out=cacc[:, c, :], in0=banks[4][:, :], scalar=-1.0 / HALF, in1=cacc[:, c, :],
                                             op0=ALU.mult, op1=ALU.add).then_inc(cln_centred, 1)
            if n == 5:
                dve.wait_ge(cln_root, 1)
                chain.link(dve.reciprocal(cstd[:, :], cstd[:, :]))
            if n == 6:
                for c in range(CT):
                    dve.tensor_tensor(cacc[:, c, :], cacc[:, c, :], cstd[:, :], ALU.mult).then_inc(cln_normed, 1)
            dve.wait_ge(y_full, n + 1)
            dve.tensor_tensor(ky[:, :, CHUNK * n:CHUNK * n + CHUNK], banks[2 + n % 2][:, 0:CT * CHUNK].rearrange("p (c t) -> p c t", c=CT),
                              ky[:, :, CHUNK * n:CHUNK * n + CHUNK], ALU.add).then_inc(y_done, 1)
        for c in range(CT):
            dve.wait_ge(gn_mean, c + 1)
            dve.scalar_tensor_tensor(out=ky[:, c, :], in0=banks[4 + c][:, :], scalar=-1.0 / 64, in1=ky[:, c, :],
                                     op0=ALU.mult, op1=ALU.add).then_inc(gn_centred, 1)

        def low(k, src, ready):
            dve.tensor_tensor(h1_lo[:, k, :], src, h1_hi[:, k, :], ALU.subtract).then_inc(ready, 1)

        for c in range(CT):
            dve.wait_ge(gn_root, c + 1)
            chain.link(dve.reciprocal(mrs[:, c % 2, :], mrs[:, c % 2, :]))
            dve.tensor_tensor(ky[:, c, :], ky[:, c, :], mrs[:, c % 2, :], ALU.mult).then_inc(gn_normed, 1)
            dve.wait_ge(mix_hi_full, c + 1)
            low(CT + c, cacc[:, c, :], mix_ready)
            dve.wait_ge(gn_scaled, c + 1)
            chain.link(dve.tensor_tensor(ky[:, c, :], ky[:, c, :], rr[:, c, :], ALU.add))
            dve.tensor_tensor(ky[:, c, :], ky[:, c, :], gg[:, c, :], ALU.mult).then_inc(mix_full, 1)
        for c in range(CT):
            dve.wait_ge(mix_hi_full, CT + c + 1)
            low(c, ky[:, c, :], mix_ready)

        def sum_squares(m0):
            for m in range(m0, m0 + KT):
                dve.wait_ge(out_sq, m + 1)
                if m > m0:
                    dve.wait_ge(out_summed, m)
                    dve.tensor_tensor(nacc[:, :], nacc[:, :], nt[:, m % 2, :], ALU.add).then_inc(out_summed, 1)
                else:
                    dve.tensor_copy(nacc[:, :], nt[:, m % 2, :]).then_inc(out_summed, 1)

        def add_normed(which, src, weight):
            dve.wait_ge(post_root, which + 1)
            chain.link(dve.reciprocal(nr[:, :], nr[:, :]))
            for k in range(KT):
                chain.mark(dve.scalar_tensor_tensor(out=src[:, k, :], in0=src[:, k, :], scalar=col(weight, k), in1=nr[:, :],
                                                    op0=ALU.mult, op1=ALU.mult))
                if k:
                    chain.wait(chain.n - 1)
                    dve.tensor_tensor(xT[:, k - 1, :], xT[:, k - 1, :], src[:, k - 1, :], ALU.add).then_inc(x_done, 1)
            chain.wait()
            dve.tensor_tensor(xT[:, KT - 1, :], xT[:, KT - 1, :], src[:, KT - 1, :], ALU.add).then_inc(x_done, 1)

        sum_squares(0)
        dve.wait_ge(x_again, 16)
        add_normed(0, mixo, "post_mix")
        dve.wait_ge(pre_root, 1)
        chain.link(dve.reciprocal(nr[:, :], nr[:, :]))
        for k in range(KT):
            if k >= 2:
                dve.wait_ge(nh_ready, k - 1)
            dve.scalar_tensor_tensor(out=nh[:, k % 2, :], in0=xT[:, k, :], scalar=col("pre_ffn", k), in1=nr[:, :],
                                     op0=ALU.mult, op1=ALU.mult).then_inc(nh_full, 1)
            if k:
                dve.wait_ge(nh_hi, k)
                low(k - 1, nh[:, (k - 1) % 2, :], nh_ready)
        dve.wait_ge(nh_hi, KT)
        low(KT - 1, nh[:, (KT - 1) % 2, :], nh_ready)

        conv = Chain(dve, conv2)
        with conv.loop(N_UP // 2, 4) as i:
            for u in range(2):
                s = half_of(STREAM["up"] + u)
                j = 2 * i + u
                for g, buf in enumerate((yg, yu)):
                    b = banks[2 * s + g]
                    dve.wait_ge(up_first, 4 * i + (2 * u + g + 1))
                    for tap in (1, 0):
                        ins = dve.scalar_tensor_tensor(out=buf[:, s, 2 - tap:], in0=b[:, 0:T - 2 + tap],
                                                       scalar=prm[:, bass.ds(6 * j + (PCOL["fconv_w"] + 3 * g + tap), 1)],
                                                       in1=buf[:, s, 2 - tap:], op0=ALU.mult, op1=ALU.add)
                        if tap:
                            conv.link(ins)
                    ins.then_inc(up_conv, 1)
                    dve.wait_ge(up_conv, 4 * i + (2 * u + g + 1))
                    dve.sem_inc(proj_free[2 * s + g], 1)
                dve.wait_ge(up_gelu, j + 1)
                dve.tensor_tensor(yg[:, s, :], yg[:, s, :], yu[:, s, :], ALU.mult).then_inc(up_prod, 1)
                dve.wait_ge(up_hi, j + 1)
                dve.tensor_tensor(act_lo[:, j, :], yg[:, s, :], act_hi[:, j, :], ALU.subtract).then_inc(act_ready, 1)
        sum_squares(KT)
        add_normed(1, fout, "post_ffn")
        for l in range(2):
            ins = dve.tensor_scalar(ada[:, l, 1, :, :], ada[:, l, 1, :, :], 1.0, None, ALU.add)
        ins.then_inc(ada_one, 1)
        dve.wait_ge(ada_one, 1)
        dve.wait_ge(s_ctx, 16)
        dve.wait_ge(x_done, 2 * KT)
        for k in range(KT):
            if k >= 2:
                dve.wait_ge(mh_ready, k - 1)
            dve.tensor_scalar(mh[:, k % 2, 0:T], xT[:, k, :], ada[:, 0, 1, k, 0:1], ada[:, 0, 0, k, 0:1], ALU.mult, ALU.add)
            dve.tensor_scalar(mh[:, k % 2, T:TA], ctxT[:, k, :], ada[:, 0, 1, k, 1:2], ada[:, 0, 0, k, 1:2],
                              ALU.mult, ALU.add).then_inc(mh_full, 1)
            if k:
                dve.wait_ge(mh_hi, k)
                dve.tensor_tensor(h2_lo[:, k - 1, :], mh[:, (k - 1) % 2, :], h2_hi[:, k - 1, :], ALU.subtract).then_inc(mh_ready, 1)
        dve.wait_ge(mh_hi, KT)
        dve.tensor_tensor(h2_lo[:, KT - 1, :], mh[:, 1, :], h2_hi[:, KT - 1, :], ALU.subtract).then_inc(mh_ready, 1)
        dve.wait_ge(lat_root, 1)
        chain.link(dve.reciprocal(lrs[:, :], lrs[:, :]))
        for c in range(2):
            dve.scalar_tensor_tensor(out=lat[:, c, :], in0=lat[:, c, :], scalar=col("g_qa", c), in1=lrs[:, :],
                                     op0=ALU.mult, op1=ALU.mult).then_inc(lat_normed, 1)
        dve.wait_ge(s_rope, 16)
        dve.wait_ge(kpe_rot, 1)
        pe_rows = slice(64, 96)
        dve.tensor_tensor(otmp[pe_rows, 0:T], banks[6][pe_rows, :], rope[pe_rows, 1, :], ALU.mult)
        chain.link(dve.tensor_tensor(kT[0][pe_rows, 0:T], kT[0][pe_rows, 0:T], rope[pe_rows, 0, :], ALU.mult))
        chain.link(dve.tensor_tensor(kT[0][pe_rows, 0:T], kT[0][pe_rows, 0:T], otmp[pe_rows, 0:T], ALU.add))
        dve.tensor_copy(kT[1][pe_rows, :], kT[0][pe_rows, :]).then_inc(kpe_done, 1)
        dve.wait_ge(lat_root, 2)
        chain.link(dve.reciprocal(lrs[:, :], lrs[:, :]))
        dve.scalar_tensor_tensor(out=lat[:, 2, :], in0=lat[:, 2, :], scalar=col("g_kva"), in1=lrs[:, :],
                                 op0=ALU.mult, op1=ALU.mult).then_inc(lat_normed, 1)
        for c in range(3):
            dve.wait_ge(lat_high, c + 1)
            dve.tensor_tensor(lat_lo[:, c, :], lat[:, c, :], lat_hi[:, c, :], ALU.subtract).then_inc(lat_ready, 1)

        with chain.loop(A_HEADS // 2, 1 + 3 + 12 + 12) as p:
            dve.wait_ge(wide_full, 17 * p + 4)
            dve.tensor_tensor(otmp[pe_rows, 0:T], pairs[0][pe_rows, 0, :], rope[pe_rows, 1, :], ALU.mult)
            chain.link(dve.tensor_tensor(qT[0][pe_rows, 0:T], qT[0][pe_rows, 0:T], rope[pe_rows, 0, :], ALU.mult))
            dve.tensor_tensor(qT[0][pe_rows, 0:T], qT[0][pe_rows, 0:T], otmp[pe_rows, 0:T], ALU.add).then_inc(rope_done, 1)
            dve.wait_ge(rope_done, 2 * p + 1)
            chain.link(dve.tensor_tensor(otmp[pe_rows, 0:T], pairs[0][pe_rows, 1, :], rope[pe_rows, 1, :], ALU.mult))
            dve.sem_inc(wide_free[0], 1)
            chain.link(dve.tensor_tensor(qT[1][pe_rows, 0:T], qT[1][pe_rows, 0:T], rope[pe_rows, 0, :], ALU.mult))
            dve.tensor_tensor(qT[1][pe_rows, 0:T], qT[1][pe_rows, 0:T], otmp[pe_rows, 0:T], ALU.add).then_inc(rope_done, 1)

            def top(v):
                keys = TA if v % 6 < 4 else C
                dve.wait_ge(wide_full, 17 * p + (5 + v))
                chain.link(dve.reduce_max(der[:, MX + v:MX + v + 1], wide((5 + v) % 2, keys), AX.X))
                dve.tensor_scalar(der[:, NM + v:NM + v + 1], der[:, MX + v:MX + v + 1], -A_SCALE, None, ALU.mult).then_inc(nm_ready, 1)

            def out(v):
                hh, qt = v // 6, v % 6
                chain.link(dve.reciprocal(der[:, RL + v:RL + v + 1], der[:, RS + v:RS + v + 1]))
                dve.wait_ge(pv_done, 12 * p + (v + 1))
                dve.tensor_scalar(Ob[:, qt, 64 * hh:64 * hh + 64], banks[6 + v % 2][:, 64 * hh:64 * hh + 64],
                                  der[:, RL + v:RL + v + 1], None, ALU.mult).then_inc(o_done, 1)

            top(0)
            for v in range(12):
                if v + 1 < 12:
                    top(v + 1)
                if v:
                    out(v - 1)
                dve.wait_ge(ta_full, 12 * p + (v + 1))
                if v:
                    dve.wait_ge(pv_done, 12 * p + v)
                n = 3 if v % 6 < 4 else 2
                dve.tensor_copy(PT[:, 0:n, :].rearrange("p a b -> p (a b)"), banks[4][:, 0:n * P]).then_inc(eva_done, 1)
            out(11)
            dve.wait_ge(wide_full, 17 * p + 17)
            dve.tensor_tensor(otmp[:, :], wide(1), gate_s[:, p, :], ALU.mult).then_inc(ot_done, 1)
            dve.wait_ge(ot_done, p + 1)
            dve.sem_inc(wide_free[1], 1)
            dve.wait_ge(ot_hi, p + 1)
            chain.link(dve.tensor_tensor(h2_lo[:, p, :], otmp[:, :], h2_hi[:, p, :], ALU.subtract))
            dve.sem_inc(ot_ready, 1)

        def layer_sum(layer, n_cols, x_src, c_src):
            zz = z_of(layer)
            for m in range(KT):
                dve.wait_ge(z_gated, KT * layer + m + 1)
                ins = dve.scalar_tensor_tensor(out=zz[:, m, 0:T], in0=x_src(m), scalar=ALPHA, in1=zz[:, m, 0:T], op0=ALU.mult, op1=ALU.add)
                if n_cols > T:
                    ins = dve.scalar_tensor_tensor(out=zz[:, m, T:TA], in0=c_src(m), scalar=ALPHA, in1=zz[:, m, T:TA], op0=ALU.mult, op1=ALU.add)
                chain.link(ins)
                if m:
                    dve.wait_ge(z_acc, KT * layer + m)
                    dve.tensor_tensor(zacc[:, 0:n_cols], zacc[:, 0:n_cols], zz[:, m, 0:n_cols], ALU.add).then_inc(z_acc, 1)
                else:
                    dve.tensor_copy(zacc[:, 0:n_cols], zz[:, m, 0:n_cols]).then_inc(z_acc, 1)
            dve.wait_ge(z_sum, 9 * layer + 1)
            for k in range(KT):
                dve.scalar_tensor_tensor(out=zz[:, k, 0:n_cols], in0=wide(2, n_cols), scalar=-1.0 / D, in1=zz[:, k, 0:n_cols],
                                         op0=ALU.mult, op1=ALU.add).then_inc(z_centred, 1)
            dve.wait_ge(z_root, layer + 1)
            chain.link(dve.reciprocal(zrs[:, 0:n_cols], zrs[:, 0:n_cols]))
            for k in range(KT):
                dve.tensor_tensor(zz[:, k, 0:n_cols], zz[:, k, 0:n_cols], zrs[:, 0:n_cols], ALU.mult).then_inc(z_normed, 1)

        dve.wait_ge(s_ctx, 32)
        layer_sum(0, TA, lambda m: xT[:, m, :], lambda m: ctx2[:, m, :])
        dve.tensor_tensor(der[0:64, LAM:LAM + 1], col("lam", 0)[0:64, :], col("lam", 1)[0:64, :], ALU.mult)
        dve.tensor_tensor(der[0:64, LAM + 1:LAM + 2], col("lam", 2)[0:64, :], col("lam", 3)[0:64, :], ALU.mult).then_inc(lam_prod, 1)
        for k in range(KT):
            dve.wait_ge(z_out, k + 1)
            if k >= 2:
                dve.wait_ge(mh_ready, KT + k - 1)
            for v, cols in ((0, slice(0, T)), (1, slice(T, TA))):
                ins = dve.tensor_scalar(zh[:, k % 2, cols], z[:, k, cols], ada[:, 1, 1, k, v:v + 1], ada[:, 1, 0, k, v:v + 1],
                                        ALU.mult, ALU.add)
            ins.then_inc(mh_full, 1)
            if k:
                dve.wait_ge(mh_hi, KT + k)
                dve.tensor_tensor(h2_lo[:, k - 1, :], zh[:, (k - 1) % 2, :], h2_hi[:, k - 1, :], ALU.subtract).then_inc(mh_ready, 1)
        dve.wait_ge(mh_hi, 2 * KT)
        dve.tensor_tensor(h2_lo[:, KT - 1, :], zh[:, 1, :], h2_hi[:, KT - 1, :], ALU.subtract).then_inc(mh_ready, 1)
        dve.wait_ge(lam_exp, 1)
        chain.link(dve.tensor_scalar(der[:, LAM + 4:LAM + 5], der[:, LAM + 3:LAM + 4], der[:, LAM + 2:LAM + 3], None, ALU.subtract))
        dve.tensor_scalar(der[:, LAM + 5:LAM + 6], der[:, LAM + 4:LAM + 5], -LAMBDA_INIT, None, ALU.add)
        chain.link(dve.tensor_scalar(der[:, LAM + 6:LAM + 7], col("g_sub"), 1.0 - LAMBDA_INIT, None, ALU.mult))
        dve.wait_ge(s_rope, 32)

        with chain.loop(B_HEADS, 2 + 8 + 8 + 4) as h:
            dve.wait_ge(wide_full, D_FULL * h + (N_MLA_FULL + 3))
            dve.wait_ge(pr_evac, D_EVAC * h + (N_MLA_EVAC + 2))
            dve.tensor_tensor(dt[:, :], pairs[0][:, 0, :], rope[:, 1, :], ALU.mult)
            chain.link(dve.tensor_tensor(dq[:, :], dq[:, :], rope[:, 0, :], ALU.mult))
            dve.tensor_tensor(dq[:, :], dq[:, :], dt[:, :], ALU.add).then_inc(rope_k, 1)
            dve.wait_ge(rope_k, h + 1)
            dve.tensor_tensor(dt[:, :], pairs[0][:, 1, :], rope[:, 1, :], ALU.mult)
            chain.link(dve.tensor_tensor(dk[:, 0:T], dk[:, 0:T], rope[:, 0, :], ALU.mult))
            dve.sem_inc(wide_free[0], 1)
            dve.tensor_tensor(dk[:, 0:T], dk[:, 0:T], dt[:, :], ALU.add).then_inc(rope_done, 1)

            def top(v):
                dve.wait_ge(wide_full, D_FULL * h + (N_MLA_FULL + 5 + v))
                chain.link(dve.reduce_max(der[:, MX + v:MX + v + 1], wide(v % 2), AX.X))
                dve.tensor_scalar(der[:, NM + v:NM + v + 1], der[:, MX + v:MX + v + 1], -B_SCALE, None, ALU.mult).then_inc(nm_ready, 1)

            def out(v):
                chain.link(dve.reciprocal(der[:, RL + v:RL + v + 1], der[:, RS + v:RS + v + 1]))
                if v % 2:
                    chain.link(dve.tensor_tensor(der[:, NL + v:NL + v + 1], der[:, RL + v:RL + v + 1], der[:, LAM + 5:LAM + 6], ALU.mult))
                    dve.wait_ge(o_done, D_UNITS * h + (N_MLA_UNITS + v))
                dve.wait_ge(pv_done, D_UNITS * h + (N_MLA_UNITS + v + 1))
                src = banks[6 + v % 2][:, 0:P]
                if v % 2:
                    ins = dve.scalar_tensor_tensor(out=O_tok[:, v // 2, bass.ds(P * h, P)], in0=src, scalar=der[:, NL + v:NL + v + 1],
                                                   in1=o_first[:, :], op0=ALU.mult, op1=ALU.add)
                else:
                    ins = dve.tensor_scalar(o_first[:, :], src, der[:, RL + v:RL + v + 1], None, ALU.mult)
                ins.then_inc(o_done, 1)

            top(0)
            for v in range(8):
                if v + 1 < 8:
                    top(v + 1)
                if v:
                    out(v - 1)
                dve.wait_ge(ta_full, D_UNITS * h + (N_MLA_UNITS + v + 1))
                if v:
                    dve.wait_ge(pv_done, D_UNITS * h + (N_MLA_UNITS + v))
                dve.tensor_copy(dPT[:, 0:3, :].rearrange("p a b -> p (a b)"), banks[4][:, 0:3 * P]).then_inc(eva_done, 1)
            out(7)

        dve.wait_ge(o_root, 1)
        chain.link(dve.reciprocal(o_rs[:, :], o_rs[:, :]))
        for qt in range(4):
            o = O_tok[:, qt, :].rearrange("p (h c) -> p h c", h=B_HEADS)
            r = o_rs[:, :].rearrange("p (h q) -> p h q", q=4)[:, :, qt:qt + 1].broadcast_to([P, B_HEADS, P])
            dve.tensor_tensor(o, o, r, ALU.mult).then_inc(o_scaled, 1)
        for h in range(B_HEADS):
            dve.wait_ge(gate_done, h + 1)
            dve.wait_ge(wide_full, N_MLA_FULL + D_FULL * B_HEADS + h + 1)
            if h >= 2:
                dve.wait_ge(og_ready, h - 1)
            dve.scalar_tensor_tensor(out=og[:, h % 2, :], in0=wide(h % 2, T), scalar=der[:, LAM + 6:LAM + 7], in1=gate2[:, h, :],
                                     op0=ALU.mult, op1=ALU.mult).then_inc(og_full, 1)
            dve.wait_ge(og_full, h + 1)
            dve.sem_inc(wide_free[h % 2], 1)
            if h:
                dve.wait_ge(og_hi, h)
                dve.tensor_tensor(h2_lo[:, h - 1, 0:T], og[:, (h - 1) % 2, :], h2_hi[:, h - 1, 0:T], ALU.subtract).then_inc(og_ready, 1)
        dve.wait_ge(og_hi, B_HEADS)
        dve.tensor_tensor(h2_lo[:, B_HEADS - 1, 0:T], og[:, 1, :], h2_hi[:, B_HEADS - 1, 0:T], ALU.subtract).then_inc(og_ready, 1)
        layer_sum(1, T, lambda m: z[:, m, 0:T], None)

    es.close()


def pack(inputs):
    g = {k: np.asarray(v) for k, v in inputs.items()}
    z = np.zeros

    def tiles(w, cols):
        w = w[:, cols]
        out = z((w.shape[0] // P, P, P), w.dtype)
        out[:, :, :w.shape[1]] = w.reshape(-1, P, w.shape[1])
        return list(out)

    s = []
    w_in = g["w_in_first"]
    for j in range(CT):
        s += tiles(w_in, slice(P * j, P * j + P)) + tiles(w_in, slice(HALF + P * j, HALF + P * j + P))
    for j in range(12):
        s += tiles(w_in, slice(1024 + P * j, 1024 + P * j + P))
    s += tiles(w_in, slice(2560, 2624)) + tiles(w_in, slice(2624, 2720))
    for j in range(KT):
        s += tiles(g["w_out"][0], slice(P * j, P * j + P))
    for j in range(FT):
        s += tiles(g["ffn_up"][0], slice(P * j, P * j + P)) + tiles(g["ffn_up"][0], slice(DFF + P * j, DFF + P * j + P))
    for j in range(KT // 2):
        s += tiles(g["ffn_down"][0], slice(2 * P * j, 2 * P * j + P)) + tiles(g["ffn_down"][0], slice(2 * P * j + P, 2 * P * j + 2 * P))
        s += [z((P, P), np.float32)] * 4
    w = g["mla_w_in_2"][0]
    for j in range(3):
        s += tiles(w, slice(P * j, P * j + P))
    s += tiles(w, slice(320, 416))
    for j in range(KT):
        s += tiles(w, slice(416 + P * j, 416 + P * j + P))
    qb, kvb = g["mla_w_qb_2"][0], g["mla_w_kvb_2"][0].reshape(P, A_HEADS, 2, 64)
    for p in range(A_HEADS // 2):
        for h in (2 * p, 2 * p + 1):
            s += tiles(qb, slice(A_QK * h, A_QK * h + A_QK))
        for part in range(2):
            s += [np.concatenate([kvb[:, 2 * p, part], kvb[:, 2 * p + 1, part]], axis=1)]
        s += [z((P, P), np.float32)] * 10
    for j in range(KT):
        s += tiles(g["out_w_2"][0], slice(P * j, P * j + P))
    w = g["diff_w_in_2"][0]
    for h in range(B_HEADS):
        for part in range(4):
            s += tiles(w, slice(D * part + P * h, D * part + P * h + P))
    for j in range(KT):
        s += tiles(g["out_w_2"][1], slice(P * j, P * j + P))
    stream = np.stack(s).reshape(N_BLOCKS, TILES, P, P).transpose(0, 2, 1, 3).reshape(N_BLOCKS, P, WBLK)

    aw = g["ada_w_2"].reshape(2, KT, P, 12, 256).transpose(0, 3, 2, 1, 4).reshape(ADA_BLOCKS, P, KT, 256)

    v = z((P, N_PCOL), np.float32)

    def put(name, a):
        a = np.asarray(a)
        v[:a.shape[0], PCOL[name]:PCOL[name] + a.shape[1]] = a

    def cols(a):
        return a.reshape(-1, P).T

    mu = g["mu_first"]
    m = z((14, P), np.float32)
    m[:12] = mu[:1536].reshape(12, P)
    m[12, :64] = mu[1536:1600]
    m[13, :96] = mu[1600:1696]
    put("mu", m.T)
    put("w0", cols(g["decay_w0"][0])); put("a0", cols(g["iclr_a0"][0]))
    put("k_k", cols(g["k_k"][0])); put("k_a", cols(g["k_a"][0])); put("r_k", cols(g["r_k"][0].reshape(-1)))
    put("lnx_g", cols(g["lnx_g"][0])); put("lnx_b", cols(g["lnx_b"][0]))
    put("cconv_w", g["cconv_w"][0].reshape(TAPS, CT, P).transpose(2, 1, 0).reshape(P, -1))
    put("cconv_b", cols(g["cconv_b"][0])); put("cln_g", cols(g["cln_g"][0])); put("cln_b", cols(g["cln_b"][0]))
    put("pre_mix", cols(g["norm_pre_mix"][0])); put("post_mix", cols(g["norm_post_mix"][0]))
    put("pre_ffn", cols(g["norm_pre_ffn"][0])); put("post_ffn", cols(g["norm_post_ffn"][0]))
    put("fconv_w", g["ffn_conv_w"][0].reshape(3, 2, FT, P).transpose(3, 2, 1, 0).reshape(P, -1))
    put("fconv_b", g["ffn_conv_b"][0].reshape(2, FT, P).transpose(2, 1, 0).reshape(P, -1))
    put("c", np.stack([cols(g["c_2"][0]), cols(g["c_ctx_2"])], axis=2).reshape(P, 16))
    put("ada_b", np.repeat(g["ada_b_2"].reshape(48, P).T, 2, axis=1))
    put("ln_g", cols(g["ln_g_2"].reshape(-1))); put("ln_b", cols(g["ln_b_2"].reshape(-1)))
    put("g_qa", cols(g["mla_g_qa_2"][0])); put("g_kva", cols(g["mla_g_kva_2"][0]))
    put("lam", g["diff_lambda_2"][0].T); put("g_sub", cols(g["diff_g_sub_2"][0]))

    lora = np.concatenate([g["decay_up"][0], g["iclr_up"][0]], axis=0)
    c = lambda a: np.ascontiguousarray(a)
    out = {
        "x_t": c(g["x"][0].T.reshape(KT, P, T).transpose(1, 0, 2)),
        "ctx_t": c(g["ctx_2"][0].T.reshape(KT, P, C).transpose(1, 0, 2)),
        "stream": c(stream), "ada_w": c(aw), "vectors": v, "lora_w": c(lora), "gate_w": c(g["gate_up"][0]),
    }
    out.update(constants())
    return out


def constants():
    j, t = np.meshgrid(np.arange(P), np.arange(P), indexing="ij")
    same = (j // CHUNK) == (t // CHUNK)
    sq = np.zeros((P, 7, P), np.float32)
    sq[:, 0] = j == t
    sq[:, 1] = 1
    sq[:, 2] = same
    sq[:, 3] = same & (j < t)
    sq[:, 4] = same & (j <= t)

    def rotation(rows, half):
        r = np.zeros((P, P), np.float32)
        for start in rows:
            for i in range(half):
                r[start + half + i, start + i] = -1
                r[start + i, start + half + i] = 1
        return r
    sq[:, 5] = rotation([64], 16)
    sq[:, 6] = rotation([0, 64], 32)
    lv = np.zeros((P, 12, P), np.float32)
    for n in range(6):
        s = 1 << n
        low = (j // (2 * s) == t // (2 * s)) & (j % (2 * s) >= s) & (t % (2 * s) < s)
        lv[:, n] = low
        lv[:, 6 + n] = low.T
    scan = np.ones((P, T), np.float32)
    scan[:, ::CHUNK] = 0

    def angles(dim):
        n = dim // 4
        inv = (np.float32(10000.0) ** (-np.arange(n, dtype=np.float32) / np.float32(n))).astype(np.float32)
        row, c = np.repeat(np.arange(T // 64, dtype=np.float32), 64), np.tile(np.arange(64, dtype=np.float32), T // 64)
        return np.concatenate([row[:, None] * inv, c[:, None] * inv], axis=-1).T
    ropes = np.zeros((2, P, 2, T), np.float32)
    a = angles(32)
    ropes[0, :, 0] = 1
    for o in (64, 80):
        ropes[0, o:o + 16, 0], ropes[0, o:o + 16, 1] = np.cos(a), np.sin(a)
    b = angles(64)
    for o in range(0, P, 32):
        ropes[1, o:o + 32, 0], ropes[1, o:o + 32, 1] = np.cos(b), np.sin(b)
    return {"squares": sq, "level_masks": lv, "scan_mask": scan, "ropes": ropes}


def kernel(**inputs):
    import numpy as _np
    import concourse.bacc as _bacc
    from concourse import mybir as _mybir
    from concourse.bass_utils import run_bass_kernel_spmd as _run

    arrays = pack(inputs)
    nc = _bacc.Bacc("TRN2", target_bir_lowering=False, num_devices=1)
    args = {name: nc.dram_tensor(f"in_{name}", list(a.shape), _mybir.dt.from_np(a.dtype), kind="ExternalInput").ap()
            for name, a in arrays.items()}
    out_t = nc.dram_tensor("out_t", [P, KT, T], F32, kind="ExternalOutput").ap()
    build(nc, out_t=out_t, **args)
    r = _run(nc, [{f"in_{name}": a for name, a in arrays.items()}], core_ids=[0])
    y = r.results[0]["out_t"]
    return _np.ascontiguousarray(y.transpose(2, 1, 0).reshape(1, T, D))
```

```python
from contextlib import ExitStack, contextmanager
import math

import numpy as np
import concourse.bass as bass
from concourse import mybir

F32 = mybir.dt.float32
F32R = mybir.dt.float32r
U8 = mybir.dt.uint8
ALU = mybir.AluOpType
ACT = mybir.ActivationFunctionType
AX = mybir.AxisListType

P = 128
T = 512
C = 256
TA = T + C
D = 1024
KT = D // P
HALF = 512
CT = HALF // P
CHUNK = 64
NCH = T // CHUNK
TAPS = 31
DFF = 2816
FT = DFF // P
A_HEADS, A_QK, A_V = 16, 96, 64
B_HEADS, B_D = 8, 64
RMS_EPS, LN_EPS, GN_EPS = 1e-6, 1e-5, 64e-5
ALPHA = 4.0 ** 0.25
LAMBDA_INIT = 0.8 - 0.6 * math.exp(-0.3)
TILES = 16
WBLK = TILES * P

N_IN, N_OUT, N_UP, N_DOWN = 11, 4, FT, 12
N_MLA_IN, N_MLA, N_MLA_OUT, N_DIFF, N_DIFF_OUT = 6, 8, 4, 16, 4
ADA_BLOCKS = 24
STREAM = {}
_at = 0
for _name, _n in (("in", N_IN), ("out", N_OUT), ("up", N_UP), ("down", N_DOWN), ("mla_in", N_MLA_IN),
                  ("mla", N_MLA), ("mla_out", N_MLA_OUT), ("diff", N_DIFF), ("diff_out", N_DIFF_OUT)):
    STREAM[_name] = _at
    _at += _n
N_BLOCKS = _at

PCOL = {}
_at = 0
for _name, _n in (("mu", 14), ("w0", 4), ("a0", 4), ("k_k", 4), ("k_a", 4), ("r_k", 4), ("lnx_g", 4),
                  ("lnx_b", 4), ("cconv_w", 4 * TAPS), ("cconv_b", 4), ("cln_g", 4), ("cln_b", 4),
                  ("pre_mix", 8), ("post_mix", 8), ("pre_ffn", 8), ("post_ffn", 8),
                  ("fconv_w", 3 * 2 * FT), ("fconv_b", 2 * FT), ("c", 16), ("ada_b", 96),
                  ("ln_g", 16), ("ln_b", 16), ("g_qa", 2), ("g_kva", 1), ("lam", 4), ("g_sub", 1)):
    PCOL[_name] = _at
    _at += _n
N_PCOL = _at


class Chain:

    def __init__(self, eng, sem):
        self.eng, self.sem, self.n, self.reg = eng, sem, 0, None

    def mark(self, ins):
        self.n += 1
        ins.then_inc(self.sem, 1)
        return self.n

    def wait(self, n=None):
        n = self.n if n is None else n
        self.eng.wait_ge(self.sem, n if self.reg is None else self.reg + n)

    def link(self, ins):
        self.mark(ins)
        self.wait()

    @contextmanager
    def loop(self, count, per):
        start = self.n
        with self.eng.Fori(0, count) as i:
            self.reg = i * per
            yield i
            assert self.n - start == per, (self.n - start, per)
            self.reg = None
        self.n = start + per * count


def build(nc, x_t, ctx_t, stream, ada_w, vectors, squares, level_masks, scan_mask, ropes, lora_w, gate_w,
          out_t):
    es = ExitStack()

    base = 16512
    place = [base]

    def at(name, shape, dt, offset):
        return nc.alloc_sbuf_tensor_at(name, shape, dt, offset=offset)

    def fixed(name, shape, dt=F32, size=4):
        n = size
        for s in shape[1:]:
            n *= s
        t = at(name, shape, dt, place[0])
        place[0] += (n + 31) // 32 * 32
        return t

    raw = fixed("raw", [P, 2, WBLK])
    w_hi = fixed("w_hi", [P, 2, TILES, P], F32R)
    w_lo = fixed("w_lo", [P, 2, TILES, P], F32R)
    sq_c = fixed("sq_c", [P, 7, P])
    lvl = fixed("lvl", [P, 12, P], U8, 1)
    prm = fixed("prm", [P, N_PCOL])
    der = fixed("der", [P, 128])
    ada = fixed("ada", [P, 2, 3, KT, 2])
    tmp_at = place[0]
    scan_m = fixed("scan_m", [P, T])
    lora = fixed("lora", [64, HALF])
    gup = fixed("gup", [96, HALF])
    S0 = place[0]
    KB = 1024

    def reg(name, shape, kb, dt=F32):
        return at(name, shape, dt, S0 + int(kb * KB))

    ident, ones, head_ones = sq_c[:, 0, :], sq_c[:, 1, :], sq_c[:, 2, :]
    before, until_m = sq_c[:, 3, :], sq_c[:, 4, :]

    lvl_f = reg("lvl_f", [P, 12, P], 137)
    xT = reg("xT", [P, KT, T], 0)
    h1_hi = reg("h1_hi", [P, KT, T], 16, F32R)
    h1_lo = reg("h1_lo", [P, KT, T], 32, F32R)
    sq = reg("sq", [P, 2, T], 48)
    htmp = reg("htmp", [P, 2, T], 52)
    rstd = reg("rstd", [P, T], 56)
    glu_s = reg("glu_s", [P, 2, T], 58)
    Q = reg("Q", [P, 14, T], 64)
    cpad = reg("cpad", [P, CT, TAPS - 1 + T], 92)
    cacc = reg("cacc", [P, CT, T], 101)
    ada_raw = reg("ada_raw", [P, 2, KT, 256], 109)
    ada_row = reg("ada_row", [32, 2, 256], 125)
    ada_col = reg("ada_col", [P, 4, 32], 127)

    aB = reg("aB", [P, CT, T], 0)
    eA = reg("eA", [P, CT, T], 8)
    lw = reg("lw", [P, CT, T], 16)
    cc = reg("cc", [P, CT, T], 24)
    e1 = reg("e1", [P, CT, T], 32)
    kk = reg("kk", [P, CT, T], 40)
    eR = reg("eR", [P, CT, T], 48)
    gg = reg("gg", [P, CT, T], 56)
    rr, ky, vv = Q[:, 0:4, :], Q[:, 4:8, :], Q[:, 8:12, :]
    A_tok = reg("A_tok", [P, CT, HALF], 16)
    B_tok = reg("B_tok", [P, CT, HALF], 24)
    K_tok = reg("K_tok", [P, CT, HALF], 32)
    V_tok = reg("V_tok", [P, CT, HALF], 40)
    U = reg("U", [P, CT, HALF], 80)
    Di = [reg(f"Di{e}", [P, 4, P], 109 + 13 * e) for e in range(2)]
    DiT = [reg(f"DiT{e}", [P, 4, P], 111 + 13 * e) for e in range(2)]
    Lt = [reg(f"Lt{e}", [P, 4, P], 113 + 13 * e) for e in range(2)]
    Gt = [reg(f"Gt{e}", [P, 4, P], 115 + 13 * e) for e in range(2)]
    Mt = [reg(f"Mt{e}", [P, 4, P], 117 + 13 * e) for e in range(2)]
    RKt = [reg(f"RKt{e}", [P, 4, P], 119 + 13 * e) for e in range(2)]
    MV = [reg(f"MV{e}", [P, 4, 64], 121 + 13 * e) for e in range(2)]
    RBt = [reg(f"RBt{h}", [P, 4, P], 92 + 2 * h if h < 4 else 135 + 2 * (h - 4)) for h in range(8)]
    SA = reg("SA", [P, HALF], 88)
    St = [reg("St0", [P, CT, P], 143), reg("St1", [P, CT, P], 90)]
    sqk = reg("sqk", [P, 2, T], 129)
    knt = reg("knt", [P, 2, T], 133)
    kft = reg("kft", [P, 2, T], 137)

    pairs = [es.enter_context(nc.psum_tensor(f"banks{2 * i}{2 * i + 1}", [P, 2, 512], F32)) for i in range(4)]
    banks = [pairs[i // 2][:, i % 2, :] for i in range(8)]

    def wide(w, n=TA):
        return pairs[w][:, :, :].rearrange("p a b -> p (a b)")[:, 0:n]


    def sem(name):
        return es.enter_context(nc.semaphore(name))

    def col(name, i=0, n=1):
        return prm[:, bass.ds(i + PCOL[name], n)] if not isinstance(i, int) else prm[:, PCOL[name] + i:PCOL[name] + i + n]

    s_x = [sem(f"x_loaded{k}") for k in range(2)]
    s_const = sem("constants_loaded")
    raw_full = [sem("raw_full0"), sem("raw_full1")]
    split_full = sem("split_full")
    block_done = sem("block_done")
    tile0_full = sem("tile0_full")
    hi_done = sem("hi_done")
    ada_full = [sem("ada_full0"), sem("ada_full1")]
    ada_free = [sem("ada_free0"), sem("ada_free1")]
    act_step, dve_step = sem("act_step"), sem("dve_step")
    sq_full, sq_free, sqrt_done = sem("sq_full"), sem("sq_free"), sem("sqrt_done")
    htmp_full = sem("htmp_full")
    h_hi_full, h_ready = sem("h_hi_full"), sem("h_ready")
    proj_free = [sem(f"proj_free{i}") for i in range(4)]
    glu_s_full, glu_s_free = sem("glu_s_full"), sem("glu_s_free")
    q_copied = sem("q_copied")
    silu_c, ada_done = sem("silu_c"), sem("ada_done")
    prep_done = sem("prep_done")
    one_done = sem("pool_constants")
    q_mixed = sem("q_mixed")
    conv_done = sem("conv_done")
    out_done = sem("out_done")

    ONE = 124
    OMU, OKA = 0, 14
    SILU_C = 18

    lora_in, lora_full, lora_evac = sem("lora_in"), sem("lora_full"), sem("lora_evac")
    chunk_end, exps_in, exps_done = sem("chunk_end"), sem("exps_in"), sem("exps_done")
    kk_raw, kk_sq, kk_sum, kk_max, kk_root = (sem(n) for n in ("kk_raw", "kk_sq", "kk_sum", "kk_max", "kk_root"))
    bonus_in, bonus_sum, bonus_done = sem("bonus_in"), sem("bonus_sum"), sem("bonus_done")
    ada_rows, ada_rows_free = sem("ada_rows"), sem("ada_rows_free")
    abkv_ready = sem("abkv_ready")
    tok_full, tok_done = sem("tok_full"), sem("tok_done")
    CT_END, ECT = 40, 72
    cln_sum, cln_centred, cln_sq, cln_root, cln_normed, conv_out = (sem(n) for n in (
        "cln_sum", "cln_centred", "cln_sq", "cln_root", "cln_normed", "conv_out"))
    csq = reg("csq", [P, CT, T], 109)
    cstd = reg("cstd", [P, T], 117)
    PE_STEPS = ["L", "LT", "MT", "RB", "RK", "MV", "Y0"] + [s + str(n) for n in range(1, 6) for s in "GPQ"][:-2] + ["Q5", "W", "U"]
    ACT_STEPS = ["DI", "DIT", "LT", "MV", "Y0", "G1", "G2", "G3", "G4", "G5", "W", "U"]
    DVE_STEPS = ["MT", "RB", "D0", "DT0", "RK"] + [s + str(n) for n in range(1, 5) for s in "PQ"] + ["Q5"]
    u_pe = [sem(f"unit_tensor{e}") for e in range(2)]
    u_act = [sem(f"unit_scalar{e}") for e in range(2)]
    u_dve = [sem(f"unit_vector{e}") for e in range(2)]

    def pe_at(c, step):
        return len(PE_STEPS) * c + PE_STEPS.index(step) + 1

    def act_at(c, step):
        return len(ACT_STEPS) * c + ACT_STEPS.index(step) + 1

    def dve_at(c, step):
        return len(DVE_STEPS) * c + DVE_STEPS.index(step) + 1

    sa_full, sa_done, st_full, st_done, y_full, y_done = (sem(n) for n in ("sa_full", "sa_done", "st_full", "st_done", "y_full", "y_done"))
    st_zero = sem("st_zero")
    mixo = reg("mixo", [P, KT, T], 64)
    fout = reg("fout", [P, KT, T], 16)
    act_hi = reg("act_hi", [P, FT, T], 48, F32R)
    act_lo = reg("act_lo", [P, FT, T], 92, F32R)
    yg = reg("yg", [P, 2, T], 136)
    yu = reg("yu", [P, 2, T], 140)
    nt = at("nt", [P, 2, T], F32, tmp_at)
    nr = at("nr", [P, T], F32, tmp_at + 4 * KB)
    nh = reg("nh", [P, 2, T], 140)
    nacc = reg("nacc", [P, T], 138)
    msq = reg("msq", [P, 2, T], 121)
    mrs = reg("mrs", [P, 2, T], 125)
    gn_mean, gn_centred, gn_sq, gn_var, gn_root, gn_normed, gn_scaled, mix_full, mix_hi_full, mix_ready = (sem(n) for n in (
        "gn_mean", "gn_centred", "gn_sq", "gn_var", "gn_root", "gn_normed", "gn_scaled", "mix_full", "mix_hi_full", "mix_ready"))
    out_copied, out_sq, out_summed = sem("out_copied"), sem("out_sq"), sem("out_summed")
    post_sum, post_root, x_done, pre_sq, pre_sq_read, pre_root = (sem(n) for n in (
        "post_sum", "post_root", "x_done", "pre_sq", "pre_sq_read", "pre_root"))
    nh_full, nh_hi, nh_ready = sem("nh_full"), sem("nh_hi"), sem("nh_ready")
    up_first, up_conv, up_gelu, up_prod, up_hi, act_ready = (sem(n) for n in (
        "up_first", "up_conv", "up_gelu", "up_prod", "up_hi", "act_ready"))
    down_full, down_free, conv2 = sem("down_full"), sem("down_free"), sem("ffn_conv_step")

    def half_of(n):
        return n % 2

    def both_parts(k):
        return (k + CT) % KT
    gate_s = reg("gate_s", [P, KT, TA], 16)
    lat = reg("lat", [P, 3, TA], 40)
    lat_hi = reg("lat_hi", [P, 3, TA], 49, F32R)
    lat_lo = reg("lat_lo", [P, 3, TA], 58, F32R)
    h2_hi = reg("h2_hi", [P, KT, TA], 67, F32R)
    h2_lo = reg("h2_lo", [P, KT, TA], 91, F32R)
    ctxT = reg("ctxT", [P, KT, C], 115)
    mh = reg("mh", [P, 2, TA], 123)
    lsq = reg("lsq", [P, 2, TA], 115)
    lrs = reg("lrs", [P, TA], 136)
    q_hi, q_lo, k_hi, k_lo = ([reg(f"{n}{e}", [P, TA], kb + 3 * e, F32R) for e in range(2)]
                              for n, kb in (("q_hi", 67), ("q_lo", 73), ("k_hi", 79), ("k_lo", 85)))
    V_hi, V_lo = ([reg(f"{n}{e}", [P, 6, P], kb + 3 * e, F32R) for e in range(2)] for n, kb in (("V_hi", 91), ("V_lo", 97)))
    Pf = reg("Pf", [P, 3, TA], 40)
    P_hi = reg("P_hi", [P, 3, TA], 103, F32R)
    P_lo = reg("P_lo", [P, 3, TA], 112, F32R)
    Vf = reg("Vf", [P, 6, P], 121)
    qf = reg("qf", [P, TA], 124)
    kf = [reg(f"kf{e}", [P, TA], 127 + 3 * e) for e in range(2)]
    otmp = reg("otmp", [P, TA], 133)
    Ls = reg("Ls", [P, TA], 136)
    Of = reg("Of", [P, TA], 139)
    rope = at("rope", [P, 2, T], F32, tmp_at)
    z = reg("z", [P, KT, TA], 16)
    ctx2 = reg("ctx2", [P, KT, C], 40)
    zacc = reg("zacc", [P, TA], 115)
    zsq = reg("zsq", [P, 2, TA], 118)
    zrs = reg("zrs", [P, TA], 124)
    zh = reg("zh", [P, 2, TA], 127)
    MX, NM, RS, RL = 40, 52, 64, 76
    s_ctx, s_rope = sem("ctx_loaded"), sem("rope_loaded")
    mh_full, mh_hi, mh_ready = sem("mh_full"), sem("mh_hi"), sem("mh_ready")
    wide_free = [sem("wide_free0"), sem("wide_free1")]
    wide_full = sem("wide_full")
    lat_sq, lat_sum, lat_root, lat_normed, lat_high, lat_ready = (sem(n) for n in (
        "lat_sq", "lat_sum", "lat_root", "lat_normed", "lat_high", "lat_ready"))
    kpe_copied, kpe_rot, kpe_done, gate_done = sem("kpe_copied"), sem("kpe_rot"), sem("kpe_done"), sem("gate_done")
    pr_evac, rope_done = sem("head_evac"), sem("rope_done")
    head_high, head_low, top_ready, top_row = sem("head_high"), sem("head_low"), sem("top_ready"), sem("top_row")
    exp_full, exp_high, exp_low, kt_done = sem("exp_full"), sem("exp_high"), sem("exp_low"), sem("key_tile_done")
    o_copied, pair_out, lat_dead = sem("o_copied"), sem("pair_out"), sem("head_constants")
    kv_copied, sums_inverse, pair_divided = sem("kv_copied"), sem("sums_inverse"), sem("pair_divided")
    ot_done, ot_hi, ot_ready = sem("ot_done"), sem("ot_hi"), sem("ot_ready")
    z_gated, z_acc, z_sum, z_centred, z_sq, z_root, z_normed, z_out = (sem(n) for n in (
        "z_gated", "z_acc", "z_sum", "z_centred", "z_sq", "z_root", "z_normed", "z_out"))
    ada_one = sem("ada_one")
    mod_done = gn_scaled
    z1 = reg("z1", [P, KT, T], 0)

    def z_of(layer):
        return z if layer == 0 else z1
    A_SCALE = (A_QK) ** -0.5
    T0_MLA = STREAM["down"]
    SCORE_USES = ["S2", "M0", "S3", "M1", "S4", "M2", "S5", "M3", "M4", "top"]
    SLOTS = [["q", "S0", "R", "S1"] + SCORE_USES, ["q", "k", "R", "V", "S0", "S1"] + SCORE_USES]
    FIRST_SLOT = ["q", "k", "R", "V", "M0", "M1", "M2", "M3", "M4", "top"]
    LAST_SLOT = [f"S{j}" for j in range(6)]
    PAIR_USES = len(SLOTS[0]) + len(SLOTS[1])
    N_PAIRS = A_HEADS // 2

    def use_of(p, e, name):
        if e is None:
            i = FIRST_SLOT.index(name)
            return i % 2, 6 + i // 2, i + 1
        slot = LAST_SLOT if isinstance(p, int) and p == N_PAIRS - 1 and e == 1 else SLOTS[e]
        i = len(FIRST_SLOT) + e * len(SLOTS[0]) + slot.index(name)
        return i % 2, p * (PAIR_USES // 2) + (6 + i // 2), p * (PAIR_USES - 1) + i
    N_MLA_USES = 6 + (len(FIRST_SLOT) + (N_PAIRS - 1) * PAIR_USES + len(SLOTS[0]) + len(LAST_SLOT)) // 2 + 4
    N_MLA_FULL = len(FIRST_SLOT) + (N_PAIRS - 1) * (PAIR_USES - 1) + len(SLOTS[0]) - 1 + len(LAST_SLOT)
    O_tok = reg("O_tok", [P, 4, D], 0)
    gate2 = reg("gate2", [P, KT, T], 40)
    dq = reg("dq", [P, T], 115)
    dk = reg("dk", [P, TA], 117)
    dV = reg("dV", [P, 6, P], 120)
    dP = [reg(f"dP{i}", [P, TA], 123 + 3 * i) for i in range(2)]
    dPT = reg("dPT", [P, 6, P], 129)
    dv = reg("dv", [P, TA], 132)
    dt = reg("dt", [P, T], 135)
    o_first = reg("o_first", [P, P], 137)
    o_junk = reg("o_junk", [P, 2, P], 143)
    og = reg("og", [P, 2, T], 138)
    QQ = [reg(f"QQ{m}", [P, T], 56 + 2 * m, F32R) for m in range(2)]
    KK = [reg(f"KK{m}", [P, TA], 60 + 3 * m, F32R) for m in range(2)]
    KL = reg("KL", [P, TA], 138, F32R)
    o_ss = reg("o_ss", [P, 32], 142)
    o_rs = reg("o_rs", [P, 32], 142.25)
    NL, LAM = 88, 96
    lam_prod, lam_sum, lam_exp = (sem(n) for n in ("lam_prod", "lam_sum", "lam_exp"))
    o_sq, o_root, o_scaled = (sem(n) for n in ("o_sq", "o_root", "o_scaled"))
    nm_ready, p_full, ta_full, tb_full, eva_done, evb_done, pv_done, o_done = (
        top_ready, exp_full, exp_high, exp_low, head_high, head_low, kt_done, o_copied)
    AFTER_MLA = {"nm": A_HEADS, "p": 6 * A_HEADS, "ta": 6 * A_HEADS, "tb": 6 * A_HEADS, "eva": 3 * A_HEADS, "evb": 3 * A_HEADS,
                 "pv": 6 * A_HEADS, "o": A_HEADS + 2}
    og_full, og_hi, og_ready = mh_full, mh_hi, mh_ready
    qk_high, qk_low = lat_high, lat_ready
    B_SCALE = B_D ** -0.5
    N_MLA_EVAC = 2 * N_PAIRS
    D_USES, D_FULL, D_UNITS, D_EVAC = 7, 12, 8, 5
    block = es.enter_context(nc.Block())

    @block.sync
    def _(sp):
        for k in range(2):
            sp.dma_start(xT[:, 4 * k:4 * k + 4, :], x_t[:, 4 * k:4 * k + 4, :]).then_inc(s_x[k], 16)
        sp.dma_start(prm[:, :], vectors).then_inc(s_const, 16)
        sp.dma_start(sq_c[:, :, :], squares).then_inc(s_const, 16)
        sp.dma_start(lvl_f[:, :, :], level_masks).then_inc(s_const, 16)
        sp.dma_start(scan_m[:, :], scan_mask).then_inc(s_const, 16)
        sp.dma_start(lora[:, :], lora_w).then_inc(s_const, 16)
        sp.dma_start(gup[:, :], gate_w).then_inc(s_const, 16)

        def weights(n, half, first=False):
            if not first:
                sp.wait_ge(split_full, n - 1)
            sp.dma_start(raw[:, half, :], stream[n, :, :]).then_inc(raw_full[half], 16)

        def ada_block(b, half, use, first=False):
            if not first:
                sp.wait_ge(ada_free[half], use)
            sp.dma_start(ada_raw[:, half, :, :], ada_w[b, :, :, :]).then_inc(ada_full[half], 16)

        for s in range(2):
            weights(s, s, first=True)
        with sp.Fori(0, N_IN // 2 - 1) as i:
            for s in range(2):
                weights(2 * i + (2 + s), s)
        weights(N_IN - 1, 0)
        for a in range(2):
            ada_block(a, a, 0, first=True)
        with sp.Fori(1, ADA_BLOCKS // 2) as i:
            for a in range(2):
                ada_block(2 * i + a, a, i)
        weights(N_IN, 1)
        with sp.Fori(0, (N_BLOCKS - N_IN - 1) // 2) as i:
            for s in range(2):
                weights(2 * i + (N_IN + 1 + s), s)
        if (N_BLOCKS - N_IN - 1) % 2:
            weights(N_BLOCKS - 1, 0)
        for k in range(KT):
            sp.wait_ge(z_out, KT + k + 1)
            sp.dma_start(out_t[:, k, :], z1[:, k, :]).then_inc(out_done, 16)
        sp.wait_ge(out_done, 16 * KT)

    @block.gpsimd
    def _(pool):
        def split(n, half, use, first=False):
            pool.wait_ge(raw_full[half], 16 * (use + 1))
            if not first:
                pool.wait_ge(block_done, n - 1)
            src = raw[:, half, :].rearrange("p (t c) -> p t c", t=TILES)
            pool.tensor_tensor(w_hi[:, half, :, :], src, one, ALU.mult).then_inc(hi_done, 1)
            pool.wait_ge(hi_done, n + 1)
            pool.tensor_tensor(w_lo[:, half, :, :], src, w_hi[:, half, :, :], ALU.subtract).then_inc(split_full, 1)

        pool.memset(der[:, ONE:ONE + 1], 1.0).then_inc(one_done, 1)
        pool.wait_ge(one_done, 1)
        one = der[:, ONE:ONE + 1].unsqueeze(1).broadcast_to([P, TILES, P])
        pool.memset(cpad[:, :, 0:TAPS - 1], 0.0).then_inc(one_done, 1)
        for s in range(2):
            split(s, s, 0, first=True)
        before = STREAM["mla"] + 2
        with pool.Fori(0, before // 2 - 1) as i:
            for s in range(2):
                split(2 * i + (2 + s), s, i + 1)
        if before % 2:
            split(before - 1, 0, before // 2)
        def low_part(p, e, part):
            n = 6 * p + (3 * e + part + 1)
            pool.wait_ge(head_high, n)
            if part == 0:
                ins = pool.tensor_tensor(k_lo[e][0:64, :], kf[e][0:64, :], k_hi[e][0:64, :], ALU.subtract)
            elif part == 1:
                c = slice(64 * e, 64 * e + 64)
                ins = pool.tensor_tensor(V_lo[e][:, :, c], Vf[:, :, c], V_hi[e][:, :, c], ALU.subtract)
            else:
                ins = pool.tensor_tensor(q_lo[e][0:96, :], qf[0:96, :], q_hi[e][0:96, :], ALU.subtract)
            ins.then_inc(head_low, 1)

        def finish(p):
            pool.wait_ge(sums_inverse, 3 * p + 3)
            pool.tensor_tensor(Of[:, :], Of[:, :], Ls[:, :], ALU.mult).then_inc(pair_divided, 1)
            pool.wait_ge(pair_divided, p + 1)
            pool.tensor_tensor(gate_s[:, p, :], gate_s[:, p, :], Of[:, :], ALU.mult).then_inc(pair_out, 1)

        def mla_pair(p, n, half, use, done=True):
            low_part(p, 1, 0)
            low_part(p, 1, 1)
            split(n, half, use)
            low_part(p, 1, 2)
            if not (isinstance(p, int) and p == N_PAIRS - 1):
                low_part(p + 1, 0, 0)
                low_part(p + 1, 0, 1)
            if done:
                finish(p - 1)
            if not (isinstance(p, int) and p == N_PAIRS - 1):
                low_part(p + 1, 0, 2)

        pool.sem_inc(pair_out, 1)
        for part in range(3):
            low_part(0, 0, part)
        first = STREAM["mla"] + 2
        mla_pair(0, first, half_of(first), first // 2, done=False)
        with pool.Fori(0, (N_PAIRS - 2) // 2) as i:
            for u in range(2):
                n = first + 1 + u
                mla_pair(2 * i + (1 + u), 2 * i + n, half_of(n), i + n // 2)
        mla_pair(N_PAIRS - 1, first + N_PAIRS - 1, half_of(first + N_PAIRS - 1), (first + N_PAIRS - 1) // 2)
        finish(N_PAIRS - 1)
        after = before + N_PAIRS
        if after % 2:
            split(after, 1, after // 2)
        rest = after + after % 2
        with pool.Fori(0, (N_BLOCKS - rest) // 2) as i:
            for s in range(2):
                split(2 * i + (rest + s), s, i + rest // 2)
        if N_BLOCKS % 2:
            split(N_BLOCKS - 1, 0, N_BLOCKS // 2)

    @block.tensor
    def _(pe):
        pe.wait_ge(s_const, 96)
        for k in range(KT):
            pe.wait_ge(sq_full, k + 1)
            pe.matmul(banks[6][:, :], ones, sq[:, k % 2, :], start=(k == 0), stop=(k == KT - 1)).then_inc(sq_free, 1)

        def project(bank_of, half, n, frees, rhs_hi, rhs_lo, ready=None, order=range(KT)):
            pe.wait_ge(split_full, n + 1)
            for j in range(2):
                b = bank_of[j]
                pe.wait_ge(proj_free[b], frees)
                for at_k, k in enumerate(order):
                    t = KT * j + k
                    if ready is not None and j == 0:
                        pe.wait_ge(ready, at_k + 1)
                    hi, lo = w_hi[:, half, t, :], w_lo[:, half, t, :]
                    pe.matmul(banks[b][:, :], hi, rhs_hi[:, k, :], start=(at_k == 0), stop=False)
                    pe.matmul(banks[b][:, :], hi, rhs_lo[:, k, :], start=False, stop=False)
                    mm = pe.matmul(banks[b][:, :], lo, rhs_hi[:, k, :], start=False, stop=(at_k == KT - 1))
                mm.then_inc(tile0_full if j == 0 else block_done, 1)

        with pe.Fori(0, N_IN // 2) as i:
            for s in range(2):
                project([2 * s, 2 * s + 1], s, 2 * i + s, i + 1, h1_hi, h1_lo, ready=None if s else h_ready)
        project([0, 1], 0, N_IN - 1, N_IN // 2 + 1, h1_hi, h1_lo)
        pe.wait_ge(lora_in, 2)
        for c in range(CT):
            for j, (w, x) in enumerate(((lora[0:32], Q[0:32, 12]), (lora[32:64], Q[32:64, 12]), (gup[0:96], Q[0:96, 13]))):
                m = 3 * c + j
                if m == 0:
                    pe.wait_ge(q_mixed, 14)
                if m >= 6:
                    pe.wait_ge(lora_evac, m - 5)
                pe.matmul(banks[m % 6][:, :], w[:, P * c:P * c + P], x, start=True, stop=True).then_inc(lora_full, 1)

        def ada_rows_of(g):
            if g >= 2:
                pe.wait_ge(ada_rows_free, g - 1)
            for a in range(2):
                pe.wait_ge(ada_full[a], 16 * (g + 1))
                for k in range(KT):
                    mm = pe.matmul(banks[6 + g % 2][0:2, 256 * a:256 * a + 256], der[:, SILU_C + 2 * k:SILU_C + 2 * k + 2],
                                   ada_raw[:, a, k, :], start=(k == 0), stop=(k == KT - 1))
                mm.then_inc(ada_free[a] if a == 0 else ada_rows, 1)

        def head_sums(ready, src, full, b0, c):
            pe.wait_ge(ready, c + 1)
            pe.matmul(banks[b0 + c][:, :], head_ones, src, start=True, stop=True).then_inc(full, 1)

        pe.wait_ge(silu_c, 1)
        for c in range(CT):
            if c < 2:
                pe.wait_ge(lora_evac, 7 + c)
            head_sums(kk_sq, sqk[:, c % 2, :], kk_sum, 0, c)
            ada_rows_of(c)
        for g in range(4, 8):
            ada_rows_of(g)
        for c in range(CT):
            if c < 2:
                pe.wait_ge(lora_evac, 11 + c)
            head_sums(bonus_in, rr[:, c, :], bonus_sum, 0, c)
        for g in range(8, 12):
            ada_rows_of(g)
        n = 0
        for a, src in enumerate((eA, aB, ky, vv)):
            pe.wait_ge(abkv_ready, min(a + 1, 3))
            for tt in range(4):
                b = n % 4
                if n < 4:
                    pe.wait_ge(bonus_done, CT)
                else:
                    pe.wait_ge(tok_done, n - 3)
                for c in range(CT):
                    mm = pe.transpose(banks[b][:, P * c:P * c + P], src[:, c, P * tt:P * tt + P], ident)
                mm.then_inc(tok_full, 1)
                n += 1
        def unit(c, e, step):
            X = banks[4 * e:4 * e + 4]
            rows, h = slice(64 * e, 64 * e + 64), 2 * c + e
            cols = slice(64 * h, 64 * h + 64)
            if step == "L":
                if c == 0:
                    pe.wait_ge(tok_done, 16)
                    pe.wait_ge(ada_rows_free, 12)
                else:
                    pe.wait_ge(u_act[e], act_at(c - 1, "W"))
                b, lhs, rhs = X[0], eA[rows, c, :], aB[rows, c, :]
            elif step == "LT":
                if c:
                    pe.wait_ge(u_act[e], act_at(c - 1, "U"))
                b, lhs, rhs = X[1], aB[rows, c, :], eA[rows, c, :]
            elif step == "MT":
                if c:
                    pe.wait_ge(u_dve[e], dve_at(c - 1, "Q5"))
                b, lhs, rhs = X[2], ky[rows, c, :], eA[rows, c, :]
            elif step == "RB":
                if c:
                    pe.wait_ge(u_act[e], act_at(c - 1, "Y0"))
                b, lhs, rhs = X[3], aB[rows, c, :], eR[rows, c, :]
            elif step == "RK":
                pe.wait_ge(u_dve[e], dve_at(c, "MT"))
                b, lhs, rhs = X[2], ky[rows, c, :], eR[rows, c, :]
            elif step == "MV":
                pe.wait_ge(u_dve[e], dve_at(c, "RB"))
                for tt in range(4):
                    mm = pe.matmul(X[3][:, 64 * tt:64 * tt + 64], Mt[e][:, tt, :], V_tok[:, tt, cols], start=True, stop=True)
                mm.then_inc(u_pe[e], 1)
                return
            elif step == "Y0":
                pe.wait_ge(u_dve[e], dve_at(c, "RK"))
                pe.wait_ge(u_act[e], act_at(c, "MV"))
                for tt in range(4):
                    mm = pe.matmul(X[3][rows, P * tt:P * tt + P], V_tok[:, tt, cols], RKt[e][:, tt, :], start=True, stop=True)
                mm.then_inc(u_pe[e], 1)
                return
            elif step == "W":
                pe.wait_ge(u_dve[e], dve_at(c, "Q5"))
                for tt in range(4):
                    mm = pe.matmul(X[0][rows, P * tt:P * tt + P], A_tok[:, tt, cols], DiT[e][:, tt, :], start=True, stop=True)
                mm.then_inc(u_pe[e], 1)
                return
            elif step == "U":
                for tt in range(4):
                    mm = pe.matmul(X[1][:, 64 * tt:64 * tt + 64], DiT[e][:, tt, :], MV[e][:, tt, :], start=True, stop=True)
                mm.then_inc(u_pe[e], 1)
                return
            else:
                n = int(step[1])
                if step[0] == "G":
                    if n == 1:
                        pe.wait_ge(u_act[e], act_at(c, "LT"))
                        pe.wait_ge(u_dve[e], dve_at(c, "D0"))
                    else:
                        pe.wait_ge(u_dve[e], dve_at(c, f"P{n - 1}"))
                    b, lhs, rhs = X[0], Lt[e], Di[e]
                elif step[0] == "P":
                    pe.wait_ge(u_act[e], act_at(c, f"G{n}"))
                    pe.wait_ge(u_dve[e], dve_at(c, f"Q{n - 1}" if n > 1 else "DT0"))
                    b, lhs, rhs = X[1], DiT[e], Gt[e]
                else:
                    if n == 1:
                        pe.wait_ge(u_dve[e], dve_at(c, "RK"))
                    pe.wait_ge(u_act[e], act_at(c, f"G{n}"))
                    if n == 5:
                        pe.wait_ge(u_dve[e], dve_at(c, "Q4"))
                    b, lhs, rhs = X[2], Gt[e], DiT[e]
                for tt in range(4):
                    mm = pe.matmul(b[:, P * tt:P * tt + P], lhs[:, tt, :], rhs[:, tt, :], start=True, stop=True)
                mm.then_inc(u_pe[e], 1)
                return
            for tt in range(4):
                ts = slice(P * tt, P * tt + P)
                mm = pe.matmul(b[:, ts], lhs[:, ts], rhs[:, ts], start=True, stop=True)
            mm.then_inc(u_pe[e], 1)

        for c in range(CT):
            for step in PE_STEPS:
                for e in range(2):
                    unit(c, e, step)

        pe.wait_ge(st_zero, 1)
        for e in range(2):
            pe.wait_ge(u_act[e], act_at(CT - 1, "U"))
        for n in range(NCH):
            tt, r = n // 2, slice(64 * (n % 2), 64 * (n % 2) + 64)
            t0 = CHUNK * n
            state = St[n % 2]
            if n:
                pe.wait_ge(st_done, 2 * n)
            for c in range(CT):
                mm = pe.matmul(banks[0][r, P * c:P * c + P], eA[:, c, t0:t0 + CHUNK], state[:, c, :], start=True, stop=True)
            mm.then_inc(sa_full, 1)
            if n >= 2:
                pe.wait_ge(y_done, n - 1)
            yb = banks[2 + n % 2]
            for c in range(CT):
                pe.matmul(yb[:, CHUNK * c:CHUNK * c + CHUNK], state[:, c, :], eR[:, c, t0:t0 + CHUNK], start=(c == 0), stop=False,
                          skip_group_check=True)
            if n < NCH - 1:
                for c in range(CT):
                    pe.matmul(banks[1][:, P * c:P * c + P], ident, state[:, c, :], start=(c == 0), stop=False, skip_group_check=True)
            pe.wait_ge(sa_done, n + 1)
            if n < NCH - 1:
                for c in range(CT):
                    ch = slice(P * c, P * c + P)
                    pe.matmul(banks[1][:, ch], B_tok[r, tt, ch], SA[r, ch], start=False, stop=False, skip_group_check=True)
                    mm = pe.matmul(banks[1][:, ch], K_tok[r, tt, ch], V_tok[r, tt, ch], start=False, stop=(c == CT - 1), skip_group_check=True)
                mm.then_inc(st_full, 1)
            for h in range(8):
                c, hr = h // 2, slice(64 * (h % 2), 64 * (h % 2) + 64)
                mm = pe.matmul(yb[hr, CHUNK * c:CHUNK * c + CHUNK], SA[r, 64 * h:64 * h + 64],
                               RBt[h][r, tt, 64 * (n % 2):64 * (n % 2) + 64], start=False, stop=(h == 7), skip_group_check=True)
            mm.then_inc(y_full, 1)
            if n == 0:
                for c in range(CT):
                    mm = pe.matmul(banks[4][:, :], ones, cacc[:, c, :], start=(c == 0), stop=(c == CT - 1))
                mm.then_inc(cln_sum, 1)
            if n == 3:
                for c in range(CT):
                    pe.wait_ge(cln_sq, c + 1)
                    pe.matmul(banks[5][:, :], ones, csq[:, c, :], start=(c == 0), stop=(c == CT - 1)).then_inc(cln_sum, 1)
        pe.wait_ge(y_done, NCH)
        for c in range(CT):
            pe.matmul(banks[4 + c][:, :], head_ones, ky[:, c, :], start=True, stop=True).then_inc(gn_mean, 1)
        for c in range(CT):
            pe.wait_ge(gn_sq, c + 1)
            pe.matmul(banks[4 + c][:, :], head_ones, msq[:, c % 2, :], start=True, stop=True).then_inc(gn_var, 1)
        for n in range(STREAM["out"], STREAM["out"] + N_OUT):
            s = half_of(n)
            project([2 * s, 2 * s + 1], s, n, n // 2 + 1, h1_hi, h1_lo, ready=mix_ready if n == STREAM["out"] else None,
                    order=[both_parts(k) for k in range(KT)])

        def post_and_pre(m):
            pe.wait_ge(out_summed, KT * (m + 1))
            pe.matmul(banks[6][:, :], ones, nacc[:, :], start=True, stop=True).then_inc(post_sum, 1)
            if m == 0:
                for k in range(KT):
                    pe.wait_ge(pre_sq, k + 1)
                    pe.matmul(banks[7][:, :], ones, nt[:, k % 2, :], start=(k == 0), stop=(k == KT - 1)).then_inc(pre_sq_read, 1)

        post_and_pre(0)
        with pe.Fori(0, N_UP // 2) as i:
            for u in range(2):
                s = half_of(STREAM["up"] + u)
                n = 2 * i + (STREAM["up"] + u)
                project([2 * s, 2 * s + 1], s, n, i + (STREAM["up"] + u) // 2 + 1, h1_hi, h1_lo, ready=None if u else nh_ready)
        pe.wait_ge(act_ready, FT)
        with pe.Fori(0, 2) as i:
            for u in range(6):
                s = half_of(STREAM["down"] + u)
                pe.wait_ge(split_full, 6 * i + (STREAM["down"] + u + 1))
                for t in range(TILES):
                    t_of = TILES * (u % 3) + t
                    j, k = t_of // FT, t_of % FT
                    if j == 2:
                        break
                    m = 2 * (u // 3) + j
                    b = banks[4 + m]
                    if k == 0:
                        pe.wait_ge(down_free, 4 * i + (m + 1))
                    hi, lo = w_hi[:, s, t, :], w_lo[:, s, t, :]
                    pe.matmul(b[:, :], hi, act_hi[:, k, :], start=(k == 0), stop=False)
                    pe.matmul(b[:, :], hi, act_lo[:, k, :], start=False, stop=False)
                    mm = pe.matmul(b[:, :], lo, act_hi[:, k, :], start=False, stop=(k == FT - 1))
                    if k == FT - 1 and j == 0:
                        mm.then_inc(down_full, 1)
                mm.then_inc(block_done, 1)
        post_and_pre(1)
        def wide_project(j, k0, kn, w, s, rhs_hi, rhs_lo, n_cols=TA, tile0=0, ready=None, ready_base=0):
            for k in range(kn):
                if ready is not None:
                    pe.wait_ge(ready, ready_base + k + 1)
                t = tile0 + k
                hi, lo = w_hi[:, s, t, :], w_lo[:, s, t, :]
                for a, b in ((0, 512), (512, TA)):
                    if a >= n_cols:
                        continue
                    out = pairs[w][:, a // 512, 0:b - a]
                    pe.matmul(out, hi, rhs_hi[:, k0 + k, a:b], start=(k == 0), stop=False)
                    pe.matmul(out, hi, rhs_lo[:, k0 + k, a:b], start=False, stop=False)
                for a, b in ((0, 512), (512, TA)):
                    if a >= n_cols:
                        continue
                    mm = pe.matmul(pairs[w][:, a // 512, 0:b - a], lo, rhs_hi[:, k0 + k, a:b], start=False, stop=(k == kn - 1))
            return mm

        def wide_sum(src, n, first, last, w=2):
            for a, b in ((0, 512), (512, n)):
                mm = pe.matmul(pairs[w][:, a // 512, 0:b - a], ones, src[:, a:b], start=first, stop=last, skip_group_check=True)
            return mm

        for m in range(12):
            n = STREAM["mla_in"] + m // 2
            if m % 2 == 0:
                pe.wait_ge(split_full, n + 1)
            if m >= 2:
                pe.wait_ge(wide_free[m % 2], m // 2)
            mm = wide_project(0, 0, KT, m % 2, half_of(n), h2_hi, h2_lo, tile0=KT * (m % 2), ready=None if m else mh_ready)
            mm.then_inc(tile0_full if m % 2 == 0 else block_done, 1)
            if m == 3:
                for c in range(2):
                    pe.wait_ge(lat_sq, c + 1)
                    mm = wide_sum(lsq[:, c, :], TA, c == 0, c == 1)
                mm.then_inc(lat_sum, 1)
            if m == 5:
                pe.wait_ge(lat_root, 1)
                pe.wait_ge(lat_sq, 3)
                wide_sum(lsq[:, 0, :], TA, True, True).then_inc(lat_sum, 1)
                pe.wait_ge(kpe_copied, 1)
                pe.matmul(banks[6][64:96, :], sq_c[64:96, 5, 64:96], kf[0][64:96, 0:T], start=True, stop=True).then_inc(kpe_rot, 1)

        def take(p, e, name):
            w, frees, _ = use_of(p, e, name)
            pe.wait_ge(wide_free[w], frees)
            return w

        def head_q(p, e, slot, s):
            mm = wide_project(0, 0, 2, take(*slot, "q"), s, lat_hi, lat_lo, tile0=2 * e)
            mm.then_inc(block_done if e else wide_full, 1)

        def head_k(p, slot, s):
            wide_project(0, 2, 1, take(*slot, "k"), s, lat_hi, lat_lo, tile0=4).then_inc(wide_full, 1)

        def head_v(p, slot, s):
            w = take(*slot, "V")
            for tt in range(6):
                out = wide(w)[:, P * tt:P * tt + P]
                ts = slice(P * tt, P * tt + P)
                pe.matmul(out, lat_hi[:, 2, ts], w_hi[:, s, 5, :], start=True, stop=False)
                pe.matmul(out, lat_hi[:, 2, ts], w_lo[:, s, 5, :], start=False, stop=False)
                mm = pe.matmul(out, lat_lo[:, 2, ts], w_hi[:, s, 5, :], start=False, stop=True)
            mm.then_inc(wide_full, 1)

        def head_rotate(p, e, slot):
            w = take(*slot, "R")
            pe.wait_ge(pr_evac, 2 * p + (e + 1))
            pe.matmul(pairs[w][0:96, 0, :], sq_c[0:96, 5, 0:96], qf[0:96, 0:T], start=True, stop=True).then_inc(wide_full, 1)

        def head_top(p, e, slot, qt):
            w = take(*slot, f"M{qt}")
            if qt == 0:
                pe.wait_ge(head_high, 6 * p + (3 * e + 3))
            if qt < 4:
                q = q_hi[e][0:96, P * qt:P * qt + P]
                pe.matmul(pairs[w][:, 0, :], q, k_hi[e][0:96, 0:512], start=True, stop=True)
                mm = pe.matmul(pairs[w][:, 1, 0:256], q, k_hi[e][0:96, 512:TA], start=True, stop=True)
            else:
                for i in range(2):
                    mm = pe.matmul(pairs[w][:, i, 0:256], q_hi[e][0:96, T + P * i:T + P * i + P], k_hi[e][0:96, T:TA], start=True, stop=True)
            mm.then_inc(wide_full, 1)

        def head_row(p, e, slot):
            w = take(*slot, "top")
            pe.wait_ge(top_ready, 2 * p + (e + 1))
            for t in range(6):
                mm = pe.matmul(wide(w)[96:97, P * t:P * t + P], der[:, NM + t:NM + t + 1], ident, start=True, stop=True)
            mm.then_inc(wide_full, 1)

        def scores(p, e, j):
            w = take(p, e, f"S{j}")
            if j == 0:
                pe.wait_ge(head_low, 6 * p + (3 * e + 3))
                pe.wait_ge(top_row, 2 * p + (e + 1))
            ks = slice(P * j, P * j + P)
            for k, q, first, last in ((k_hi, q_hi, True, False), (k_hi, q_lo, False, False), (k_lo, q_hi, False, True)):
                mm = pe.matmul(pairs[w][:, 0, :], k[e][0:97, ks], q[e][0:97, 0:T], start=first, stop=last)
                if j >= 4:
                    mm = pe.matmul(pairs[w][:, 1, 0:C], k[e][0:97, ks], q[e][0:97, T:TA], start=first, stop=last)
            mm.then_inc(wide_full, 1)

        def values(p, e, j):
            if j == 0:
                pe.wait_ge(o_copied, 2 * p + (e + 1))
            pe.wait_ge(exp_low, 12 * p + (6 * e + j + 1))
            for v, x, first, last in ((V_hi, P_hi, True, False), (V_hi, P_lo, False, False), (V_lo, P_hi, False, True)):
                mm = pe.matmul(pairs[2 + e][:, 0, :], v[e][:, j, :], x[:, j % 3, 0:T], start=(j == 0 and first), stop=(j == 5 and last),
                               skip_group_check=True)
                if j >= 4:
                    mm = pe.matmul(pairs[2 + e][:, 1, 0:C], v[e][:, j, :], x[:, j % 3, T:TA], start=(j == 4 and first),
                                   stop=(j == 5 and last), skip_group_check=True)
            mm.then_inc(kt_done, 1)

        def slot(p, e, s):
            last = isinstance(p, int) and p == N_PAIRS - 1 and e == 1
            nxt = None if last else (p, 1) if e == 0 else (p + 1, 0)
            here = (p, e)
            if nxt:
                if nxt[1] == 0:
                    pe.wait_ge(split_full, p + (STREAM["mla"] + 2))
                head_q(*nxt, here, s)
            if nxt and nxt[1] == 0:
                head_k(nxt[0], here, s)
                head_rotate(*nxt, here)
                head_v(nxt[0], here, s)
            scores(p, e, 0)
            if nxt and nxt[1]:
                head_rotate(*nxt, here)
            scores(p, e, 1)
            for j in range(6):
                if j + 2 < 6:
                    scores(p, e, j + 2)
                values(p, e, j)
                if nxt and j < 5:
                    head_top(*nxt, here, j)
            if nxt:
                head_row(*nxt, here)

        pe.wait_ge(lat_ready, 3)
        pe.wait_ge(kpe_done, 1)
        before_loop = (0, None)
        pe.wait_ge(split_full, STREAM["mla"] + 1)
        head_q(0, 0, before_loop, half_of(STREAM["mla"]))
        head_k(0, before_loop, half_of(STREAM["mla"]))
        head_rotate(0, 0, before_loop)
        head_v(0, before_loop, half_of(STREAM["mla"]))
        for qt in range(5):
            head_top(0, 0, before_loop, qt)
        head_row(0, 0, before_loop)
        with pe.Fori(0, N_PAIRS // 2 - 1) as i:
            for u in range(2):
                for e in range(2):
                    slot(2 * i + u, e, half_of(STREAM["mla"] + u + e))
        for p in range(N_PAIRS - 2, N_PAIRS):
            for e in range(2):
                slot(p, e, half_of(STREAM["mla"] + p + e))

        def residual_product(name, before_uses, n_cols, layer, ready, ready_base):
            for m in range(KT):
                n = STREAM[name] + m // 2
                if m % 2 == 0:
                    pe.wait_ge(split_full, n + 1)
                pe.wait_ge(wide_free[m % 2], before_uses + m // 2)
                mm = wide_project(0, 0, KT, m % 2, half_of(n), h2_hi, h2_lo, n_cols=n_cols, tile0=KT * (m % 2),
                                  ready=None if m else ready, ready_base=ready_base)
                mm.then_inc(tile0_full if m % 2 == 0 else block_done, 1)
            pe.wait_ge(z_acc, KT * (layer + 1))
            wide_sum(zacc, n_cols, True, True).then_inc(z_sum, 1) if n_cols > 512 else \
                pe.matmul(banks[4][:, :], ones, zacc[:, 0:T], start=True, stop=True).then_inc(z_sum, 1)
            for k in range(KT):
                pe.wait_ge(z_sq, KT * layer + k + 1)
                if n_cols > 512:
                    for a, b in ((0, 512), (512, TA)):
                        mm = pe.matmul(pairs[3][:, a // 512, 0:b - a], ones, zsq[:, k % 2, a:b], start=(k == 0), stop=(k == KT - 1),
                                       skip_group_check=True)
                else:
                    mm = pe.matmul(banks[6][:, :], ones, zsq[:, k % 2, 0:T], start=(k == 0), stop=(k == KT - 1))
                mm.then_inc(z_sum, 1)

        residual_product("mla_out", N_MLA_USES - 4, TA, 0, ot_ready, 0)
        pe.wait_ge(lam_prod, 1)
        pe.matmul(banks[4][:, 0:2], ones[0:64, :], der[0:64, LAM:LAM + 2], start=True, stop=True).then_inc(lam_sum, 1)

        with pe.Fori(0, B_HEADS) as h:
            def take(i):
                pe.wait_ge(wide_free[i % 2], D_USES * h + (N_MLA_USES + i // 2))
                return i % 2

            A, B = half_of(STREAM["diff"]), half_of(STREAM["diff"] + 1)
            pe.wait_ge(split_full, 2 * h + (STREAM["diff"] + 1))
            wide_project(0, 0, KT, take(0), A, h2_hi, h2_lo, n_cols=T, ready=mh_ready, ready_base=KT).then_inc(wide_full, 1)
            wide_project(0, 0, KT, take(1), A, h2_hi, h2_lo, tile0=KT).then_inc(block_done, 1)
            take(2)
            pe.wait_ge(pr_evac, D_EVAC * h + (N_MLA_EVAC + 2))
            pe.matmul(pairs[0][:, 0, :], sq_c[:, 6, :], dq[:, :], start=True, stop=True)
            pe.matmul(pairs[0][:, 1, :], sq_c[:, 6, :], dk[:, 0:T], start=True, stop=True).then_inc(wide_full, 1)
            pe.wait_ge(split_full, 2 * h + (STREAM["diff"] + 2))
            wide_project(0, 0, KT, take(3), B, h2_hi, h2_lo).then_inc(wide_full, 1)
            wide_project(0, 0, KT, take(4), B, h2_hi, h2_lo, n_cols=T, tile0=KT).then_inc(block_done, 1)
            take(5)
            pe.wait_ge(pr_evac, D_EVAC * h + (N_MLA_EVAC + 3))
            for kt in range(6):
                mm = pe.transpose(wide(1)[:, P * kt:P * kt + P], dv[:, P * kt:P * kt + P], ident)
            mm.then_inc(wide_full, 1)

            def scores(v):
                qt, m = v // 2, v % 2
                if v == 0:
                    pe.wait_ge(qk_high, 2 * h + (3 + 2))
                    pe.wait_ge(qk_low, h + (3 + 1))
                w = take(6 + v)
                rows, cols = slice(64 * m, 64 * m + 64), slice(P * qt, P * qt + P)
                for q, k, last in ((QQ[m][:, cols], KK[m][:, :], False), (QQ[m][rows, cols], KL[rows, :], True)):
                    pe.matmul(pairs[w][:, 0, :], q, k[:, 0:512], start=not last, stop=last)
                    mm = pe.matmul(pairs[w][:, 1, 0:256], q, k[:, 512:TA], start=not last, stop=last)
                mm.then_inc(wide_full, 1)

            def turn(v):
                pe.wait_ge(p_full, D_UNITS * h + (AFTER_MLA["p"] + v + 1))
                for kt in range(6):
                    mm = pe.transpose(banks[4 + kt // 3][:, P * (kt % 3):P * (kt % 3) + P], dP[v % 2][:, P * kt:P * kt + P], ident)
                    if kt % 3 == 2:
                        mm.then_inc([ta_full, tb_full][kt // 3], 1)

            def values(v):
                pe.wait_ge(eva_done, D_UNITS * h + (AFTER_MLA["eva"] + v + 1))
                pe.wait_ge(evb_done, D_UNITS * h + (AFTER_MLA["evb"] + v + 1))
                pe.wait_ge(o_done, D_UNITS * h + (AFTER_MLA["o"] + v - 1))
                if v == 0:
                    pe.wait_ge(pr_evac, D_EVAC * h + (N_MLA_EVAC + 5))
                for kt in range(6):
                    mm = pe.matmul(banks[6 + v % 2][:, 0:P], dPT[:, kt, :], dV[:, kt, :], start=(kt == 0), stop=(kt == 5))
                mm.then_inc(pv_done, 1)

            scores(0)
            for v in range(8):
                if v + 1 < 8:
                    scores(v + 1)
                if v:
                    values(v - 1)
                turn(v)
            values(7)

        pe.wait_ge(o_scaled, 4)
        for h in range(B_HEADS):
            pe.wait_ge(wide_free[h % 2], N_MLA_USES + D_USES * B_HEADS + h // 2)
            for qt in range(4):
                mm = pe.transpose(wide(h % 2)[:, P * qt:P * qt + P], O_tok[:, qt, P * h:P * h + P], ident)
            mm.then_inc(wide_full, 1)
        residual_product("diff_out", N_MLA_USES + D_USES * B_HEADS + KT // 2, T, 1, og_ready, 2 * KT)

    @block.scalar
    def _(act):
        chain = Chain(act, act_step)
        for k in range(KT):
            act.wait_ge(s_x[k // 4], 16)
            if k >= 2:
                act.wait_ge(sq_free, k - 1)
            act.activation(sq[:, k % 2, :], xT[:, k, :], ACT.Square).then_inc(sq_full, 1)
        act.wait_ge(s_const, 96)
        act.activation(der[:, SILU_C:SILU_C + 16], col("c", 0, 16), ACT.Silu).then_inc(silu_c, 1)
        act.wait_ge(sq_free, KT)
        act.wait_ge(prep_done, 2)
        act.activation(rstd[:, :], banks[6][:, :], ACT.Sqrt, scale=1.0 / D, bias=der[:, 127:128]).then_inc(sqrt_done, 1)
        for k in range(KT):
            act.wait_ge(htmp_full, k + 1)
            act.activation(h1_hi[:, k, :], htmp[:, k % 2, :], ACT.Copy).then_inc(h_hi_full, 1)
        with act.Fori(0, 2) as i:
            for s in range(2):
                act.wait_ge(block_done, 2 * i + (s + 1))
                act.wait_ge(glu_s_free, 2 * i + (s + 1))
                act.activation(glu_s[:, s, :], banks[2 * s + 1][:, :], ACT.Sigmoid).then_inc(glu_s_full, 1)

        def q_tile(j, b, n):
            act.wait_ge(tile0_full if b % 2 == 0 else block_done, n + 1)
            act.activation(Q[:, j, :], banks[b][:, :], ACT.Copy, scale=der[:, bass.ds(j + OMU, 1)]).then_inc(q_copied, 1)

        with act.Fori(0, 3) as i:
            for s in range(4):
                q_tile(4 * i + s, s, 2 * i + (4 + s // 2))
        for s in range(2):
            q_tile(12 + s, s, N_IN - 1)
        act.wait_ge(q_mixed, 14)
        act.activation(Q[0:32, 12, :], Q[0:32, 12, :], ACT.Tanh).then_inc(lora_in, 1)
        act.activation(Q[0:96, 13, :], Q[0:96, 13, :], ACT.Sigmoid).then_inc(lora_in, 1)
        for c in range(CT):
            for j in range(3):
                m = 3 * c + j
                act.wait_ge(lora_full, m + 1)
                if j == 2:
                    act.activation(gg[:, c, :], banks[m % 6][:, :], ACT.Copy).then_inc(lora_evac, 1)
                else:
                    act.activation((lw, aB)[j][:, c, :], banks[m % 6][:, :], ACT.Sigmoid,
                                   bias=col(("w0", "a0")[j], c)).then_inc(lora_evac, 1)
        for c in range(CT):
            act.wait_ge(kk_raw, c + 1)
            if c >= 2:
                act.wait_ge(kk_sum, c - 1)
            act.activation(sqk[:, c % 2, :], kk[:, c, :], ACT.Square).then_inc(kk_sq, 1)
        act.wait_ge(chunk_end, 1)
        act.activation(der[:, ECT:ECT + 32], der[:, CT_END:CT_END + 32], ACT.Exp).then_inc(exps_done, 1)
        act.wait_ge(exps_in, 1)
        act.activation(e1[:, :, :], cc[:, :, :], ACT.Exp, scale=-1.0).then_inc(exps_done, 1)
        act.activation(eR[:, :, :], cc[:, :, :], ACT.Exp).then_inc(exps_done, 1)
        act.wait_ge(exps_in, 2)
        act.activation(eA[:, :, :], eA[:, :, :], ACT.Exp).then_inc(exps_done, 1)
        for c in range(CT):
            act.wait_ge(kk_max, c + 1)
            act.activation(knt[:, c % 2, :], knt[:, c % 2, :], ACT.Sqrt).then_inc(kk_root, 1)
        for n in range(16):
            act.wait_ge(tok_full, n + 1)
            act.activation((A_tok, B_tok, K_tok, V_tok)[n // 4][:, n % 4, :], banks[n % 4][:, :], ACT.Copy).then_inc(tok_done, 1)
        ident4 = ident.unsqueeze(1).broadcast_to([P, 4, P])

        def unit(c, e, step):
            X = banks[4 * e:4 * e + 4]
            rows, h = slice(64 * e, 64 * e + 64), 2 * c + e
            if step in ("DI", "DIT"):
                if c:
                    act.wait_ge(u_pe[e], pe_at(c - 1, "U"))
                else:
                    act.wait_ge(ada_done, 1)
                act.activation((Di if step == "DI" else DiT)[e][:, :, :], ident4, ACT.Copy).then_inc(u_act[e], 1)
                return
            act.wait_ge(u_pe[e], pe_at(c, step))
            if step == "LT":
                out, src = Lt[e][:, :, :], X[1][:, :]
            elif step == "MV":
                out, src = MV[e][:, :, :], X[3][:, 0:256]
            elif step == "Y0":
                out, src = ky[rows, c, :], X[3][rows, :]
            elif step[0] == "G":
                out, src = Gt[e][:, :, :], X[0][:, :]
            elif step == "W":
                out, src = eA[rows, c, :], X[0][rows, :]
            else:
                out, src = U[:, :, 64 * h:64 * h + 64], X[1][:, 0:256]
            if len(out.shape) == 3:
                src = src.rearrange("p (a b) -> p a b", a=4)
            act.activation(out, src, ACT.Copy).then_inc(u_act[e], 1)

        for c in range(CT):
            for step in ACT_STEPS:
                for e in range(2):
                    unit(c, e, step)
        for c in range(CT):
            act.wait_ge(cln_centred, c + 1)
            act.activation(csq[:, c, :], cacc[:, c, :], ACT.Square).then_inc(cln_sq, 1)
        act.wait_ge(cln_sum, 1 + CT)
        act.activation(cstd[:, :], banks[5][:, :], ACT.Sqrt, scale=1.0 / HALF, bias=der[:, 126:127]).then_inc(cln_root, 1)
        for c in range(CT):
            act.wait_ge(cln_normed, c + 1)
            act.activation(cacc[:, c, :], cacc[:, c, :], ACT.Silu, scale=col("cln_g", c), bias=col("cln_b", c)).then_inc(conv_out, 1)
        for c in range(CT):
            act.wait_ge(gn_centred, c + 1)
            if c >= 2:
                act.wait_ge(gn_var, c - 1)
            act.activation(msq[:, c % 2, :], ky[:, c, :], ACT.Square).then_inc(gn_sq, 1)

        def high(k, src, done):
            act.activation(h1_hi[:, k, :], src, ACT.Copy).then_inc(done, 1)

        for c in range(CT):
            act.wait_ge(gn_var, c + 1)
            act.activation(mrs[:, c % 2, :], banks[4 + c][:, :], ACT.Sqrt, scale=1.0 / 64, bias=der[:, 125:126]).then_inc(gn_root, 1)
            if c == 0:
                act.wait_ge(y_done, NCH)
                act.dma_start(xT[:, :, :], x_t).then_inc(s_x[0], 16)
            high(CT + c, cacc[:, c, :], mix_hi_full)
            act.wait_ge(gn_normed, c + 1)
            act.activation(ky[:, c, :], ky[:, c, :], ACT.Identity, scale=col("lnx_g", c), bias=col("lnx_b", c)).then_inc(gn_scaled, 1)
        for c in range(CT):
            act.wait_ge(mix_full, c + 1)
            high(c, ky[:, c, :], mix_hi_full)

        def copy_and_square(m, bank, out, wait, free):
            wait()
            act.activation(out, banks[bank][:, :], ACT.Copy).then_inc(out_copied, 1)
            if m >= 2:
                act.wait_ge(out_summed, m - 1)
            act.activation(nt[:, m % 2, :], banks[bank][:, :], ACT.Square).then_inc(out_sq, 1)
            act.wait_ge(out_sq, m + 1)
            act.sem_inc(free, 1)

        for m in range(KT):
            n = STREAM["out"] + m // 2
            b = 2 * half_of(n) + m % 2
            copy_and_square(m, b, mixo[:, m, :], lambda: act.wait_ge(tile0_full if m % 2 == 0 else block_done, n + 1), proj_free[b])

        act.wait_ge(post_sum, 1)
        act.activation(nr[:, :], banks[6][:, :], ACT.Sqrt, scale=1.0 / D, bias=der[:, 127:128]).then_inc(post_root, 1)
        for k in range(KT):
            act.wait_ge(x_done, k + 1)
            if k >= 2:
                act.wait_ge(pre_sq_read, k - 1)
            act.activation(nt[:, k % 2, :], xT[:, k, :], ACT.Square).then_inc(pre_sq, 1)
        act.wait_ge(pre_sq_read, KT)
        act.activation(nr[:, :], banks[7][:, :], ACT.Sqrt, scale=1.0 / D, bias=der[:, 127:128]).then_inc(pre_root, 1)
        for k in range(KT):
            act.wait_ge(nh_full, k + 1)
            act.activation(h1_hi[:, k, :], nh[:, k % 2, :], ACT.Copy).then_inc(nh_hi, 1)

        for _ in range(4):
            act.sem_inc(down_free, 1)
        with act.Fori(0, N_UP // 2) as i:
            for u in range(2):
                n0 = STREAM["up"] + u
                s = half_of(n0)
                j = 2 * i + u
                for g, buf in enumerate((yg, yu)):
                    act.wait_ge(tile0_full if g == 0 else block_done, 2 * i + (n0 + 1))
                    act.activation(buf[:, s, :], banks[2 * s + g][:, :], ACT.Identity,
                                   scale=prm[:, bass.ds(6 * j + (PCOL["fconv_w"] + 3 * g + 2), 1)],
                                   bias=prm[:, bass.ds(2 * j + (PCOL["fconv_b"] + g), 1)]).then_inc(up_first, 1)
                act.wait_ge(up_conv, 4 * i + (2 * u + 1))
                act.activation(yg[:, s, :], yg[:, s, :], ACT.Gelu_apprx_tanh).then_inc(up_gelu, 1)
                act.wait_ge(up_prod, j + 1)
                act.activation(act_hi[:, j, :], yg[:, s, :], ACT.Copy).then_inc(up_hi, 1)

        for q in range(4):
            for j in range(2):
                m = KT + 2 * q + j
                n = STREAM["down"] + 3 * q + 3
                copy_and_square(m, 4 + (2 * q + j) % 4, fout[:, 2 * q + j, :],
                                lambda: act.wait_ge(down_full, q + 1) if j == 0 else act.wait_ge(block_done, n), down_free)
        act.wait_ge(post_sum, 2)
        act.activation(nr[:, :], banks[6][:, :], ACT.Sqrt, scale=1.0 / D, bias=der[:, 127:128]).then_inc(post_root, 1)
        act.wait_ge(block_done, STREAM["mla_in"])
        act.dma_start(ctxT[:, :, :], ctx_t).then_inc(s_ctx, 16)
        act.wait_ge(x_done, KT + 1)
        act.dma_start(rope[:, :, :], ropes[0, :, :, :]).then_inc(s_rope, 16)
        act.wait_ge(ada_one, 1)
        for k in range(KT):
            act.wait_ge(x_done, KT + k + 1)
            if k >= 2:
                act.wait_ge(mh_ready, k - 1)
            act.activation(mh[:, k % 2, 0:T], xT[:, k, :], ACT.Identity, scale=ada[:, 0, 1, k, 0:1],
                           bias=ada[:, 0, 0, k, 0:1]).then_inc(mod_done, 1)
            act.wait_ge(mod_done, CT + k + 1)
            act.wait_ge(mh_full, k + 1)
            act.activation(h2_hi[:, k, :], mh[:, k % 2, :], ACT.Copy).then_inc(mh_hi, 1)
        T0 = STREAM["down"] + 1
        freed = [0, 0]
        for m in range(12):
            w = m % 2
            act.wait_ge(*((tile0_full, T0 + m // 2) if w == 0 else (block_done, STREAM["mla_in"] + m // 2 + 1)))
            if m < 3:
                act.activation(lat[:, m, :], wide(w), ACT.Copy)
                if m == 2:
                    act.wait_ge(lat_sum, 1)
                act.activation(lsq[:, m % 2, :], wide(w), ACT.Square).then_inc(lat_sq, 1)
                act.wait_ge(lat_sq, m + 1)
                act.sem_inc(wide_free[w], 1)
                if m == 2:
                    act.activation(lrs[:, :], wide(2), ACT.Sqrt, scale=1.0 / 256, bias=der[:, 127:128]).then_inc(lat_root, 1)
            elif m == 3:
                act.activation(kf[0][64:96, :], wide(w)[64:96, :], ACT.Copy).then_inc(kpe_copied, 1)
                act.wait_ge(kpe_copied, 1)
                act.sem_inc(wide_free[w], 1)
            else:
                act.activation(gate_s[:, m - 4, :], wide(w), ACT.Silu).then_inc(wide_free[w], 1)
            if m == 5:
                act.wait_ge(lat_normed, 2)
                act.wait_ge(lat_sum, 2)
                act.activation(lrs[:, :], wide(2), ACT.Sqrt, scale=1.0 / 128, bias=der[:, 127:128]).then_inc(lat_root, 1)
            if m == 8:
                for c in range(2):
                    act.activation(lat_hi[:, c, :], lat[:, c, :], ACT.Copy).then_inc(lat_high, 1)
            if m == 11:
                act.wait_ge(lat_normed, 3)
                act.activation(lat_hi[:, 2, :], lat[:, 2, :], ACT.Copy).then_inc(lat_high, 1)

        def full(p, e, name):
            w, _, n = use_of(p, e, name)
            act.wait_ge(wide_full, n)
            return w

        def first_copies(p, e, here):
            w, _, _ = use_of(*here, "q")
            if here[1] is not None:
                act.wait_ge(head_low, 6 * p + 3 * e)
            if e:
                act.wait_ge(block_done, p + (STREAM["mla"] + 1))
            else:
                full(*here, "q")
            act.activation(qf[0:96, :], wide(w)[0:96, :], ACT.Copy).then_inc(pr_evac, 1)
            act.wait_ge(pr_evac, 2 * p + (e + 1))
            act.sem_inc(wide_free[w], 1)

        def high_k(p, e):
            act.wait_ge(kv_copied, 2 * p + 1)
            act.activation(k_hi[e][0:64, :], kf[e][0:64, :], ACT.Copy).then_inc(head_high, 1)

        def high_v(p, e):
            act.wait_ge(kv_copied, 2 * p + 2)
            act.activation(V_hi[e][:, :, 64 * e:64 * e + 64], Vf[:, :, 64 * e:64 * e + 64], ACT.Copy).then_inc(head_high, 1)

        def high_q(p, e):
            act.wait_ge(rope_done, 2 * p + (e + 1))
            act.activation(q_hi[e][0:96, :], qf[0:96, :], ACT.Copy).then_inc(head_high, 1)

        def top_copy(p, e, here):
            w = full(*here, "top")
            act.activation(q_hi[e][96:97, :], wide(w)[96:97, :], ACT.Copy).then_inc(top_row, 1)
            act.wait_ge(top_row, 2 * p + (e + 1))
            act.sem_inc(wide_free[w], 1)

        def weights_of(p, e, j):
            cols = T if j < 4 else TA
            if j >= 3:
                act.wait_ge(exp_low, 12 * p + (6 * e + j - 2))
            w = full(p, e, f"S{j}")
            act.activation(Pf[:, j % 3, 0:cols], wide(w, cols), ACT.Exp, scale=A_SCALE).then_inc(exp_full, 1)
            act.wait_ge(exp_full, 12 * p + (6 * e + j + 1))
            act.sem_inc(wide_free[w], 1)
            if j >= 3:
                act.wait_ge(kt_done, 12 * p + (6 * e + j - 2))
            act.activation(P_hi[:, j % 3, 0:cols], Pf[:, j % 3, 0:cols], ACT.Copy).then_inc(exp_high, 1)

        def copy_out(p, e):
            act.wait_ge(kt_done, 12 * p + (6 * e + 6))
            if e == 0:
                act.wait_ge(pair_out, p + 1)
            mine, ones_at = slice(64 * e, 64 * e + 64), slice(64 - 64 * e, 128 - 64 * e)
            act.activation(Of[mine, :], wide(2 + e)[mine, :], ACT.Copy)
            act.activation(Ls[mine, :], wide(2 + e)[ones_at, :], ACT.Copy).then_inc(o_copied, 1)

        def head_slot(p, e, done=True):
            last = isinstance(p, int) and p == N_PAIRS - 1 and e == 1
            nxt = None if last else (p, 1) if e == 0 else (p + 1, 0)
            if e == 0 and done:
                copy_out(p - 1, 1)
            if nxt:
                first_copies(*nxt, (p, e))
                high_k(*nxt)
                if nxt[1]:
                    high_v(*nxt)
            for j in range(6):
                if nxt and not nxt[1] and j == 1:
                    high_v(*nxt)
                weights_of(p, e, j)
                if nxt and j == 1:
                    high_q(*nxt)
            if e:
                copy_out(p, 0)
            if nxt:
                top_copy(*nxt, (p, e))
        act.sem_inc(o_copied, 2)
        act.wait_ge(kpe_done, 1)
        for e in range(2):
            act.activation(k_hi[e][64:96, :], kf[0][64:96, :], ACT.Copy).then_inc(lat_dead, 1)
        first_copies(0, 0, (0, None))
        high_k(0, 0)
        high_v(0, 0)
        high_q(0, 0)
        top_copy(0, 0, (0, None))
        for e in range(2):
            head_slot(0, e, done=False)
        with act.Fori(1, N_PAIRS - 1) as p:
            for e in range(2):
                head_slot(p, e)
        for e in range(2):
            head_slot(N_PAIRS - 1, e)
        copy_out(N_PAIRS - 1, 1)
        for k in range(KT):
            act.wait_ge(pair_out, k + 2)
            act.activation(h2_hi[:, k, :], gate_s[:, k, :], ACT.Copy).then_inc(ot_hi, 1)

        def norm_out(layer, name, n_cols, t0):
            xg = ada[:, layer, 2, :, :]
            for m in range(KT):
                w = m % 2
                act.wait_ge(*((tile0_full, t0 + m // 2) if w == 0 else (block_done, STREAM[name] + m // 2 + 1)))
                ins = act.activation(z_of(layer)[:, m, 0:T], wide(w, T), ACT.Copy, scale=xg[:, m, 0:1])
                if n_cols > T:
                    ins = act.activation(z_of(layer)[:, m, T:TA], wide(w)[:, T:TA], ACT.Copy, scale=xg[:, m, 1:2])
                ins.then_inc(z_gated, 1)
                act.wait_ge(z_gated, KT * layer + m + 1)
                act.sem_inc(wide_free[w], 1)
            for k in range(KT):
                act.wait_ge(z_centred, KT * layer + k + 1)
                if k >= 2:
                    act.wait_ge(z_sum, 9 * layer + k)
                act.activation(zsq[:, k % 2, 0:n_cols], z_of(layer)[:, k, 0:n_cols], ACT.Square).then_inc(z_sq, 1)
            act.wait_ge(z_sum, 9 * layer + 9)
            act.activation(zrs[:, 0:n_cols], wide(3, n_cols), ACT.Sqrt, scale=1.0 / D, bias=der[:, 127:128]).then_inc(z_root, 1)
            for k in range(KT):
                act.wait_ge(z_normed, KT * layer + k + 1)
                act.activation(z_of(layer)[:, k, 0:n_cols], z_of(layer)[:, k, 0:n_cols], ACT.Identity, scale=col("ln_g", KT * layer + k),
                               bias=col("ln_b", KT * layer + k)).then_inc(z_out, 1)

        act.wait_ge(ot_ready, A_HEADS // 2)
        act.dma_start(ctx2[:, :, :], ctx_t).then_inc(s_ctx, 16)
        norm_out(0, "mla_out", TA, T0 + N_MLA_IN)
        act.dma_start(rope[:, :, :], ropes[1, :, :, :]).then_inc(s_rope, 16)
        for k in range(KT):
            act.wait_ge(z_out, k + 1)
            if k >= 2:
                act.wait_ge(mh_ready, KT + k - 1)
            act.activation(zh[:, k % 2, 0:T], z[:, k, 0:T], ACT.Identity, scale=ada[:, 1, 1, k, 0:1],
                           bias=ada[:, 1, 0, k, 0:1]).then_inc(mod_done, 1)
            act.wait_ge(mod_done, CT + KT + k + 1)
            act.wait_ge(mh_full, KT + k + 1)
            act.activation(h2_hi[:, k, :], zh[:, k % 2, :], ACT.Copy).then_inc(mh_hi, 1)
        act.wait_ge(lam_sum, 1)
        act.activation(der[:, LAM + 2:LAM + 4], banks[4][:, 0:2], ACT.Exp).then_inc(lam_exp, 1)

        with act.Fori(0, B_HEADS) as h:
            def evacuate(i, w, dst, src):
                act.activation(dst, src, ACT.Copy).then_inc(pr_evac, 1)
                act.wait_ge(pr_evac, D_EVAC * h + (N_MLA_EVAC + i + 1))
                act.sem_inc(wide_free[w], 1)

            act.wait_ge(wide_full, D_FULL * h + (N_MLA_FULL + 1))
            evacuate(0, 0, dq[:, :], wide(0, T))
            act.wait_ge(block_done, 2 * h + (STREAM["diff"] + 1))
            evacuate(1, 1, dk[:, :], wide(1))
            act.wait_ge(rope_done, h + (A_HEADS + 1))
            low_rows, high_rows = slice(0, 64), slice(64, 128)
            act.activation(QQ[0][low_rows, :], dq[low_rows, :], ACT.Copy)
            act.activation(QQ[1][high_rows, :], dq[high_rows, :], ACT.Copy)
            act.activation(KK[0][low_rows, :], dk[low_rows, :], ACT.Copy)
            act.activation(KK[1][high_rows, :], dk[high_rows, :], ACT.Copy).then_inc(qk_high, 1)
            act.activation(KK[0][high_rows, :], dk[low_rows, :], ACT.Copy)
            act.activation(KK[1][low_rows, :], dk[high_rows, :], ACT.Copy).then_inc(qk_high, 1)
            act.wait_ge(wide_full, D_FULL * h + (N_MLA_FULL + 3))
            evacuate(2, 1, dv[:, :], wide(1))
            act.wait_ge(block_done, 2 * h + (STREAM["diff"] + 2))
            evacuate(3, 0, gate2[:, h, :], wide(0, T))
            act.wait_ge(wide_full, D_FULL * h + (N_MLA_FULL + 4))
            evacuate(4, 1, dV[:, :, :].rearrange("p a b -> p (a b)"), wide(1))

            def square(v):
                act.wait_ge(o_done, D_UNITS * h + (AFTER_MLA["o"] + v + 1))
                act.activation(o_junk[:, (v // 2) % 2, :], O_tok[:, v // 2, bass.ds(P * h, P)], ACT.Square,
                               accum_out=o_ss[:, bass.ds(4 * h + v // 2, 1)]).then_inc(o_sq, 1)

            for v in range(8):
                act.wait_ge(nm_ready, D_UNITS * h + (AFTER_MLA["nm"] + v + 1))
                act.activation(dP[v % 2][:, :], wide(v % 2), ACT.Exp, scale=B_SCALE, bias=der[:, NM + v:NM + v + 1],
                               accum_out=der[:, RS + v:RS + v + 1]).then_inc(p_full, 1)
                act.wait_ge(p_full, D_UNITS * h + (AFTER_MLA["p"] + v + 1))
                act.sem_inc(wide_free[v % 2], 1)
                act.wait_ge(tb_full, D_UNITS * h + (AFTER_MLA["tb"] + v + 1))
                if v:
                    act.wait_ge(pv_done, D_UNITS * h + (AFTER_MLA["pv"] + v))
                act.activation(dPT[:, 3:6, :].rearrange("p a b -> p (a b)"), banks[5][:, 0:3 * P], ACT.Copy).then_inc(evb_done, 1)
                if v % 2 and v > 1:
                    square(v - 2)
            square(7)

        act.wait_ge(o_sq, 4 * B_HEADS)
        act.activation(o_rs[:, :], o_ss[:, :], ACT.Sqrt, scale=1.0 / P, bias=der[:, 127:128]).then_inc(o_root, 1)
        for m in range(KT):
            act.activation(gate2[:, m, :], gate2[:, m, :], ACT.Silu).then_inc(gate_done, 1)
        for h in range(B_HEADS):
            act.wait_ge(og_full, 2 * KT + h + 1)
            act.activation(h2_hi[:, h, 0:T], og[:, h % 2, :], ACT.Copy).then_inc(og_hi, 1)
        norm_out(1, "diff_out", T, T0 + N_MLA_IN + N_MLA_OUT)

    @block.vector
    def _(dve):
        chain = Chain(dve, dve_step)
        for b in range(4):
            dve.sem_inc(proj_free[b], 1)
        dve.sem_inc(glu_s_free, 2)
        dve.memset(der[:, 127:128], RMS_EPS)
        dve.memset(der[:, 126:127], LN_EPS)
        dve.memset(der[:, 125:126], GN_EPS).then_inc(prep_done, 1)
        dve.wait_ge(s_const, 96)
        chain.link(dve.tensor_copy(lvl[:, :, :], lvl_f[:, :, :]))
        dve.tensor_scalar(der[:, OMU:OMU + 14], col("mu", 0, 14), -1.0, 1.0, ALU.mult, ALU.add)
        chain.link(dve.tensor_scalar(der[:, OKA:OKA + 4], col("k_a", 0, 4), -1.0, 1.0, ALU.mult, ALU.add))
        dve.sem_inc(prep_done, 1)
        dve.wait_ge(sqrt_done, 1)
        chain.link(dve.reciprocal(rstd[:, :], rstd[:, :]))
        for k in range(KT):
            if k >= 2:
                dve.wait_ge(h_hi_full, k - 1)
            dve.scalar_tensor_tensor(out=htmp[:, k % 2, :], in0=xT[:, k, :], scalar=col("pre_mix", k), in1=rstd[:, :],
                                     op0=ALU.mult, op1=ALU.mult).then_inc(htmp_full, 1)
            if k:
                dve.wait_ge(h_hi_full, k)
                dve.tensor_tensor(h1_lo[:, k - 1, :], htmp[:, (k - 1) % 2, :], h1_hi[:, k - 1, :], ALU.subtract).then_inc(h_ready, 1)
                dve.wait_ge(h_ready, k)
        dve.wait_ge(h_hi_full, KT)
        dve.tensor_tensor(h1_lo[:, KT - 1, :], htmp[:, (KT - 1) % 2, :], h1_hi[:, KT - 1, :], ALU.subtract).then_inc(h_ready, 1)
        dve.wait_ge(one_done, 2)
        with chain.loop(2, 2) as i:
            for s in range(2):
                dve.wait_ge(glu_s_full, 2 * i + s + 1)
                chain.link(dve.tensor_tensor(cpad[:, 2 * i + s, TAPS - 1:], banks[2 * s][:, :], glu_s[:, s, :], ALU.mult))
                dve.sem_inc(proj_free[2 * s], 1)
                dve.sem_inc(proj_free[2 * s + 1], 1)
                dve.sem_inc(glu_s_free, 1)

        conv = Chain(dve, conv_done)
        for j in range(CT):
            conv.mark(dve.tensor_scalar(cacc[:, j, :], cpad[:, j, 0:T], col("cconv_w", TAPS * j), col("cconv_b", j),
                                        ALU.mult, ALU.add))

        def tap(t):
            for j in range(CT):
                conv.wait(conv.n - (CT - 1))
                conv.mark(dve.scalar_tensor_tensor(out=cacc[:, j, :], in0=cpad[:, j, bass.ds(t, T)],
                                                   scalar=prm[:, bass.ds(t + (PCOL["cconv_w"] + TAPS * j), 1)],
                                                   in1=cacc[:, j, :], op0=ALU.mult, op1=ALU.add))

        def q_tile(j, b, copied):
            dve.wait_ge(q_copied, copied)
            dve.scalar_tensor_tensor(out=Q[:, j, 1:T], in0=banks[b][:, 0:T - 1], scalar=prm[:, bass.ds(j + PCOL["mu"], 1)],
                                     in1=Q[:, j, 1:T], op0=ALU.mult, op1=ALU.add).then_inc(q_mixed, 1)
            dve.wait_ge(q_mixed, copied)
            dve.sem_inc(proj_free[b], 1)

        with conv.loop(3, 8 * CT) as i:
            for s in range(2):
                for j in range(2):
                    q_tile(4 * i + 2 * s + j, 2 * s + j, 4 * i + (2 * s + j + 1))
                    for u in range(2):
                        tap(8 * i + (4 * s + 2 * j + u + 1))
        for j in range(2):
            q_tile(12 + j, j, 13 + j)
        for t in range(25, TAPS):
            tap(t)
        chain.mark(dve.memset(ada_row[:, :, :], 0.0))
        for c in range(CT):
            dve.wait_ge(lora_evac, 3 * c + 1)
            chain.link(dve.tensor_scalar(lw[:, c, :], lw[:, c, :], -math.exp(-0.5), None, ALU.mult))
            chain.mark(dve.tensor_tensor_scan(cc[:, c, :], scan_m[:, :], lw[:, c, :], 0.0, ALU.mult, ALU.add))
            dve.tensor_scalar(kk[:, c, :], ky[:, c, :], col("k_k", c), None, ALU.mult).then_inc(kk_raw, 1)
        chain.wait()
        by_chunk = cc[:, :, :].rearrange("p c (n t) -> p (c n) t", t=CHUNK)
        chain.link(dve.tensor_copy(der[:, CT_END:CT_END + 32], by_chunk[:, :, CHUNK - 1]))
        dve.sem_inc(chunk_end, 1)
        chain.link(dve.tensor_tensor(by_chunk, by_chunk, der[:, CT_END:CT_END + 32].unsqueeze(2).broadcast_to([P, 32, CHUNK]),
                                     ALU.subtract))
        dve.sem_inc(exps_in, 1)
        dve.tensor_tensor(eA[:, :, :], cc[:, :, :], lw[:, :, :], ALU.subtract).then_inc(exps_in, 1)

        def ada_columns(g):
            dve.wait_ge(ada_rows, g + 1)
            chain.link(dve.tensor_copy(ada_row[0:2, :, :], banks[6 + g % 2][0:2, :].rearrange("p (a n) -> p a n", a=2)))
            dve.sem_inc(ada_rows_free, 1)
            dve.sem_inc(ada_free[1], 1)
            row = ada_row[:, :, :].rearrange("p a (t q c) -> p (a t) q c", t=2, q=4)
            for q in range(4):
                last = dve.transpose(ada_col[32 * q:32 * q + 32, :, :], row[:, :, q, :])
            chain.link(last)
            n = slice(8 * g, 8 * g + 8)
            flat = ada[:, :, :, :, :].rearrange("p l s k v -> p (l s k v)")
            chain.link(dve.tensor_tensor(flat[:, n].rearrange("p (t v) -> p t v", v=2), ada_col[:, :, 0:2],
                                         col("ada_b", 8 * g, 8).rearrange("p (t v) -> p t v", v=2), ALU.add))

        for c in range(CT):
            dve.wait_ge(kk_sum, c + 1)
            if c >= 2:
                chain.wait()
            dve.tensor_scalar(knt[:, c % 2, :], banks[c][:, :], 1e-24, None, ALU.max).then_inc(kk_max, 1)
            ada_columns(c)
            dve.wait_ge(kk_root, c + 1)
            chain.link(dve.reciprocal(knt[:, c % 2, :], knt[:, c % 2, :]))
            chain.link(dve.tensor_tensor(kk[:, c, :], kk[:, c, :], knt[:, c % 2, :], ALU.mult))
        for c in range(CT):
            chain.link(dve.tensor_scalar(kft[:, c % 2, :], aB[:, c, :], col("k_a", c), der[:, OKA + c:OKA + c + 1], ALU.mult, ALU.add))
            chain.link(dve.tensor_tensor(ky[:, c, :], ky[:, c, :], kft[:, c % 2, :], ALU.mult))
        dve.wait_ge(exps_done, 3)
        chain.link(dve.tensor_tensor(eR[:, :, :], eR[:, :, :], rr, ALU.mult))
        for c in range(CT):
            dve.scalar_tensor_tensor(out=rr[:, c, :], in0=rr[:, c, :], scalar=col("r_k", c), in1=ky[:, c, :],
                                     op0=ALU.mult, op1=ALU.mult).then_inc(bonus_in, 1)
        for g in range(4, 8):
            ada_columns(g)
        dve.wait_ge(exps_done, 4)
        dve.scalar_tensor_tensor(out=eA[:, :, :].rearrange("p c t -> p (c t)"), in0=kk[:, :, :].rearrange("p c t -> p (c t)"), scalar=-1.0,
                                 in1=eA[:, :, :].rearrange("p c t -> p (c t)"), op0=ALU.mult, op1=ALU.mult).then_inc(abkv_ready, 1)
        chain.link(dve.tensor_tensor(aB[:, :, :], aB[:, :, :], kk[:, :, :], ALU.mult))
        dve.tensor_tensor(aB[:, :, :], aB[:, :, :], e1[:, :, :], ALU.mult).then_inc(abkv_ready, 1)
        dve.wait_ge(bonus_in, CT)
        dve.tensor_tensor(ky, ky, e1[:, :, :], ALU.mult).then_inc(abkv_ready, 1)
        for c in range(CT):
            dve.wait_ge(bonus_sum, c + 1)
            dve.tensor_tensor(rr[:, c, :], banks[c][:, :], vv[:, c, :], ALU.mult).then_inc(bonus_done, 1)
        for g in range(8, 12):
            ada_columns(g)
        dve.sem_inc(ada_done, 1)
        def unit(c, e, step):
            X = banks[4 * e:4 * e + 4]

            def bank(i):
                return X[i][:, :].rearrange("p (a b) -> p a b", a=4)

            def masked(out, src, mask):
                dve.tensor_tensor(out[:, :, :], src, mask.unsqueeze(1).broadcast_to([P, 4, P]), ALU.mult).then_inc(u_dve[e], 1)

            def placed(out, src, n):
                dve.copy_predicated(out[:, :, :], lvl[:, n, :].unsqueeze(1).broadcast_to([P, 4, P]), src).then_inc(u_dve[e], 1)

            if step == "MT":
                dve.wait_ge(u_pe[e], pe_at(c, "MT"))
                masked(Mt[e], bank(2), before)
            elif step == "RB":
                dve.wait_ge(u_pe[e], pe_at(c, "RB"))
                masked(RBt[2 * c + e], bank(3), until_m)
            elif step == "RK":
                dve.wait_ge(u_pe[e], pe_at(c, "RK"))
                masked(RKt[e], bank(2), until_m)
            elif step == "D0":
                dve.wait_ge(u_act[e], act_at(c, "LT"))
                placed(Di[e], bank(0), 0)
            elif step == "DT0":
                placed(DiT[e], Lt[e][:, :, :], 6)
            else:
                n = int(step[1])
                dve.wait_ge(u_pe[e], pe_at(c, step))
                placed(*((Di[e], bank(1), n) if step[0] == "P" else (DiT[e], bank(2), 6 + n)))

        for st in St:
            last = dve.memset(st[:, :, :], 0.0)
        last.then_inc(st_zero, 1)
        for c in range(CT):
            for step in DVE_STEPS:
                for e in range(2):
                    unit(c, e, step)
        for n in range(NCH):
            tt, r = n // 2, slice(64 * (n % 2), 64 * (n % 2) + 64)
            dve.wait_ge(sa_full, n + 1)
            if n:
                dve.wait_ge(y_full, n)
            dve.tensor_tensor(SA[r, :], banks[0][r, :], U[r, tt, :], ALU.add).then_inc(sa_done, 1)
            if n < NCH - 1:
                dve.wait_ge(st_full, n + 1)
                for e in range(2):
                    hr = slice(64 * e, 64 * e + 64)
                    src = banks[1][hr, :].rearrange("p (c v) -> p c v", c=CT)[:, :, hr]
                    decay = der[hr, ECT:ECT + 32].rearrange("p (c n) -> p c n", n=NCH)[:, :, n + 1:n + 2].broadcast_to([64, CT, 64])
                    dve.tensor_tensor(St[(n + 1) % 2][hr, :, hr], src, decay, ALU.mult).then_inc(st_done, 1)
            if n == 1:
                dve.wait_ge(cln_sum, 1)
                for c in range(CT):
                    dve.scalar_tensor_tensor(out=cacc[:, c, :], in0=banks[4][:, :], scalar=-1.0 / HALF, in1=cacc[:, c, :],
                                             op0=ALU.mult, op1=ALU.add).then_inc(cln_centred, 1)
            if n == 5:
                dve.wait_ge(cln_root, 1)
                chain.link(dve.reciprocal(cstd[:, :], cstd[:, :]))
            if n == 6:
                for c in range(CT):
                    dve.tensor_tensor(cacc[:, c, :], cacc[:, c, :], cstd[:, :], ALU.mult).then_inc(cln_normed, 1)
            dve.wait_ge(y_full, n + 1)
            dve.tensor_tensor(ky[:, :, CHUNK * n:CHUNK * n + CHUNK], banks[2 + n % 2][:, 0:CT * CHUNK].rearrange("p (c t) -> p c t", c=CT),
                              ky[:, :, CHUNK * n:CHUNK * n + CHUNK], ALU.add).then_inc(y_done, 1)
        for c in range(CT):
            dve.wait_ge(gn_mean, c + 1)
            dve.scalar_tensor_tensor(out=ky[:, c, :], in0=banks[4 + c][:, :], scalar=-1.0 / 64, in1=ky[:, c, :],
                                     op0=ALU.mult, op1=ALU.add).then_inc(gn_centred, 1)

        def low(k, src, ready):
            dve.tensor_tensor(h1_lo[:, k, :], src, h1_hi[:, k, :], ALU.subtract).then_inc(ready, 1)

        for c in range(CT):
            dve.wait_ge(gn_root, c + 1)
            chain.link(dve.reciprocal(mrs[:, c % 2, :], mrs[:, c % 2, :]))
            dve.tensor_tensor(ky[:, c, :], ky[:, c, :], mrs[:, c % 2, :], ALU.mult).then_inc(gn_normed, 1)
            dve.wait_ge(mix_hi_full, c + 1)
            low(CT + c, cacc[:, c, :], mix_ready)
            dve.wait_ge(gn_scaled, c + 1)
            chain.link(dve.tensor_tensor(ky[:, c, :], ky[:, c, :], rr[:, c, :], ALU.add))
            dve.tensor_tensor(ky[:, c, :], ky[:, c, :], gg[:, c, :], ALU.mult).then_inc(mix_full, 1)
        for c in range(CT):
            dve.wait_ge(mix_hi_full, CT + c + 1)
            low(c, ky[:, c, :], mix_ready)

        def sum_squares(m0):
            for m in range(m0, m0 + KT):
                dve.wait_ge(out_sq, m + 1)
                if m > m0:
                    dve.wait_ge(out_summed, m)
                    dve.tensor_tensor(nacc[:, :], nacc[:, :], nt[:, m % 2, :], ALU.add).then_inc(out_summed, 1)
                else:
                    dve.tensor_copy(nacc[:, :], nt[:, m % 2, :]).then_inc(out_summed, 1)

        def add_normed(which, src, weight):
            dve.wait_ge(post_root, which + 1)
            chain.link(dve.reciprocal(nr[:, :], nr[:, :]))
            for k in range(KT):
                chain.mark(dve.scalar_tensor_tensor(out=src[:, k, :], in0=src[:, k, :], scalar=col(weight, k), in1=nr[:, :],
                                                    op0=ALU.mult, op1=ALU.mult))
                if k:
                    chain.wait(chain.n - 1)
                    dve.tensor_tensor(xT[:, k - 1, :], xT[:, k - 1, :], src[:, k - 1, :], ALU.add).then_inc(x_done, 1)
            chain.wait()
            dve.tensor_tensor(xT[:, KT - 1, :], xT[:, KT - 1, :], src[:, KT - 1, :], ALU.add).then_inc(x_done, 1)

        sum_squares(0)
        dve.wait_ge(s_x[0], 32)
        add_normed(0, mixo, "post_mix")
        dve.wait_ge(pre_root, 1)
        chain.link(dve.reciprocal(nr[:, :], nr[:, :]))
        for k in range(KT):
            if k >= 2:
                dve.wait_ge(nh_ready, k - 1)
            dve.scalar_tensor_tensor(out=nh[:, k % 2, :], in0=xT[:, k, :], scalar=col("pre_ffn", k), in1=nr[:, :],
                                     op0=ALU.mult, op1=ALU.mult).then_inc(nh_full, 1)
            if k:
                dve.wait_ge(nh_hi, k)
                low(k - 1, nh[:, (k - 1) % 2, :], nh_ready)
        dve.wait_ge(nh_hi, KT)
        low(KT - 1, nh[:, (KT - 1) % 2, :], nh_ready)

        conv = Chain(dve, conv2)
        with conv.loop(N_UP // 2, 4) as i:
            for u in range(2):
                s = half_of(STREAM["up"] + u)
                j = 2 * i + u
                for g, buf in enumerate((yg, yu)):
                    b = banks[2 * s + g]
                    dve.wait_ge(up_first, 4 * i + (2 * u + g + 1))
                    for tap in (1, 0):
                        ins = dve.scalar_tensor_tensor(out=buf[:, s, 2 - tap:], in0=b[:, 0:T - 2 + tap],
                                                       scalar=prm[:, bass.ds(6 * j + (PCOL["fconv_w"] + 3 * g + tap), 1)],
                                                       in1=buf[:, s, 2 - tap:], op0=ALU.mult, op1=ALU.add)
                        if tap:
                            conv.link(ins)
                    ins.then_inc(up_conv, 1)
                    dve.wait_ge(up_conv, 4 * i + (2 * u + g + 1))
                    dve.sem_inc(proj_free[2 * s + g], 1)
                dve.wait_ge(up_gelu, j + 1)
                dve.tensor_tensor(yg[:, s, :], yg[:, s, :], yu[:, s, :], ALU.mult).then_inc(up_prod, 1)
                dve.wait_ge(up_hi, j + 1)
                dve.tensor_tensor(act_lo[:, j, :], yg[:, s, :], act_hi[:, j, :], ALU.subtract).then_inc(act_ready, 1)
        sum_squares(KT)
        add_normed(1, fout, "post_ffn")
        for l in range(2):
            ins = dve.tensor_scalar(ada[:, l, 1, :, :], ada[:, l, 1, :, :], 1.0, None, ALU.add)
        ins.then_inc(ada_one, 1)
        dve.wait_ge(ada_one, 1)
        dve.wait_ge(s_ctx, 16)
        for k in range(KT):
            if k >= 2:
                dve.wait_ge(mh_ready, k - 1)
            dve.tensor_scalar(mh[:, k % 2, T:TA], ctxT[:, k, :], ada[:, 0, 1, k, 1:2], ada[:, 0, 0, k, 1:2],
                              ALU.mult, ALU.add).then_inc(mh_full, 1)
            if k:
                dve.wait_ge(mh_hi, k)
                dve.tensor_tensor(h2_lo[:, k - 1, :], mh[:, (k - 1) % 2, :], h2_hi[:, k - 1, :], ALU.subtract).then_inc(mh_ready, 1)
        dve.wait_ge(mh_hi, KT)
        dve.tensor_tensor(h2_lo[:, KT - 1, :], mh[:, 1, :], h2_hi[:, KT - 1, :], ALU.subtract).then_inc(mh_ready, 1)
        dve.wait_ge(lat_root, 1)
        chain.link(dve.reciprocal(lrs[:, :], lrs[:, :]))
        for c in range(2):
            dve.scalar_tensor_tensor(out=lat[:, c, :], in0=lat[:, c, :], scalar=col("g_qa", c), in1=lrs[:, :],
                                     op0=ALU.mult, op1=ALU.mult).then_inc(lat_normed, 1)
        dve.wait_ge(s_rope, 16)
        dve.wait_ge(kpe_rot, 1)
        pe_rows = slice(64, 96)
        dve.tensor_tensor(otmp[pe_rows, 0:T], banks[6][pe_rows, :], rope[pe_rows, 1, :], ALU.mult)
        chain.link(dve.tensor_tensor(kf[0][pe_rows, 0:T], kf[0][pe_rows, 0:T], rope[pe_rows, 0, :], ALU.mult))
        dve.tensor_tensor(kf[0][pe_rows, 0:T], kf[0][pe_rows, 0:T], otmp[pe_rows, 0:T], ALU.add).then_inc(kpe_done, 1)
        dve.wait_ge(lat_root, 2)
        chain.link(dve.reciprocal(lrs[:, :], lrs[:, :]))
        dve.scalar_tensor_tensor(out=lat[:, 2, :], in0=lat[:, 2, :], scalar=col("g_kva"), in1=lrs[:, :],
                                 op0=ALU.mult, op1=ALU.mult).then_inc(lat_normed, 1)
        for c in range(3):
            dve.wait_ge(lat_high, c + 1)
            dve.tensor_tensor(lat_lo[:, c, :], lat[:, c, :], lat_hi[:, c, :], ALU.subtract).then_inc(lat_ready, 1)

        dve.wait_ge(block_done, STREAM["mla"])
        for e in range(2):
            dve.memset(k_hi[e][96:97, :].bitcast(F32), 1.0)
            dve.memset(k_lo[e][96:97, :].bitcast(F32), 0.0)
            dve.memset(q_lo[e][96:97, :].bitcast(F32), 0.0)
            dve.memset(V_hi[e][:, :, 64 - 64 * e:128 - 64 * e].bitcast(F32), 1.0)
            dve.memset(V_lo[e][:, :, 64 - 64 * e:128 - 64 * e].bitcast(F32), 0.0)
            dve.wait_ge(lat_dead, e + 1)
            ins = dve.tensor_tensor(k_lo[e][pe_rows, :], kf[0][pe_rows, :], k_hi[e][pe_rows, :], ALU.subtract)
        chain.link(ins)

        def turn_q(p, e, here):
            w, _, n = use_of(*here, "R")
            dve.wait_ge(wide_full, n)
            chain.link(dve.tensor_tensor(otmp[pe_rows, 0:T], wide(w)[pe_rows, 0:T], rope[pe_rows, 1, :], ALU.mult))
            dve.sem_inc(wide_free[w], 1)
            dve.wait_ge(pr_evac, 2 * p + (e + 1))
            chain.link(dve.tensor_tensor(qf[pe_rows, 0:T], qf[pe_rows, 0:T], rope[pe_rows, 0, :], ALU.mult))
            dve.tensor_tensor(qf[pe_rows, 0:T], qf[pe_rows, 0:T], otmp[pe_rows, 0:T], ALU.add).then_inc(rope_done, 1)

        def copy_kv(p, here):
            w, _, n = use_of(*here, "k")
            if here[1] is not None:
                dve.wait_ge(head_low, 6 * p - 1)
            dve.wait_ge(wide_full, n)
            dve.tensor_copy(kf[0][0:64, :], wide(w)[0:64, :])
            dve.tensor_copy(kf[1][0:64, :], wide(w)[64:128, :]).then_inc(kv_copied, 1)
            dve.wait_ge(kv_copied, 2 * p + 1)
            dve.sem_inc(wide_free[w], 1)
            turn_q(p, 0, here)
            w, _, n = use_of(*here, "V")
            dve.wait_ge(wide_full, n)
            dve.tensor_copy(Vf[:, :, :].rearrange("p a b -> p (a b)"), wide(w)).then_inc(kv_copied, 1)
            dve.wait_ge(kv_copied, 2 * p + 2)
            dve.sem_inc(wide_free[w], 1)

        def top(here, qt):
            w, _, n = use_of(*here, f"M{qt}")
            dve.wait_ge(wide_full, n)
            if qt < 4:
                chain.link(dve.reduce_max(der[:, MX + qt:MX + qt + 1], wide(w), AX.X))
            else:
                chain.link(dve.reduce_max(der[:, MX + 4:MX + 6], pairs[w][:, :, 0:C], AX.X))
            dve.sem_inc(wide_free[w], 1)
            if qt == 4:
                dve.tensor_scalar(der[:, NM:NM + 6], der[:, MX:MX + 6], -1.0, None, ALU.mult).then_inc(top_ready, 1)

        def low(p, e, j):
            cols = T if j < 4 else TA
            dve.wait_ge(exp_high, 12 * p + (6 * e + j + 1))
            if j >= 3:
                dve.wait_ge(kt_done, 12 * p + (6 * e + j - 2))
            dve.tensor_tensor(P_lo[:, j % 3, 0:cols], Pf[:, j % 3, 0:cols], P_hi[:, j % 3, 0:cols], ALU.subtract).then_inc(exp_low, 1)

        def inverse(p_done, third):
            if third == 0:
                dve.wait_ge(o_copied, 2 * p_done + 4)
            cols = slice(256 * third, 256 * third + 256)
            dve.reciprocal(Ls[:, cols], Ls[:, cols]).then_inc(sums_inverse, 1)

        def head_slot(p, e, done=True):
            last = isinstance(p, int) and p == N_PAIRS - 1 and e == 1
            nxt = None if last else (p, 1) if e == 0 else (p + 1, 0)
            here = (p, e)
            if done:
                inverse(p - 1, 2 * e)
            if nxt and nxt[1]:
                turn_q(*nxt, here)
            elif nxt:
                copy_kv(nxt[0], here)
            low(p, e, 0)
            for j in range(5):
                low(p, e, j + 1)
                if nxt:
                    top(here, j)
            if e == 0 and done:
                inverse(p - 1, 1)

        start = (0, None)
        copy_kv(0, start)
        for qt in range(5):
            top(start, qt)
        head_slot(0, 0, done=False)
        head_slot(0, 1, done=False)
        with chain.loop(N_PAIRS - 2, 2 * (2 + 5)) as i:
            for e in range(2):
                head_slot(i + 1, e)
        for e in range(2):
            head_slot(N_PAIRS - 1, e)
        for third in range(3):
            inverse(N_PAIRS - 1, third)
        for k in range(KT):
            dve.wait_ge(ot_hi, k + 1)
            dve.tensor_tensor(h2_lo[:, k, :], gate_s[:, k, :], h2_hi[:, k, :], ALU.subtract).then_inc(ot_ready, 1)

        def layer_sum(layer, n_cols, x_src, c_src):
            zz = z_of(layer)
            for m in range(KT):
                dve.wait_ge(z_gated, KT * layer + m + 1)
                ins = dve.scalar_tensor_tensor(out=zz[:, m, 0:T], in0=x_src(m), scalar=ALPHA, in1=zz[:, m, 0:T], op0=ALU.mult, op1=ALU.add)
                if n_cols > T:
                    ins = dve.scalar_tensor_tensor(out=zz[:, m, T:TA], in0=c_src(m), scalar=ALPHA, in1=zz[:, m, T:TA], op0=ALU.mult, op1=ALU.add)
                chain.link(ins)
                if m:
                    dve.wait_ge(z_acc, KT * layer + m)
                    dve.tensor_tensor(zacc[:, 0:n_cols], zacc[:, 0:n_cols], zz[:, m, 0:n_cols], ALU.add).then_inc(z_acc, 1)
                else:
                    dve.tensor_copy(zacc[:, 0:n_cols], zz[:, m, 0:n_cols]).then_inc(z_acc, 1)
            dve.wait_ge(z_sum, 9 * layer + 1)
            for k in range(KT):
                dve.scalar_tensor_tensor(out=zz[:, k, 0:n_cols], in0=wide(2, n_cols), scalar=-1.0 / D, in1=zz[:, k, 0:n_cols],
                                         op0=ALU.mult, op1=ALU.add).then_inc(z_centred, 1)
            dve.wait_ge(z_root, layer + 1)
            chain.link(dve.reciprocal(zrs[:, 0:n_cols], zrs[:, 0:n_cols]))
            for k in range(KT):
                dve.tensor_tensor(zz[:, k, 0:n_cols], zz[:, k, 0:n_cols], zrs[:, 0:n_cols], ALU.mult).then_inc(z_normed, 1)

        dve.wait_ge(s_ctx, 32)
        layer_sum(0, TA, lambda m: xT[:, m, :], lambda m: ctx2[:, m, :])
        dve.tensor_tensor(der[0:64, LAM:LAM + 1], col("lam", 0)[0:64, :], col("lam", 1)[0:64, :], ALU.mult)
        dve.tensor_tensor(der[0:64, LAM + 1:LAM + 2], col("lam", 2)[0:64, :], col("lam", 3)[0:64, :], ALU.mult).then_inc(lam_prod, 1)
        for k in range(KT):
            dve.wait_ge(z_out, k + 1)
            if k >= 2:
                dve.wait_ge(mh_ready, KT + k - 1)
            dve.tensor_scalar(zh[:, k % 2, T:TA], z[:, k, T:TA], ada[:, 1, 1, k, 1:2], ada[:, 1, 0, k, 1:2],
                              ALU.mult, ALU.add).then_inc(mh_full, 1)
            if k:
                dve.wait_ge(mh_hi, KT + k)
                dve.tensor_tensor(h2_lo[:, k - 1, :], zh[:, (k - 1) % 2, :], h2_hi[:, k - 1, :], ALU.subtract).then_inc(mh_ready, 1)
        dve.wait_ge(mh_hi, 2 * KT)
        dve.tensor_tensor(h2_lo[:, KT - 1, :], zh[:, 1, :], h2_hi[:, KT - 1, :], ALU.subtract).then_inc(mh_ready, 1)
        dve.wait_ge(lam_exp, 1)
        chain.link(dve.tensor_scalar(der[:, LAM + 4:LAM + 5], der[:, LAM + 3:LAM + 4], der[:, LAM + 2:LAM + 3], None, ALU.subtract))
        dve.tensor_scalar(der[:, LAM + 5:LAM + 6], der[:, LAM + 4:LAM + 5], -LAMBDA_INIT, None, ALU.add)
        chain.link(dve.tensor_scalar(der[:, LAM + 6:LAM + 7], col("g_sub"), 1.0 - LAMBDA_INIT, None, ALU.mult))
        dve.wait_ge(s_rope, 32)

        with chain.loop(B_HEADS, 3 + 8 + 8 + 4) as h:
            dve.wait_ge(wide_full, D_FULL * h + (N_MLA_FULL + 2))
            dve.wait_ge(pr_evac, D_EVAC * h + (N_MLA_EVAC + 2))
            dve.tensor_tensor(dt[:, :], pairs[0][:, 0, :], rope[:, 1, :], ALU.mult)
            chain.link(dve.tensor_tensor(dq[:, :], dq[:, :], rope[:, 0, :], ALU.mult))
            chain.link(dve.tensor_tensor(dq[:, :], dq[:, :], dt[:, :], ALU.add))
            dve.tensor_tensor(dt[:, :], pairs[0][:, 1, :], rope[:, 1, :], ALU.mult)
            chain.link(dve.tensor_tensor(dk[:, 0:T], dk[:, 0:T], rope[:, 0, :], ALU.mult))
            dve.sem_inc(wide_free[0], 1)
            dve.tensor_tensor(dk[:, 0:T], dk[:, 0:T], dt[:, :], ALU.add).then_inc(rope_done, 1)
            dve.wait_ge(rope_done, h + (A_HEADS + 1))
            dve.wait_ge(qk_high, 2 * h + (3 + 1))
            low_rows, high_rows = slice(0, 64), slice(64, 128)
            dve.tensor_tensor(QQ[0][high_rows, :], dq[low_rows, :], QQ[0][low_rows, :], ALU.subtract)
            dve.tensor_tensor(QQ[1][low_rows, :], dq[high_rows, :], QQ[1][high_rows, :], ALU.subtract)
            dve.tensor_tensor(KL[low_rows, :], dk[low_rows, :], KK[0][low_rows, :], ALU.subtract)
            dve.tensor_tensor(KL[high_rows, :], dk[high_rows, :], KK[1][high_rows, :], ALU.subtract).then_inc(qk_low, 1)

            def top(v):
                dve.wait_ge(wide_full, D_FULL * h + (N_MLA_FULL + 5 + v))
                chain.link(dve.reduce_max(der[:, MX + v:MX + v + 1], wide(v % 2), AX.X))
                dve.tensor_scalar(der[:, NM + v:NM + v + 1], der[:, MX + v:MX + v + 1], -B_SCALE, None, ALU.mult).then_inc(nm_ready, 1)

            def out(v):
                chain.link(dve.reciprocal(der[:, RL + v:RL + v + 1], der[:, RS + v:RS + v + 1]))
                if v % 2:
                    chain.link(dve.tensor_tensor(der[:, NL + v:NL + v + 1], der[:, RL + v:RL + v + 1], der[:, LAM + 5:LAM + 6], ALU.mult))
                    dve.wait_ge(o_done, D_UNITS * h + (AFTER_MLA["o"] + v))
                dve.wait_ge(pv_done, D_UNITS * h + (AFTER_MLA["pv"] + v + 1))
                src = banks[6 + v % 2][:, 0:P]
                if v % 2:
                    ins = dve.scalar_tensor_tensor(out=O_tok[:, v // 2, bass.ds(P * h, P)], in0=src, scalar=der[:, NL + v:NL + v + 1],
                                                   in1=o_first[:, :], op0=ALU.mult, op1=ALU.add)
                else:
                    ins = dve.tensor_scalar(o_first[:, :], src, der[:, RL + v:RL + v + 1], None, ALU.mult)
                ins.then_inc(o_done, 1)

            top(0)
            for v in range(8):
                if v + 1 < 8:
                    top(v + 1)
                if v:
                    out(v - 1)
                dve.wait_ge(ta_full, D_UNITS * h + (AFTER_MLA["ta"] + v + 1))
                if v:
                    dve.wait_ge(pv_done, D_UNITS * h + (AFTER_MLA["pv"] + v))
                dve.tensor_copy(dPT[:, 0:3, :].rearrange("p a b -> p (a b)"), banks[4][:, 0:3 * P]).then_inc(eva_done, 1)
            out(7)

        dve.wait_ge(o_root, 1)
        chain.link(dve.reciprocal(o_rs[:, :], o_rs[:, :]))
        for qt in range(4):
            o = O_tok[:, qt, :].rearrange("p (h c) -> p h c", h=B_HEADS)
            r = o_rs[:, :].rearrange("p (h q) -> p h q", q=4)[:, :, qt:qt + 1].broadcast_to([P, B_HEADS, P])
            dve.tensor_tensor(o, o, r, ALU.mult).then_inc(o_scaled, 1)
        for h in range(B_HEADS):
            dve.wait_ge(gate_done, h + 1)
            dve.wait_ge(wide_full, N_MLA_FULL + D_FULL * B_HEADS + h + 1)
            if h >= 2:
                dve.wait_ge(og_ready, 2 * KT + h - 1)
            dve.scalar_tensor_tensor(out=og[:, h % 2, :], in0=wide(h % 2, T), scalar=der[:, LAM + 6:LAM + 7], in1=gate2[:, h, :],
                                     op0=ALU.mult, op1=ALU.mult).then_inc(og_full, 1)
            dve.wait_ge(og_full, 2 * KT + h + 1)
            dve.sem_inc(wide_free[h % 2], 1)
            if h:
                dve.wait_ge(og_hi, 2 * KT + h)
                dve.tensor_tensor(h2_lo[:, h - 1, 0:T], og[:, (h - 1) % 2, :], h2_hi[:, h - 1, 0:T], ALU.subtract).then_inc(og_ready, 1)
        dve.wait_ge(og_hi, 2 * KT + B_HEADS)
        dve.tensor_tensor(h2_lo[:, B_HEADS - 1, 0:T], og[:, 1, :], h2_hi[:, B_HEADS - 1, 0:T], ALU.subtract).then_inc(og_ready, 1)
        layer_sum(1, T, lambda m: z[:, m, 0:T], None)

    es.close()


def pack(inputs):
    g = {k: np.asarray(v) for k, v in inputs.items()}
    z = np.zeros

    def tiles(w, cols):
        w = w[:, cols]
        out = z((w.shape[0] // P, P, P), w.dtype)
        out[:, :, :w.shape[1]] = w.reshape(-1, P, w.shape[1])
        return list(out)

    s = []
    w_in = g["w_in_first"]
    for j in range(CT):
        s += tiles(w_in, slice(P * j, P * j + P)) + tiles(w_in, slice(HALF + P * j, HALF + P * j + P))
    for j in range(12):
        s += tiles(w_in, slice(1024 + P * j, 1024 + P * j + P))
    s += tiles(w_in, slice(2560, 2624)) + tiles(w_in, slice(2624, 2720))
    for j in range(KT):
        s += tiles(g["w_out"][0], slice(P * j, P * j + P))
    for j in range(FT):
        s += tiles(g["ffn_up"][0], slice(P * j, P * j + P)) + tiles(g["ffn_up"][0], slice(DFF + P * j, DFF + P * j + P))
    for j in range(KT // 2):
        s += tiles(g["ffn_down"][0], slice(2 * P * j, 2 * P * j + P)) + tiles(g["ffn_down"][0], slice(2 * P * j + P, 2 * P * j + 2 * P))
        s += [z((P, P), np.float32)] * 4
    w = g["mla_w_in_2"][0]
    for j in range(3):
        s += tiles(w, slice(P * j, P * j + P))
    s += tiles(w, slice(320, 416))
    for j in range(KT):
        s += tiles(w, slice(416 + P * j, 416 + P * j + P))
    qb, kvb = g["mla_w_qb_2"][0], g["mla_w_kvb_2"][0].reshape(P, A_HEADS, 2, 64)
    for p in range(A_HEADS // 2):
        for h in (2 * p, 2 * p + 1):
            s += tiles(qb, slice(A_QK * h, A_QK * h + A_QK))
        for part in range(2):
            s += [np.concatenate([kvb[:, 2 * p, part], kvb[:, 2 * p + 1, part]], axis=1)]
        s += [z((P, P), np.float32)] * 10
    for j in range(KT):
        s += tiles(g["out_w_2"][0], slice(P * j, P * j + P))
    w = g["diff_w_in_2"][0]
    for h in range(B_HEADS):
        for part in range(4):
            s += tiles(w, slice(D * part + P * h, D * part + P * h + P))
    for j in range(KT):
        s += tiles(g["out_w_2"][1], slice(P * j, P * j + P))
    stream = np.stack(s).reshape(N_BLOCKS, TILES, P, P).transpose(0, 2, 1, 3).reshape(N_BLOCKS, P, WBLK)

    aw = g["ada_w_2"].reshape(2, KT, P, 12, 256).transpose(0, 3, 2, 1, 4).reshape(ADA_BLOCKS, P, KT, 256)

    v = z((P, N_PCOL), np.float32)

    def put(name, a):
        a = np.asarray(a)
        v[:a.shape[0], PCOL[name]:PCOL[name] + a.shape[1]] = a

    def cols(a):
        return a.reshape(-1, P).T

    mu = g["mu_first"]
    m = z((14, P), np.float32)
    m[:12] = mu[:1536].reshape(12, P)
    m[12, :64] = mu[1536:1600]
    m[13, :96] = mu[1600:1696]
    put("mu", m.T)
    put("w0", cols(g["decay_w0"][0])); put("a0", cols(g["iclr_a0"][0]))
    put("k_k", cols(g["k_k"][0])); put("k_a", cols(g["k_a"][0])); put("r_k", cols(g["r_k"][0].reshape(-1)))
    put("lnx_g", cols(g["lnx_g"][0])); put("lnx_b", cols(g["lnx_b"][0]))
    put("cconv_w", g["cconv_w"][0].reshape(TAPS, CT, P).transpose(2, 1, 0).reshape(P, -1))
    put("cconv_b", cols(g["cconv_b"][0])); put("cln_g", cols(g["cln_g"][0])); put("cln_b", cols(g["cln_b"][0]))
    put("pre_mix", cols(g["norm_pre_mix"][0])); put("post_mix", cols(g["norm_post_mix"][0]))
    put("pre_ffn", cols(g["norm_pre_ffn"][0])); put("post_ffn", cols(g["norm_post_ffn"][0]))
    put("fconv_w", g["ffn_conv_w"][0].reshape(3, 2, FT, P).transpose(3, 2, 1, 0).reshape(P, -1))
    put("fconv_b", g["ffn_conv_b"][0].reshape(2, FT, P).transpose(2, 1, 0).reshape(P, -1))
    put("c", np.stack([cols(g["c_2"][0]), cols(g["c_ctx_2"])], axis=2).reshape(P, 16))
    put("ada_b", np.repeat(g["ada_b_2"].reshape(48, P).T, 2, axis=1))
    put("ln_g", cols(g["ln_g_2"].reshape(-1))); put("ln_b", cols(g["ln_b_2"].reshape(-1)))
    put("g_qa", cols(g["mla_g_qa_2"][0])); put("g_kva", cols(g["mla_g_kva_2"][0]))
    put("lam", g["diff_lambda_2"][0].T); put("g_sub", cols(g["diff_g_sub_2"][0]))

    lora = np.concatenate([g["decay_up"][0], g["iclr_up"][0]], axis=0)
    c = lambda a: np.ascontiguousarray(a)
    out = {
        "x_t": c(g["x"][0].T.reshape(KT, P, T).transpose(1, 0, 2)),
        "ctx_t": c(g["ctx_2"][0].T.reshape(KT, P, C).transpose(1, 0, 2)),
        "stream": c(stream), "ada_w": c(aw), "vectors": v, "lora_w": c(lora), "gate_w": c(g["gate_up"][0]),
    }
    out.update(constants())
    return out


def constants():
    j, t = np.meshgrid(np.arange(P), np.arange(P), indexing="ij")
    same = (j // CHUNK) == (t // CHUNK)
    sq = np.zeros((P, 7, P), np.float32)
    sq[:, 0] = j == t
    sq[:, 1] = 1
    sq[:, 2] = same
    sq[:, 3] = same & (j < t)
    sq[:, 4] = same & (j <= t)

    def rotation(rows, half):
        r = np.zeros((P, P), np.float32)
        for start in rows:
            for i in range(half):
                r[start + half + i, start + i] = -1
                r[start + i, start + half + i] = 1
        return r
    sq[:, 5] = rotation([64], 16)
    sq[:, 6] = rotation([0, 64], 32)
    lv = np.zeros((P, 12, P), np.float32)
    for n in range(6):
        s = 1 << n
        low = (j // (2 * s) == t // (2 * s)) & (j % (2 * s) >= s) & (t % (2 * s) < s)
        lv[:, n] = low
        lv[:, 6 + n] = low.T
    scan = np.ones((P, T), np.float32)
    scan[:, ::CHUNK] = 0

    def angles(dim):
        n = dim // 4
        inv = (np.float32(10000.0) ** (-np.arange(n, dtype=np.float32) / np.float32(n))).astype(np.float32)
        row, c = np.repeat(np.arange(T // 64, dtype=np.float32), 64), np.tile(np.arange(64, dtype=np.float32), T // 64)
        return np.concatenate([row[:, None] * inv, c[:, None] * inv], axis=-1).T
    ropes = np.zeros((2, P, 2, T), np.float32)
    a = angles(32)
    ropes[0, :, 0] = 1
    for o in (64, 80):
        ropes[0, o:o + 16, 0], ropes[0, o:o + 16, 1] = np.cos(a), np.sin(a)
    b = angles(64)
    for o in range(0, P, 32):
        ropes[1, o:o + 32, 0], ropes[1, o:o + 32, 1] = np.cos(b), np.sin(b)
    return {"squares": sq, "level_masks": lv, "scan_mask": scan, "ropes": ropes}


def kernel(**inputs):
    import numpy as _np
    import concourse.bacc as _bacc
    from concourse import mybir as _mybir
    from concourse.bass_utils import run_bass_kernel_spmd as _run

    arrays = pack(inputs)
    nc = _bacc.Bacc("TRN2", target_bir_lowering=False, num_devices=1)
    args = {name: nc.dram_tensor(f"in_{name}", list(a.shape), _mybir.dt.from_np(a.dtype), kind="ExternalInput").ap()
            for name, a in arrays.items()}
    out_t = nc.dram_tensor("out_t", [P, KT, T], F32, kind="ExternalOutput").ap()
    build(nc, out_t=out_t, **args)
    r = _run(nc, [{f"in_{name}": a for name, a in arrays.items()}], core_ids=[0])
    y = r.results[0]["out_t"]
    return _np.ascontiguousarray(y.transpose(2, 1, 0).reshape(1, T, D))
```
